# Optimizing a Trainium2 kernel written in Bass

```python
import jax, jax.numpy as jnp
from jax import lax
import numpy as np
import math
import jax
import jax.numpy as jnp

D_MODEL = 1024
BATCH = 1
SEQ = 256
DEPTH = 1

CONV_CH = D_MODEL // 2
CONV_K = 31
CONV_GROUPS = 8
POOL_CH = D_MODEL // 2
POOL_WINDOWS = (2, 4, 8, 16)
N_POOL_GROUPS = len(POOL_WINDOWS)
POOL_GROUP_CH = POOL_CH // N_POOL_GROUPS
POOL_GROUP_OUT = D_MODEL // N_POOL_GROUPS
N_BRANCH = 2
COL_A_VAL = CONV_CH
COL_A_GATE = 2 * CONV_CH
COL_POOL = 2 * CONV_CH + POOL_CH
COL_GATE_A = COL_POOL + D_MODEL
IN_COLS = COL_POOL + N_BRANCH * D_MODEL
D_FF = ((8 * D_MODEL // 3 + 127) // 128) * 128
FFN_K = 3
ALPHA = (2.0 * DEPTH) ** 0.25
BETA = (8.0 * DEPTH) ** -0.25
LN_EPS = 1e-5
N_MOD = 6


def layer_norm(x, g=None, b=None):
    xf = x.astype(jnp.float32)
    mu = jnp.mean(xf, axis=-1, keepdims=True)
    var = jnp.mean(jnp.square(xf - mu), axis=-1, keepdims=True)
    y = (xf - mu) * lax.rsqrt(var + LN_EPS)
    if g is not None:
        y = y * g.astype(jnp.float32) + b.astype(jnp.float32)
    return y.astype(x.dtype)

def causal_dwconv(x, w, b):
    k, ch = w.shape
    y = lax.conv_general_dilated(
        x, w[:, None, :].astype(x.dtype), window_strides=(1,),
        padding=[(k - 1, 0)], dimension_numbers=("NWC", "WIO", "NWC"),
        feature_group_count=ch)
    return y + b.astype(x.dtype)

def causal_multiscale_pool(u):
    bsz, s, _ = u.shape
    ug = u.reshape(bsz, s, N_POOL_GROUPS, POOL_GROUP_CH).astype(jnp.float32)
    cs = jnp.cumsum(ug, axis=1)
    pos = jnp.arange(s)
    outs = []
    for gi, w in enumerate(POOL_WINDOWS):
        c_g = cs[:, :, gi]
        lag = jnp.pad(c_g, ((0, 0), (w, 0), (0, 0)))[:, :s]
        cnt = jnp.minimum(pos + 1, w).astype(jnp.float32)[None, :, None]
        outs.append((c_g - lag) / cnt)
    pooled = jnp.stack(outs, axis=2)
    return (pooled - ug).astype(u.dtype)

def first_inputs(seed: int = 0) -> dict:
    key = jax.random.key(seed)
    ks = jax.random.split(key, 24)
    f32 = jnp.float32
    L = DEPTH

    def nrm(k, shape, scale):
        return jax.random.normal(k, shape, f32) * scale

    def gain(k, shape):
        return 1.0 + 0.05 * jax.random.normal(k, shape, f32)

    return {
        "x": jax.random.normal(ks[0], (BATCH, SEQ, D_MODEL), f32),
        "c": jax.random.normal(ks[1], (BATCH, D_MODEL), f32),
        "w_ada": nrm(ks[2], (L, D_MODEL, N_MOD * D_MODEL), 0.5 * D_MODEL ** -0.5),
        "b_ada": nrm(ks[3], (L, N_MOD * D_MODEL), 0.02),
        "w_in": nrm(ks[4], (L, D_MODEL, IN_COLS), D_MODEL ** -0.5),
        "w_dw_a": nrm(ks[5], (L, CONV_K, CONV_CH), CONV_K ** -0.5),
        "b_dw_a": nrm(ks[6], (L, CONV_CH), 0.02),
        "ln_a_g": gain(ks[7], (L, CONV_CH)),
        "ln_a_b": nrm(ks[8], (L, CONV_CH), 0.02),
        "w_pw_a": nrm(ks[9], (L, CONV_CH, D_MODEL), BETA * CONV_CH ** -0.5),
        "w_pool": nrm(ks[10], (L, N_POOL_GROUPS, POOL_GROUP_CH, POOL_GROUP_OUT), BETA * POOL_GROUP_CH ** -0.5),
        "pool_scale": gain(ks[11], (L, D_MODEL)),
        "w_out": nrm(ks[12], (L, D_MODEL, D_MODEL), BETA * D_MODEL ** -0.5),
        "ln1_g": gain(ks[13], (L, D_MODEL)),
        "ln1_b": nrm(ks[14], (L, D_MODEL), 0.02),
        "w_up": nrm(ks[15], (L, D_MODEL, 2 * D_FF), BETA * D_MODEL ** -0.5),
        "w_dw_f": nrm(ks[16], (L, FFN_K, 2 * D_FF), FFN_K ** -0.5),
        "b_dw_f": nrm(ks[17], (L, 2 * D_FF), 0.02),
        "w_down": nrm(ks[18], (L, D_FF, D_MODEL), BETA * D_FF ** -0.5),
        "ln2_g": gain(ks[19], (L, D_MODEL)),
        "ln2_b": nrm(ks[20], (L, D_MODEL), 0.02),
    }

def first_block(x, c, w_ada, b_ada, w_in, w_dw_a, b_dw_a, ln_a_g, ln_a_b, w_pw_a,
              w_pool, pool_scale, w_out, ln1_g, ln1_b, w_up, w_dw_f, b_dw_f,
              w_down, ln2_g, ln2_b):
    bsz, s, _ = x.shape
    for l in range(DEPTH):
        mod = jax.nn.silu(c) @ w_ada[l] + b_ada[l]
        sh1, sc1, g1, sh2, sc2, g2 = jnp.split(mod, N_MOD, axis=-1)

        h = layer_norm(x) * (1.0 + sc1[:, None]) + sh1[:, None]
        proj = h @ w_in[l]
        a_val, a_gate, u_pool, gate_a, gate_b = jnp.split(
            proj, [COL_A_VAL, COL_A_GATE, COL_POOL, COL_GATE_A], axis=-1)

        ya = a_val * jax.nn.sigmoid(a_gate)
        ya = causal_dwconv(ya, w_dw_a[l], b_dw_a[l])
        ya = jax.nn.silu(layer_norm(ya, ln_a_g[l], ln_a_b[l]))
        ya = ya @ w_pw_a[l]

        pooled = causal_multiscale_pool(u_pool)
        yb = jnp.einsum("bsgc,gcd->bsgd", pooled, w_pool[l]).reshape(bsz, s, D_MODEL)
        yb = yb * pool_scale[l]

        merged = jax.nn.sigmoid(gate_a) * ya + jax.nn.sigmoid(gate_b) * yb
        mix = merged @ w_out[l]
        x = layer_norm(ALPHA * x + g1[:, None] * mix, ln1_g[l], ln1_b[l])

        h = layer_norm(x) * (1.0 + sc2[:, None]) + sh2[:, None]
        up = causal_dwconv(h @ w_up[l], w_dw_f[l], b_dw_f[l])
        v, gt = jnp.split(up, 2, axis=-1)
        f = (jax.nn.gelu(gt) * v) @ w_down[l]
        x = layer_norm(ALPHA * x + g2[:, None] * f, ln2_g[l], ln2_b[l])
    return x


DEPTH_2 = 2

N_MIXERS = 3

GDN_DK = 128
GDN_DV = 128
GDN_HEADS = D_MODEL // GDN_DK
GDN_CONV = 4
GDN_CHUNK = 64
GDN_QK = GDN_HEADS * GDN_DK
GDN_V = GDN_HEADS * GDN_DV
GDN_IN = 2 * GDN_QK + 2 * GDN_V + 2 * GDN_HEADS

MOBA_DH = 128
MOBA_HEADS = D_MODEL // MOBA_DH
MOBA_BLOCK = 256
MOBA_TOPK = 3
MOBA_QBLOCK = 16
ROPE_THETA = 500000.0
ROPE_DIMS = MOBA_DH // 4

RET_DK = 256
RET_DV = 512
RET_HEADS = D_MODEL // RET_DK
RET_CHUNK = 128
XPOS_BASE = 10000.0

D_FF_2 = ((8 * D_MODEL + 3 * 256 - 1) // (3 * 256)) * 256

DEEPNORM_ALPHA = (2 * DEPTH_2) ** 0.25
DEEPNORM_BETA = (8 * DEPTH_2) ** -0.25
NORM_EPS = 1e-6
NEG_INF = -1e30
F32 = jnp.float32


def layer_norm_2(x, g, b):
    xf = x.astype(F32)
    mu = jnp.mean(xf, -1, keepdims=True)
    var = jnp.mean(jnp.square(xf - mu), -1, keepdims=True)
    return ((xf - mu) * lax.rsqrt(var + LN_EPS) * g.astype(F32) + b.astype(F32)).astype(x.dtype)

def split_heads(t, n_heads):
    bsz, seq, width = t.shape
    return t.reshape(bsz, seq, n_heads, width // n_heads).transpose(0, 2, 1, 3)

def l2_normalize(t):
    tf = t.astype(F32)
    return tf * lax.rsqrt(jnp.sum(tf * tf, -1, keepdims=True) + NORM_EPS)

def apply_rotary(x, inv_freq):
    half = inv_freq.shape[0]
    seq = x.shape[2]
    ang = jnp.arange(seq, dtype=F32)[:, None] * inv_freq[None, :]
    cos, sin = jnp.cos(ang), jnp.sin(ang)
    xf = x.astype(F32)
    x1, x2 = xf[..., :half], xf[..., half:2 * half]
    out = jnp.concatenate([x1 * cos - x2 * sin, x1 * sin + x2 * cos, xf[..., 2 * half:]], -1)
    return out.astype(x.dtype)

def causal_depthwise_conv(x, w):
    width, ch = w.shape
    return lax.conv_general_dilated(
        x, w[:, None, :], window_strides=(1,), padding=[(width - 1, 0)],
        dimension_numbers=('NWC', 'WIO', 'NWC'), feature_group_count=ch)

def chunk_gated_delta_rule(q, k, v, g, beta):
    bsz, nh, seq, dk = q.shape
    dv = v.shape[-1]
    c = GDN_CHUNK
    n = seq // c
    q = q.astype(F32).reshape(bsz, nh, n, c, dk)
    k = k.astype(F32).reshape(bsz, nh, n, c, dk)
    v = v.astype(F32).reshape(bsz, nh, n, c, dv)
    gc = jnp.cumsum(g.reshape(bsz, nh, n, c), -1)
    beta = beta.reshape(bsz, nh, n, c)
    tril = jnp.tril(jnp.ones((c, c), bool))
    tril_strict = jnp.tril(jnp.ones((c, c), bool), -1)
    diff = gc[..., :, None] - gc[..., None, :]
    decay = jnp.where(tril, jnp.exp(jnp.where(tril, diff, 0.0)), 0.0)
    k_beta = k * beta[..., None]
    v_beta = v * beta[..., None]
    low = jnp.where(tril_strict, jnp.einsum('bhncd,bhnsd->bhncs', k_beta, k) * decay, 0.0)
    rhs = jnp.concatenate([v_beta, k_beta * jnp.exp(gc)[..., None]], -1)
    sol = lax.linalg.triangular_solve(low, rhs, left_side=True, lower=True, unit_diagonal=True)
    u, w = sol[..., :dv], sol[..., dv:]
    attn_intra = jnp.where(tril, jnp.einsum('bhncd,bhnsd->bhncs', q, k) * decay, 0.0)
    q_dec = q * jnp.exp(gc)[..., None]
    k_dec = k * jnp.exp(gc[..., -1:] - gc)[..., None]
    chunk_decay = jnp.exp(gc[..., -1])

    def step(state, inp):
        u_i, w_i, qd_i, kd_i, a_i, cd_i = inp
        v_new = u_i - w_i @ state
        o_i = qd_i @ state + a_i @ v_new
        state = state * cd_i[..., None, None] + jnp.swapaxes(kd_i, -1, -2) @ v_new
        return state, o_i

    xs = tuple(jnp.moveaxis(t, 2, 0) for t in (u, w, q_dec, k_dec, attn_intra, chunk_decay))
    state0 = jnp.zeros((bsz, nh, dk, dv), F32)
    _, o = lax.scan(step, state0, xs)
    return o.transpose(1, 2, 0, 3, 4).reshape(bsz, nh, seq, dv)

def gated_deltanet(x, w_in, w_conv, a_log, dt_bias, norm_g, w_out):
    bsz, seq, _ = x.shape
    nh = GDN_HEADS
    proj = x @ w_in
    qkv, z, b_logit, a_in = jnp.split(
        proj, [2 * GDN_QK + GDN_V, 2 * GDN_QK + 2 * GDN_V, 2 * GDN_QK + 2 * GDN_V + nh], axis=-1)
    qkv = jax.nn.silu(causal_depthwise_conv(qkv, w_conv))
    q, k, v = jnp.split(qkv, [GDN_QK, 2 * GDN_QK], axis=-1)
    q = l2_normalize(split_heads(q, nh)) * GDN_DK ** -0.5
    k = l2_normalize(split_heads(k, nh))
    v = split_heads(v, nh).astype(F32)
    beta = jax.nn.sigmoid(b_logit.astype(F32)).transpose(0, 2, 1)
    g = -(jnp.exp(a_log.astype(F32)) *
          jax.nn.softplus(a_in.astype(F32) + dt_bias.astype(F32))).transpose(0, 2, 1)
    o = chunk_gated_delta_rule(q, k, v, g, beta).transpose(0, 2, 1, 3)
    o = o * lax.rsqrt(jnp.mean(o * o, -1, keepdims=True) + NORM_EPS) * norm_g.astype(F32)
    o = o * jax.nn.silu(z.astype(F32)).reshape(bsz, seq, nh, GDN_DV)
    return o.reshape(bsz, seq, GDN_V).astype(x.dtype) @ w_out

def moba_attention(x, w_qkv, w_out):
    bsz, seq, _ = x.shape
    nh, dh, bs, qb = MOBA_HEADS, MOBA_DH, MOBA_BLOCK, MOBA_QBLOCK
    q, k, v = jnp.split(x @ w_qkv, 3, axis=-1)
    half = ROPE_DIMS // 2
    inv_freq = jnp.power(ROPE_THETA, -jnp.arange(half, dtype=F32) / half)
    q = apply_rotary(split_heads(q, nh), inv_freq)
    k = apply_rotary(split_heads(k, nh), inv_freq)
    v = split_heads(v, nh)
    nkb = -(-seq // bs)
    pad = nkb * bs - seq
    kp = jnp.pad(k, ((0, 0), (0, 0), (0, pad), (0, 0)))
    vp = jnp.pad(v, ((0, 0), (0, 0), (0, pad), (0, 0)))
    k_blocks = kp.reshape(bsz, nh, nkb, bs, dh)
    v_blocks = vp.reshape(bsz, nh, nkb, bs, dh)
    k_mean = jnp.mean(k_blocks.astype(F32), axis=3)
    topk = min(MOBA_TOPK, nkb)
    scale = dh ** -0.5
    b_idx = jnp.arange(bsz)[:, None, None, None]
    h_idx = jnp.arange(nh)[None, :, None, None]

    def one_query_block(qi):
        q0 = qi * qb
        own = q0 // bs
        q_blk = lax.dynamic_slice_in_dim(q, q0, qb, axis=2).astype(F32)
        gate = jnp.einsum('bhqd,bhnd->bhqn', q_blk, k_mean)
        gate = jnp.where(jnp.arange(nkb) < own, gate, -jnp.inf)
        _, sel = lax.top_k(gate, topk)
        sel_valid = sel < own
        k_sel = k_blocks[b_idx, h_idx, sel].astype(F32)
        v_sel = v_blocks[b_idx, h_idx, sel].astype(F32)
        s_sel = jnp.einsum('bhqd,bhqnkd->bhqnk', q_blk, k_sel) * scale
        s_sel = jnp.where(sel_valid[..., None], s_sel, NEG_INF)
        k_own = lax.dynamic_slice_in_dim(kp, own * bs, bs, axis=2).astype(F32)
        v_own = lax.dynamic_slice_in_dim(vp, own * bs, bs, axis=2).astype(F32)
        s_own = jnp.einsum('bhqd,bhkd->bhqk', q_blk, k_own) * scale
        q_pos = q0 + jnp.arange(qb)
        k_pos = own * bs + jnp.arange(bs)
        s_own = jnp.where(k_pos[None, :] <= q_pos[:, None], s_own, NEG_INF)
        s = jnp.concatenate([s_sel.reshape(bsz, nh, qb, topk * bs), s_own], -1)
        p = jax.nn.softmax(s, axis=-1)
        p_sel = p[..., :topk * bs].reshape(bsz, nh, qb, topk, bs)
        p_own = p[..., topk * bs:]
        return (jnp.einsum('bhqnk,bhqnkd->bhqd', p_sel, v_sel) +
                jnp.einsum('bhqk,bhkd->bhqd', p_own, v_own))

    o = lax.map(one_query_block, jnp.arange(seq // qb))
    o = o.transpose(1, 0, 3, 2, 4).reshape(bsz, seq, nh * dh)
    return o.astype(x.dtype) @ w_out

def chunk_retention(q, k, v, log_gamma):
    bsz, nh, seq, dk = q.shape
    dv = v.shape[-1]
    c = RET_CHUNK
    n = seq // c
    q = q.astype(F32).reshape(bsz, nh, n, c, dk)
    k = k.astype(F32).reshape(bsz, nh, n, c, dk)
    v = v.astype(F32).reshape(bsz, nh, n, c, dv)
    pos = jnp.arange(c, dtype=F32)
    tril = jnp.tril(jnp.ones((c, c), bool))
    rel = jnp.where(tril, pos[:, None] - pos[None, :], 0.0)
    dmat = jnp.where(tril, jnp.exp(log_gamma[:, None, None] * rel), 0.0)
    inner = jnp.einsum('bhncd,bhnsd->bhncs', q, k) * dmat[None, :, None]
    o_inner = jnp.einsum('bhncs,bhnsd->bhncd', inner, v)
    q_dec = q * jnp.exp(log_gamma[:, None] * (pos + 1.0))[None, :, None, :, None]
    k_dec = k * jnp.exp(log_gamma[:, None] * (c - 1.0 - pos))[None, :, None, :, None]
    chunk_decay = jnp.exp(log_gamma * c)[None, :, None, None]

    def step(state, inp):
        qd_i, kd_i, v_i = inp
        out = qd_i @ state
        state = state * chunk_decay + jnp.swapaxes(kd_i, -1, -2) @ v_i
        return state, out

    xs = tuple(jnp.moveaxis(t, 2, 0) for t in (q_dec, k_dec, v))
    state0 = jnp.zeros((bsz, nh, dk, dv), F32)
    _, o_cross = lax.scan(step, state0, xs)
    o = o_inner + o_cross.transpose(1, 2, 0, 3, 4)
    return o.reshape(bsz, nh, seq, dv)

def retention(x, w_in, gn_g, w_out):
    bsz, seq, _ = x.shape
    nh = RET_HEADS
    q, k, v, gate = jnp.split(x @ w_in, [nh * RET_DK, 2 * nh * RET_DK, 2 * nh * RET_DK + nh * RET_DV], axis=-1)
    inv_freq = jnp.power(XPOS_BASE, -jnp.linspace(0.0, 1.0, RET_DK // 2, dtype=F32))
    q = apply_rotary(split_heads(q, nh), inv_freq)
    k = apply_rotary(split_heads(k, nh), inv_freq).astype(F32) * RET_DK ** -0.5
    v = split_heads(v, nh)
    log_gamma = jnp.log1p(-jnp.exp2(-5.0 - jnp.arange(nh, dtype=F32)))
    o = chunk_retention(q, k, v, log_gamma).transpose(0, 2, 1, 3)
    mu = jnp.mean(o, -1, keepdims=True)
    var = jnp.mean(jnp.square(o - mu), -1, keepdims=True)
    o = ((o - mu) * lax.rsqrt(var + LN_EPS)).reshape(bsz, seq, nh * RET_DV) * gn_g.astype(F32)
    o = jax.nn.silu(gate.astype(F32)) * o
    return o.astype(x.dtype) @ w_out

def swiglu(x, w13, w2):
    g, u = jnp.split(x @ w13, 2, axis=-1)
    return (jax.nn.silu(g) * u) @ w2

def second_inputs(seed: int = 0) -> dict:
    key = jax.random.key(seed)
    ks = jax.random.split(key, 24)
    n_a = len(range(0, DEPTH_2, N_MIXERS))
    n_b = len(range(1, DEPTH_2, N_MIXERS))
    n_c = len(range(2, DEPTH_2, N_MIXERS))

    def dense(k, shape, fan_in, gain=1.0):
        return jax.random.normal(k, shape, F32) * (gain * fan_in ** -0.5)

    def gain(k, shape):
        return 1.0 + 0.02 * jax.random.normal(k, shape, F32)

    x = jax.random.normal(ks[0], (BATCH, SEQ, D_MODEL), F32)
    a_w_in = dense(ks[1], (n_a, D_MODEL, GDN_IN), D_MODEL)
    a_conv = dense(ks[2], (n_a, GDN_CONV, 2 * GDN_QK + GDN_V), GDN_CONV)
    a_a_log = jnp.log(jax.random.uniform(ks[3], (n_a, GDN_HEADS), F32, 1.0, 16.0))
    dt = jnp.exp(jax.random.uniform(ks[4], (n_a, GDN_HEADS), F32, math.log(1e-3), math.log(1e-1)))
    a_dt_bias = dt + jnp.log(-jnp.expm1(-dt))
    a_norm_g = gain(ks[5], (n_a, GDN_DV))
    a_w_out = dense(ks[6], (n_a, GDN_V, D_MODEL), GDN_V, DEEPNORM_BETA)
    b_w_qkv = dense(ks[7], (n_b, D_MODEL, 3 * MOBA_HEADS * MOBA_DH), D_MODEL)
    b_w_out = dense(ks[8], (n_b, MOBA_HEADS * MOBA_DH, D_MODEL), MOBA_HEADS * MOBA_DH, DEEPNORM_BETA)
    c_w_in = dense(ks[9], (n_c, D_MODEL, 2 * RET_HEADS * RET_DK + 2 * RET_HEADS * RET_DV), D_MODEL)
    c_gn_g = gain(ks[10], (n_c, RET_HEADS * RET_DV))
    c_w_out = dense(ks[11], (n_c, RET_HEADS * RET_DV, D_MODEL), RET_HEADS * RET_DV, DEEPNORM_BETA)
    f_w13 = dense(ks[12], (DEPTH_2, D_MODEL, 2 * D_FF_2), D_MODEL)
    f_w2 = dense(ks[13], (DEPTH_2, D_FF_2, D_MODEL), D_FF_2, DEEPNORM_BETA)
    ln1_g = gain(ks[14], (DEPTH_2, D_MODEL))
    ln1_b = 0.02 * jax.random.normal(ks[15], (DEPTH_2, D_MODEL), F32)
    ln2_g = gain(ks[16], (DEPTH_2, D_MODEL))
    ln2_b = 0.02 * jax.random.normal(ks[17], (DEPTH_2, D_MODEL), F32)
    return {'x': x, 'a_w_in': a_w_in, 'a_conv': a_conv, 'a_a_log': a_a_log, 'a_dt_bias': a_dt_bias,
            'a_norm_g': a_norm_g, 'a_w_out': a_w_out, 'b_w_qkv': b_w_qkv, 'b_w_out': b_w_out,
            'c_w_in': c_w_in, 'c_gn_g': c_gn_g, 'c_w_out': c_w_out, 'f_w13': f_w13, 'f_w2': f_w2,
            'ln1_g': ln1_g, 'ln1_b': ln1_b, 'ln2_g': ln2_g, 'ln2_b': ln2_b}

def second_block(x, a_w_in, a_conv, a_a_log, a_dt_bias, a_norm_g, a_w_out, b_w_qkv, b_w_out,
              c_w_in, c_gn_g, c_w_out, f_w13, f_w2, ln1_g, ln1_b, ln2_g, ln2_b):
    h = x
    for i in range(DEPTH_2):
        kind, j = i % N_MIXERS, i // N_MIXERS
        if kind == 0:
            mix = gated_deltanet(h, a_w_in[j], a_conv[j], a_a_log[j], a_dt_bias[j], a_norm_g[j], a_w_out[j])
        elif kind == 1:
            mix = moba_attention(h, b_w_qkv[j], b_w_out[j])
        else:
            mix = retention(h, c_w_in[j], c_gn_g[j], c_w_out[j])
        h = layer_norm_2(DEEPNORM_ALPHA * h + mix, ln1_g[i], ln1_b[i])
        h = layer_norm_2(DEEPNORM_ALPHA * h + swiglu(h, f_w13[i], f_w2[i]), ln2_g[i], ln2_b[i])
    return h


def setup_inputs(seed=0):
    out = dict(first_inputs(seed))
    for name, value in second_inputs(seed + 1).items():
        if name != "x":
            out[name + "_2"] = value
    return out


def reference(
    x, c, w_ada, b_ada, w_in, w_dw_a, b_dw_a, ln_a_g, ln_a_b, w_pw_a, w_pool, pool_scale, w_out,
    ln1_g, ln1_b, w_up, w_dw_f, b_dw_f, w_down, ln2_g, ln2_b, a_w_in_2, a_conv_2, a_a_log_2,
    a_dt_bias_2, a_norm_g_2, a_w_out_2, b_w_qkv_2, b_w_out_2, c_w_in_2, c_gn_g_2, c_w_out_2,
    f_w13_2, f_w2_2, ln1_g_2, ln1_b_2, ln2_g_2, ln2_b_2,
):
    x = first_block(
        x, c, w_ada, b_ada, w_in, w_dw_a, b_dw_a, ln_a_g, ln_a_b, w_pw_a, w_pool, pool_scale,
        w_out, ln1_g, ln1_b, w_up, w_dw_f, b_dw_f, w_down, ln2_g, ln2_b,
    )
    return second_block(
        x, a_w_in_2, a_conv_2, a_a_log_2, a_dt_bias_2, a_norm_g_2, a_w_out_2, b_w_qkv_2,
        b_w_out_2, c_w_in_2, c_gn_g_2, c_w_out_2, f_w13_2, f_w2_2, ln1_g_2, ln1_b_2, ln2_g_2,
        ln2_b_2,
    )


_drawn_inputs = setup_inputs


def setup_inputs(seed=0):
    import zlib

    import numpy as np

    out = dict(_drawn_inputs(seed))
    spreads = {}
    factors = {'b_ada': 8.0,
     'b_dw_a': 8.0,
     'ln_a_g': 8.0,
     'ln_a_b': 49.013,
     'pool_scale': 8.0,
     'b_dw_f': 8.0,
     'a_norm_g_2': 22.712}
    for name, (base, spread) in spreads.items():
        noise = np.random.default_rng([zlib.crc32(name.encode()), seed]).standard_normal(out[name].shape)
        drawn = base * np.exp(spread * noise) if base else spread * noise
        out[name] = jnp.asarray(drawn.astype(out[name].dtype))
    for name, factor in factors.items():
        out[name] = (out[name] * factor).astype(out[name].dtype)
    return out
```

```python
from contextlib import ExitStack

import numpy as np

import concourse.bass as bass
from concourse import mybir

F = mybir.dt.float32
FR = mybir.dt.float32r
ALU = mybir.AluOpType
ACT = mybir.ActivationFunctionType
AX = mybir.AxisListType

P = 128
S = 256
D = 1024
NC = D // P
FF = 22
HEADS = 8
ALPHA1 = 2.0 ** 0.25
ALPHA2 = 4.0 ** 0.25
LN_EPS = 1e-5
NORM_EPS = 1e-6
RAW = 8
SPLIT = 5
NEG = -1e30

VEC = [("c", 8), ("b_ada", 48), ("b_dw_a", 4), ("ln_a_g", 4), ("ln_a_b", 4), ("pool_scale", 8), ("ln1_g", 8),
       ("ln1_b", 8), ("b_dw_f", 44), ("w_dw_f", 132), ("w_dw_a", 124), ("ln2_g", 8), ("ln2_b", 8),
       ("a_conv", 96), ("a_norm_g", 1), ("ln1_g_2", 16), ("ln1_b_2", 16), ("ln2_g_2", 16), ("ln2_b_2", 16),
       ("a_log", 8), ("dt", 8), ("w_ba", 128)]
VOFF = {}
_n = 0
for _name, _k in VEC:
    VOFF[_name] = _n
    _n += _k
NVEC = _n

CST = [("ident", 128), ("tri", 128), ("mlow", 128), ("mstrict", 128), ("caus", 128), ("lev", 7 * 128),
       ("levT1", 128), ("cos", 256), ("sin", 256), ("icnt", 64)]
COFF = {}
_n = 0
for _name, _k in CST:
    COFF[_name] = _n
    _n += _k
NCST = _n

MODS = {"sh1": 0, "sc1": 8, "g1": 16, "sh2": 24, "sc2": 32, "g2": 40}


def stream_plan():
    w = []
    for t in range(4):
        w += [("in", 4 + t), ("in", t)]
    w += [("in", 8 + t) for t in range(4)]
    w += [("pool", 0)]
    w += [("in", 20 + t) for t in range(8)] + [("in", 12 + t) for t in range(8)]
    w += [("pw", k) for k in range(4)] + [("out", k) for k in range(8)]
    ffn = []
    for j in range(FF):
        ffn += [("up", j), ("up", FF + j)]
        if j >= 1:
            ffn += [("down", j - 1)]
    ffn += [("down", FF - 1)]
    w += ffn
    w += [("gdn", t) for t in range(32)] + [("gout", k) for k in range(8)]

    def swiglu(i):
        out = []
        for j in range(FF):
            out += [(f"w13{i}", j), (f"w13{i}", FF + j)]
            if j >= 1:
                out += [(f"w2{i}", j - 1)]
        return out + [(f"w2{i}", FF - 1)]

    w += swiglu(0)
    w += [("qkv", t) for t in range(16)] + [("vt", k) for k in range(8)] + [("bout", k) for k in range(8)]
    w += swiglu(1)
    plan = [("ada", n) for n in range(16)]
    rest = [("ada", n) for n in range(16, 48)]
    for i, u in enumerate(w):
        plan.append(u)
        if rest:
            plan.append(rest.pop(0))
    return plan


PLAN = stream_plan()


def program(nc, wts, vecs, csts, xT, out):
    with ExitStack() as ctx:
        def sb(name, shape, dt=F):
            return ctx.enter_context(nc.sbuf_tensor(name, shape, dt))

        def sem(name):
            return ctx.enter_context(nc.semaphore(name))

        raw = sb("raw", [P, RAW, 1024])
        hi = sb("hi", [P, SPLIT, 1024], FR)
        lo = sb("lo", [P, SPLIT, 1024], FR)
        vec = sb("vec", [P, NVEC])
        cst = sb("cst", [P, NCST])
        ones = sb("ones", [P, 3, P])
        eps = sb("eps", [P, 2])
        mod = sb("mod", [P, 48])
        cs = sb("cs", [P, 8])
        xa = sb("xa", [P, NC, S])
        h = sb("h", [P, NC, S])
        hh = sb("hh", [P, NC, S], FR)
        hl = sb("hl", [P, NC, S], FR)
        B = [sb(f"B{i}", [P, NC, S]) for i in range(6)]
        st = sb("st", [P, 2, S])
        ev = sb("ev", [P, 4, S])
        fh = sb("fh", [P, 4, S], FR)
        fl = sb("fl", [P, 4, S], FR)
        Z = sb("Z", [P, 24 * 256])
        ypad = Z[:, 0:4 * 288].rearrange("p (g s) -> p g s", g=4)
        sm = sb("sm", [P, 256])
        bank = [ctx.enter_context(nc.psum_tensor(f"ps{i}", [P, 512], F)) for i in range(8)]

        def V(name, i=0, n=1):
            return vec[:, VOFF[name] + i:VOFF[name] + i + n]

        def C(name, a=0, b=None):
            n = dict(CST)[name]
            return cst[:, COFF[name] + a:COFF[name] + (n if b is None else b)]

        ident = C("ident")

        names = ["sync", "gpsimd", "scalar", "tensor", "vector"]
        done = {e: sem("d_" + e) for e in names[1:]}
        raws = [sem(f"s_raw{i}") for i in range(RAW)]
        s_vec, s_cst, s_x, s_out = sem("s_vec"), sem("s_cst"), sem("s_x"), sem("s_out")
        count = {e: 0 for e in names}
        queue = {e: [] for e in names}
        passed = {e: {} for e in names}

        def put(e, waits, make, sig=True):
            for t in waits:
                if t is None:
                    continue
                s, v = t
                if passed[e].get(id(s), 0) < v:
                    passed[e][id(s)] = v
                    queue[e].append(lambda g, s=s, v=v: g.wait_ge(s, v))
            if sig:
                queue[e].append(lambda g: make(g).then_inc(done[e], 1))
                count[e] += 1
                return (done[e], count[e])
            queue[e].append(lambda g: make(g))
            return None

        def pe(waits, make, sig=True):
            return put("tensor", waits, make, sig)

        def act(waits, o, i, f, sig=True, **kw):
            return put("scalar", waits, lambda g: g.activation(o, i, f, **kw), sig)

        def ve(waits, make):
            return put("vector", waits, make)

        def tt(waits, o, a, b, op, e="vector"):
            return put(e, waits, lambda g: g.tensor_tensor(o, a, b, op))

        def MM(o, l, r, start, stop):
            return lambda g: g.matmul(o, l, r, start=start, stop=stop, skip_group_check=True)

        def TR(o, i, idn):
            return lambda g: g.transpose(o, i, idn)

        def RC(o, i):
            return lambda g: g.reciprocal(o, i)

        def RD(o, i, ax, op):
            return lambda g: g.tensor_reduce(o, i, ax, op)

        def SH(o, i):
            return lambda g: g.stream_shuffle(o, i, [(p + 16) % 32 for p in range(32)])

        def ts(waits, o, a, s1, s2, op0, op1=None, e="vector"):
            if op1 is None:
                return put(e, waits, lambda g: g.tensor_scalar(o, a, s1, None, op0))
            return put(e, waits, lambda g: g.tensor_scalar(o, a, s1, s2, op0, op1))

        def stt(waits, o, a, s, b, op0, op1):
            return put("vector", waits, lambda g: g.scalar_tensor_tensor(out=o, in0=a, scalar=s, in1=b, op0=op0,
                                                                         op1=op1))

        def cp(waits, o, i, e="vector"):
            return put(e, waits, lambda g: g.tensor_copy(o, i))

        sent = [0]
        fed = [0]
        nsplit = [0]
        ready = []
        used = []

        def send(tok):
            i = sent[0]
            if i >= len(PLAN):
                return
            sent[0] += 1
            for t in [tok] if tok else []:
                s, v = t
                if passed["sync"].get(id(s), 0) < v:
                    passed["sync"][id(s)] = v
                    queue["sync"].append(lambda g, s=s, v=v: g.wait_ge(s, v))
            src = wts[i]
            queue["sync"].append(lambda g: g.dma_start(raw[:, i % RAW, :], src).then_inc(raws[i % RAW], 16))

        def landed(i):
            return (raws[i % RAW], 16 * (i // RAW + 1))

        modtok = {}

        def feed_one():
            i = fed[0]
            fed[0] += 1
            kind, n = PLAN[i]
            r = raw[:, i % RAW, :]
            if kind == "ada":
                b = n // 8
                name = ["sh1", "sc1", "g1", "sh2", "sc2", "g2"][MB_ORDER[b]]
                c = n % 8
                for k in range(8):
                    t = pe([landed(i), cstok, modtok.get("free")],
                           MM(bank[7][:, c:c + 1], r[:, k * 128:k * 128 + 128], cs[:, k:k + 1],
                                                   start=(c == 0 and k == 0), stop=(k == 7)),
                           k == 7)
                if c == 7:
                    col = MODS[name]
                    one = 1.0 if name[:2] == "sc" else 0.0
                    modtok[name] = modtok["free"] = stt([t, t_vec], mod[:, col:col + 8], bank[7][:, 0:8], one,
                                                        V("b_ada", col, 8), ALU.add, ALU.add)
                send(t)
                return False
            j = nsplit[0]
            nsplit[0] += 1
            free = used[j - SPLIT] if j >= SPLIT else None
            a = act([landed(i), free], hi[:, j % SPLIT, :], r, ACT.Copy)
            b = tt([a, landed(i), free], lo[:, j % SPLIT, :], r, hi[:, j % SPLIT, :].bitcast(F), ALU.subtract)
            ready.append(b)
            send(b)
            return True

        MB_ORDER = [1, 0, 2, 4, 3, 5]

        def feed():
            while fed[0] < len(PLAN) and not feed_one():
                pass

        bg = []

        def background(n):
            for _ in range(min(n, len(bg))):
                bg.pop(0)()

        order = [u for u in PLAN if u[0] != "ada"]

        def take(kind, n, back=0):
            j = len(used)
            assert order[j] == (kind, n), (order[j], kind, n)
            while nsplit[0] <= j:
                feed()
            return j, hi[:, j % SPLIT, :], lo[:, j % SPLIT, :], ready[j]

        def finish(tok):
            used.append(tok)

        def mm3(o, wh, wl, xh, xl, waits, first, last, sig, flip=False):
            for n, (a, b) in enumerate(((wh, xh), (wh, xl), (wl, xh))):
                l, r = (b, a) if flip else (a, b)
                t = pe(waits if n == 0 else [], MM(
                    o, l, r, start=(first and n == 0), stop=(last and n == 2)),
                    sig and n == 2)
            return t

        def nmaj(kind, n, o, xh, xl, xt, free):
            j, wh, wl, t = take(kind, n)
            for k in range(8):
                w = [t, xt[k]] + (free if k == 0 else [])
                last = mm3(o, wh[:, k * 128:k * 128 + 128], wl[:, k * 128:k * 128 + 128], xh[:, k, :], xl[:, k, :],
                           w, k == 0, k == 7, k == 7)
            finish(last)
            return last

        def acc(b0, n):
            return bank[b0 + n // 2][:, (n % 2) * S:(n % 2) * S + S]

        def kmaj(kind, k, b0, xh, xl, xt, first, last, free):
            j, wh, wl, t = take(kind, k)
            toks = []
            for n in range(8):
                w = [t, xt] + (free if n == 0 else [])
                tok = mm3(acc(b0, n), wh[:, n * 128:n * 128 + 128], wl[:, n * 128:n * 128 + 128], xh, xl, w,
                          first and n % 2 == 0, last, n % 2 == 1)
                toks.append(tok)
            toks = [toks[n | 1] for n in range(8)]
            finish(toks[-1])
            return toks

        queue["sync"].append(lambda g: g.dma_start(vec[:, :], vecs).then_inc(s_vec, 16))
        queue["sync"].append(lambda g: g.dma_start(xa[:, :, :], xT).then_inc(s_x, 16))
        t_vec, t_x, t_cst = (s_vec, 16), (s_x, 16), (s_cst, 16)
        for i in range(RAW):
            send(None)
        queue["scalar"].append(lambda g: g.dma_start(cst[:, :], csts).then_inc(s_cst, 16))

        t_ones = put("gpsimd", [], lambda g: g.memset(ones[:, 0, :], 1.0 / 1024))
        t_ones = put("gpsimd", [], lambda g: g.memset(ones[:, 1, :], 1.0 / 512))
        t_ones = put("gpsimd", [], lambda g: g.memset(ones[:, 2, :], 1.0))
        t_ones = put("gpsimd", [], lambda g: g.memset(eps[:, 0:1], LN_EPS))
        t_ones = put("gpsimd", [], lambda g: g.memset(eps[:, 1:2], NORM_EPS))
        t_ones = put("gpsimd", [], lambda g: g.memset(ypad[:, :, 0:32], 0.0))

        cstok = act([t_vec], cs[:, :], V("c", 0, 8), ACT.Silu)

        def bc(a, n):
            return a.unsqueeze(1).to_broadcast([P, n, S])

        def stats_rstd(y, ytoks, nch, one, sq, yc, bm, bv, free):
            for k in range(nch):
                m = pe([ytoks[k], t_ones] + free, MM(bank[bm][:, 0:S], ones[:, one, :],
                       y[:, k, :], start=(k == 0), stop=(k == nch - 1)), k == nch - 1)
            ct = []
            for k in range(0, nch, 2):
                c = tt([m] + free, yc[:, k:k + 2, :], y[:, k:k + 2, :], bc(bank[bm][:, 0:S], 2), ALU.subtract)
                q = act([c], sq[:, k:k + 2, :], yc[:, k:k + 2, :], ACT.Square)
                ct += [c, c]
                for kk in (k, k + 1):
                    v = pe([q], MM(bank[bv][:, 0:S], ones[:, one, :], sq[:, kk, :], start=(kk == 0),
                                  stop=(kk == nch - 1)), kk == nch - 1)
            s = act([v], st[:, 0, :], bank[bv][:, 0:S], ACT.Sqrt, bias=eps[:, 0:1])
            r = ve([s], RC(st[:, 1, :], st[:, 0, :]))
            return ct, r, m, v

        def norm(y, ytoks, nch, one, sq, yc, bm, bv, free, gain, bias, o, gtoks=()):
            ct, r, m, v = stats_rstd(y, ytoks, nch, one, sq, yc, bm, bv, free)
            toks = []
            for k in range(0, nch, 2):
                a = tt([r, ct[k]], yc[:, k:k + 2, :], yc[:, k:k + 2, :], bc(st[:, 1, :], 2), ALU.mult)
                for kk in (k, k + 1):
                    toks.append(ts([a, *gtoks], o[:, kk, :], yc[:, kk, :], gain(kk), bias(kk), ALU.mult, ALU.add))
            return toks

        def split(src, toks, oh, ol, n=NC, free=()):
            out = []
            for k in range(n):
                a = act([toks[k], *free], oh[:, k, :], src[:, k, :], ACT.Copy)
                out.append(tt([a], ol[:, k, :], src[:, k, :], oh[:, k, :].bitcast(F), ALU.subtract))
            return out

        def modcol(name):
            return lambda k: mod[:, MODS[name] + k:MODS[name] + k + 1]

        while PLAN[fed[0]][0] == "ada":
            feed_one()
        for _ in range(SPLIT - 1):
            feed()
        ht = norm(xa, [t_x] * 8, 8, 0, B[0], B[1], 0, 1, [], modcol("sc1"), modcol("sh1"), h,
                  [modtok["sc1"], modtok["sh1"]])
        ht = split(h, ht, hh, hl)

        nb = [0]
        pfree = {b: [] for b in range(8)}

        def tile_out(kind, n, banks, x=None):
            b = banks[nb[0] % len(banks)]
            nb[0] += 1
            feed()
            t = nmaj(kind, n, bank[b][:, 0:S], hh, hl, ht, pfree[b])
            return b, t

        R4 = [2, 3, 4, 5]
        ya = ypad
        yt = []
        pad = t_ones
        for t in range(4):
            b, m = tile_out("in", 4 + t, R4)
            a = act([m], ev[:, t, :], bank[b][:, 0:S], ACT.Sigmoid)
            pfree[b] = [a]
            b, m = tile_out("in", t, R4)
            v = tt([m, a, pad], ya[:, t, 32:32 + S], bank[b][:, 0:S], ev[:, t, :], ALU.mult)
            pfree[b] = [v]
            yt.append(v)

        cv = B[0]
        cvt = [None] * 4

        def conv_tap(i):
            for t in range(4):
                w = V("w_dw_a", t * 31 + i)
                src = ya[:, t, 2 + i:2 + i + S]
                if i == 0:
                    cvt[t] = ts([yt[t], t_vec, pad], cv[:, t, :], src, w, V("b_dw_a", t), ALU.mult, ALU.add)
                else:
                    cvt[t] = stt([cvt[t]], cv[:, t, :], src, w, cv[:, t, :], ALU.mult, ALU.add)

        for i in range(31):
            bg.append(lambda i=i: conv_tap(i))

        pu = B[1][:, :, :].rearrange("p c s -> p (c s)")
        up = pu[:, 0:4 * 272].rearrange("p (g s) -> p g s", g=4)
        pz = put("gpsimd", [ht[7]], lambda g: g.memset(up[:, :, 0:16], 0.0))
        ut = []
        for t in range(4):
            b, m = tile_out("in", 8 + t, R4)
            a = act([m, ht[7]], up[:, t, 16:272], bank[b][:, 0:S], ACT.Copy)
            pfree[b] = [a]
            ut.append(a)
            background(2)
        pa, pb_ = B[2], B[3]
        ws = [pa[:, 0:5, :].rearrange("p c s -> p (c s)")[:, 0:1088].rearrange("p (g s) -> p g s", g=4),
              pb_[:, 0:5, :].rearrange("p c s -> p (c s)")[:, 0:1088].rearrange("p (g s) -> p g s", g=4)]
        src = up
        tk = ut[3]
        lv = []
        for lev in range(4):
            g0 = lev
            sh = 1 << lev
            dst = ws[lev % 2]
            t1 = tt([tk, pz, ut[3]], dst[:, g0:4, sh:272], src[:, g0:4, sh:272], src[:, g0:4, 0:272 - sh], ALU.add,
                    e="gpsimd")
            t2 = cp([tk, t1], dst[:, g0:4, 0:sh], src[:, g0:4, 0:sh], e="gpsimd")
            lv.append((dst, t2))
            src, tk = dst, t2
        pooled = B[4]
        pt = []
        for g in range(4):
            sgrp = lv[g][0][:, g, 16:272]
            a = tt([lv[3][1], t_cst], pooled[:, g, 0:16], sgrp[:, 0:16], C("icnt", g * 16, g * 16 + 16), ALU.mult,
                   e="gpsimd")
            a = ts([a], pooled[:, g, 16:S], sgrp[:, 16:S], 0.5 ** (g + 1), None, ALU.mult, e="gpsimd")
            pt.append(tt([a], pooled[:, g, :], pooled[:, g, :], up[:, g, 16:272], ALU.subtract, e="gpsimd"))
        ph, plo = fh, fl
        pst = []
        for g in range(4):
            a = cp([pt[g]], ph[:, g, :], pooled[:, g, :], e="gpsimd")
            pst.append(tt([a], plo[:, g, :], pooled[:, g, :], ph[:, g, :].bitcast(F), ALU.subtract, e="gpsimd"))
        feed()
        j, wh, wl, wt = take("pool", 0)
        ybt = []
        yb = B[5]
        for n in range(8):
            b = R4[nb[0] % 4]
            nb[0] += 1
            m = mm3(bank[b][:, 0:S], wh[:, n * 128:n * 128 + 128], wl[:, n * 128:n * 128 + 128], ph[:, n // 2, :],
                    plo[:, n // 2, :], [wt, pst[n // 2], *pfree[b]], True, True, True)
            a = act([m, t_vec], yb[:, n, :], bank[b][:, 0:S], ACT.Copy, scale=V("pool_scale", n))
            pfree[b] = [a]
            ybt.append(a)
        finish(m)
        mg = B[1]
        for n in range(8):
            b, m = tile_out("in", 20 + n, R4)
            a = act([m, yt[n] if n < 4 else ybt[n - 4]], ev[:, n % 4, :], bank[b][:, 0:S], ACT.Sigmoid)
            pfree[b] = [a]
            ybt[n] = tt([a, ybt[n]], yb[:, n, :], yb[:, n, :], ev[:, n % 4, :], ALU.mult, e="gpsimd")
            background(2)
        ga = B[4]
        gat = []
        for n in range(8):
            b, m = tile_out("in", 12 + n, R4)
            a = act([m, pst[3]], ga[:, n, :], bank[b][:, 0:S], ACT.Sigmoid)
            pfree[b] = [a]
            gat.append(a)
            background(2)
        background(99)
        yn = B[2]
        at = norm(cv, cvt, 4, 1, B[3], yn, 0, 1, [pst[3], lv[3][1]], lambda k: V("ln_a_g", k), lambda k: V("ln_a_b", k), yn)
        yh, yl = hh[:, 4:8, :], hl[:, 4:8, :]
        gates_done = used[-1]
        s4 = []
        for k in range(4):
            a = act([at[k]], cv[:, k, :], yn[:, k, :], ACT.Silu)
            b = cp([a, gates_done], yh[:, k, :], cv[:, k, :])
            s4.append(tt([b], yl[:, k, :], cv[:, k, :], yh[:, k, :].bitcast(F), ALU.subtract))
        for k in range(4):
            feed()
            toks = kmaj("pw", k, 2, yh[:, k, :], yl[:, k, :], s4[k], k == 0, k == 3,
                        [t for b in R4 for t in pfree[b]])
        mt = []
        for n in range(8):
            a = tt([toks[n], gat[n]], mg[:, n, :], acc(2, n), ga[:, n, :], ALU.mult)
            pfree[2 + n // 2] = [a]
            mt.append(tt([a, ybt[n]], mg[:, n, :], mg[:, n, :], yb[:, n, :], ALU.add))
        mt = split(mg, mt, hh, hl)
        for k in range(8):
            feed()
            toks = kmaj("out", k, 2, hh[:, k, :], hl[:, k, :], mt[k], k == 0, k == 7,
                        [t for b in R4 for t in pfree[b]])

        def residual(toks, b0, gate, gtok, alpha):
            out = []
            for n in range(8):
                if gate is None:
                    t = stt([toks[n]], xa[:, n, :], xa[:, n, :], alpha, acc(b0, n), ALU.mult, ALU.add)
                else:
                    a = act([toks[n], gtok], B[2][:, n, :], acc(b0, n), ACT.Copy, scale=gate(n))
                    t = stt([a], xa[:, n, :], xa[:, n, :], alpha, B[2][:, n, :], ALU.mult, ALU.add)
                out.append(t)
                pfree[b0 + n // 2] = [a if gate is not None else t]
            return out

        rt = residual(toks, 2, modcol("g1"), modtok["g1"], ALPHA1)
        x1 = norm(xa, rt, 8, 0, B[0], B[1], 0, 1, [], lambda k: V("ln1_g", k), lambda k: V("ln1_b", k), xa)
        h2 = norm(xa, x1, 8, 0, B[0], B[1], 0, 1, [], modcol("sc2"), modcol("sh2"), h,
                  [modtok["sc2"], modtok["sh2"]])
        ht = split(h, h2, hh, hl)

        R3 = [4, 5, 6]
        lastnorm = h2[7]

        def ffn(kup, kdown, conv):
            hist = []
            sums = [None]
            fhtok = []
            ftoks = []
            ffree = []

            def down(j):
                feed()
                fr = [t for b in range(4) for t in pfree[b]] if j == 0 else []
                ts_ = kmaj(kdown, j, 0, fh[:, j % 4, :], fl[:, j % 4, :], ftoks[j], j == 0, j == FF - 1, fr)
                ffree.append(ts_[-1])
                return ts_

            evf = [None] * 4
            for j in range(FF):
                got = []
                for half in (0, 1):
                    n = j + half * FF
                    b, m = tile_out(kup, n, R3)
                    slot = (2 * j + half) % 4
                    e = ev[:, slot, :]
                    p0 = bank[b][:, 0:S]
                    if conv:
                        a = act([m, evf[slot], t_vec], e, p0, ACT.Identity, scale=V("w_dw_f", n * 3 + 2),
                                bias=V("b_dw_f", n))
                        a = stt([a, m], e[:, 1:], p0[:, 0:S - 1], V("w_dw_f", n * 3 + 1), e[:, 1:], ALU.mult, ALU.add)
                        a = stt([a], e[:, 2:], p0[:, 0:S - 2], V("w_dw_f", n * 3), e[:, 2:], ALU.mult, ALU.add)
                        pfree[b] = [a]
                        if half == 1:
                            a = act([a], e, e, ACT.Gelu_apprx_tanh)
                    else:
                        a = act([m, evf[slot]], e, p0, ACT.Silu if half == 0 else ACT.Copy)
                        pfree[b] = [a]
                    got.append(a)
                s0, s1 = (2 * j) % 4, (2 * j + 1) % 4
                f = tt(got, ev[:, s0, :], ev[:, s0, :], ev[:, s1, :], ALU.mult)
                fr = [ffree[j - 4]] if j >= 4 else []
                a = cp([f] + fr, fh[:, j % 4, :], ev[:, s0, :], e="gpsimd")
                z = tt([a], fl[:, j % 4, :], ev[:, s0, :], fh[:, j % 4, :].bitcast(F), ALU.subtract, e="gpsimd")
                evf[s0] = z
                evf[s1] = f
                ftoks.append(z)
                if j >= 1:
                    down(j - 1)
            return down(FF - 1)

        evlast = [None]
        toks = ffn("up", "down", True)
        rt = residual(toks, 0, modcol("g2"), modtok["g2"], ALPHA1)
        x2 = norm(xa, rt, 8, 0, B[0], B[1], 4, 5, pfree[4] + pfree[5], lambda k: V("ln2_g", k), lambda k: V("ln2_b", k), xa)
        ht = split(xa, x2, hh, hl)

        qb, kb, vb, zb = B[2], B[3], B[4], B[5]
        R2 = [4, 5]
        pfree[4], pfree[5] = [x2[0]], [x2[0]]

        def ba():
            for c in range(2):
                for k in range(8):
                    t = pe([x2[k], t_vec] + pfree[6], MM(
                        bank[6][:, c * 16:c * 16 + 16], xa[:, k, c * 128:c * 128 + 128], V("w_ba", k * 16, 16),
                        start=(c == 0 and k == 0), stop=(k == 7)), k == 7)
            return t

        bat = ba()
        pba = bank[6][:, 0:32].rearrange("p (c n) -> p c n", c=2)

        def smv(o, n=2):
            return sm[:, o:o + 8 * n].rearrange("p (c n) -> p c n", c=n)

        beta = smv(0)
        gg = smv(16)
        ex = smv(96)
        ax = smv(112)
        rl = smv(128)
        bt = act([bat], beta, pba[:, :, 0:8], ACT.Sigmoid)
        at0 = tt([bat, bt, t_vec], ax, pba[:, :, 8:16], V("dt", 0, 8).unsqueeze(1).to_broadcast([P, 2, 8]), ALU.add)
        pfree[6] = [bt, at0]
        a1 = ts([at0], rl, ax, 0.0, None, ALU.max)
        a2 = stt([a1], ex, rl, -2.0, ax, ALU.mult, ALU.add)
        a3 = act([a2], ex, ex, ACT.Exp)
        a3b = act([t_vec], sm[:, 80:88], V("a_log", 0, 8), ACT.Exp)
        a4 = act([a3], ex, ex, ACT.Ln, bias=1.0)
        a5 = tt([a4], ex, ex, rl, ALU.add)
        gt = stt([a5, a3b], gg, ex, -1.0, sm[:, 80:88].unsqueeze(1).to_broadcast([P, 2, 8]), ALU.mult, ALU.mult)

        def conv4(n, dst, b, m):
            p0 = bank[b][:, 0:S]
            w = lambda i: V("a_conv", n * 4 + i)
            a = act([m, t_vec], dst, p0, ACT.Copy, scale=w(3))
            for i in (2, 1, 0):
                d = 3 - i
                a = stt([a, m], dst[:, d:], p0[:, 0:S - d], w(i), dst[:, d:], ALU.mult, ALU.add)
            pfree[b] = [a]
            return act([a], dst, dst, ACT.Silu)

        def l2(dst, toks, scale, sqb, banks, busy):
            res = {}

            def squares(i):
                q = act([toks[2 * i + 1], *busy[i]], sqb[:, 2 * i:2 * i + 2, :], dst[:, 2 * i:2 * i + 2, :], ACT.Square)
                res["m", i] = pe([q, t_ones] + pfree[banks[i]], MM(
                    bank[banks[i]][:, :], ones[:, 2, :], sqb[:, 2 * i:2 * i + 2, :].rearrange("p a b -> p (a b)"),
                    start=True, stop=True))

            def root(i):
                a = act([res["m", i]], sqb[:, 2 * i:2 * i + 2, :].rearrange("p a b -> p (a b)"), bank[banks[i]][:, :],
                        ACT.Sqrt, bias=eps[:, 1:2])
                pfree[banks[i]] = [a]
                v = sqb[:, 2 * i:2 * i + 2, :]
                b = ve([a], RC(v, v))
                toks[2 * i] = toks[2 * i + 1] = stt([b], dst[:, 2 * i:2 * i + 2, :], dst[:, 2 * i:2 * i + 2, :], scale,
                                                    v, ALU.mult, ALU.mult)
            return ([lambda i=i: squares(i) for i in range(4)] + [lambda i=i: root(i) for i in range(4)])

        qt, kt = [], []
        for n in range(8):
            b, m = tile_out("gdn", n, R2)
            qt.append(conv4(n, qb[:, n, :], b, m))
        bg.extend(l2(qb, qt, 128.0 ** -0.5, B[0], [0, 1, 2, 3], [[]] * 4))
        for n in range(8):
            b, m = tile_out("gdn", 8 + n, R2)
            kt.append(conv4(8 + n, kb[:, n, :], b, m))
            background(1)

        gr = Z[:, 0:2048].rearrange("p (c n s) -> p c n s", c=2, n=8)
        dmat = gr
        gcol = smv(32)
        egc = smv(144)
        nbeg = smv(48)
        kdec = smv(160)
        G = {}

        def gates():
            for c in range(2):
                m = pe([gt, t_cst] + pfree[6], MM(
                    bank[6][:, c * 8:c * 8 + 8], C("tri"), gg[:, c, :], start=(c == 0), stop=True))
            G["gc"] = cp([m], gcol, bank[6][:, 0:16].rearrange("p (c n) -> p c n", c=2))
            pfree[6] = [G["gc"]]
            a = act([G["gc"]], egc, gcol, ACT.Exp)
            G["nbeg"] = stt([a, bt], nbeg, egc, -1.0, beta, ALU.mult, ALU.mult)

        qdec = Z[:, 2048:3072].rearrange("p (n s) -> p n s", n=8)

        def rows(c, q):
            bk = [0, 1, 2, 3][(2 * c + q) % 4]
            for i in range(4):
                hd = 4 * q + i
                m = pe([gt, t_cst] + pfree[bk], MM(
                    bank[bk][:, i * P:i * P + P], gg[:, c, hd:hd + 1].to_broadcast([P, P]), C("tri"),
                    start=(i == 0), stop=True), i == 3)
            for i in range(4):
                hd = 4 * q + i
                G["read"] = a = ts([m, G["gc"]], gr[:, c, hd, :], bank[bk][:, i * P:i * P + P], gcol[:, c, hd:hd + 1], -1.0,
                       ALU.subtract, ALU.mult)
                if c == 0:
                    G["read"] = G["kl", hd] = ts([m, G["gc"]], kdec[:, 0, hd:hd + 1], bank[bk][:, i * P + P - 1:i * P + P],
                                     gcol[:, c, hd:hd + 1], None, ALU.subtract)
            v = gr[:, c, 4 * q:4 * q + 4, :]
            a = ts([a], v, v, 0.0, None, ALU.min)
            a = act([a], v, v, ACT.Exp)
            a = tt([a, t_cst], v, v, C("mlow").unsqueeze(1).to_broadcast([P, 4, P]), ALU.mult)
            G["D", c, q] = a
            fr = [a]
            if c == 1:
                qv = qdec[:, 4 * q:4 * q + 4, :].rearrange("p a b -> p (a b)")
                e = act([m, G["read"]], qv, bank[bk][:, :], ACT.Exp)
                fr.append(e)
                G["qd", q] = tt([e, qt[4 * q + 3]], qdec[:, 4 * q:4 * q + 4, :], qdec[:, 4 * q:4 * q + 4, :],
                                qb[:, 4 * q:4 * q + 4, P:2 * P], ALU.mult)
            pfree[bk] = fr
            if c == 0 and q == 1:
                G["kdec"] = act([G["kl", 7]], kdec[:, 0, :], kdec[:, 0, :], ACT.Exp)

        bg.append(gates)
        for c in range(2):
            for q in range(2):
                bg.append(lambda c=c, q=q: rows(c, q))
        bg.extend(l2(kb, kt, 1.0, B[0], [0, 1, 2, 3], [[qt[2 * i]] for i in range(4)]))

        lt = Z[:, 3072:5120].rearrange("p (g i s) -> p g i s", g=4, i=4)
        tm = B[0][:, :, :].rearrange("p a b -> p (a b)").rearrange("p (g i s) -> p g i s", g=4, i=4)
        tT = B[1][:, :, :].rearrange("p a b -> p (a b)").rearrange("p (g i s) -> p g i s", g=4, i=4)
        aT = Z[:, 0:2048].rearrange("p (g i s) -> p g i s", g=4, i=4)
        pm = ev[:, :, :].rearrange("p a b -> p (a b)").rearrange("p (g i s) -> p g i s", g=2, i=4)
        T = {}
        npm = [0]
        BK = [0, 1, 2, 3, 6]
        nbk = [0]

        def nextbank():
            b = BK[nbk[0] % 5]
            nbk[0] += 1
            return b

        def ga_(c, q):
            g_ = 2 * c + q
            b1 = nextbank()
            sl = slice(c * P, c * P + P)
            for i in range(4):
                hd = 4 * q + i
                m = pe([kt[hd]] + pfree[b1], MM(
                    bank[b1][:, i * P:i * P + P], kb[:, hd, sl], kb[:, hd, sl], start=(i == 0), stop=True), i == 3)
            b2 = nextbank()
            for i in range(4):
                hd = 4 * q + i
                m2 = pe([kt[hd], qt[hd]] + pfree[b2], MM(
                    bank[b2][:, i * P:i * P + P], qb[:, hd, sl], kb[:, hd, sl], start=(i == 0), stop=True), i == 3)
            x = pm[:, npm[0] % 2]
            w = T.get(("pm", npm[0] % 2))
            for i in range(4):
                hd = 4 * q + i
                a = stt([m, G["D", c, q], bt, w], x[:, i, :], bank[b1][:, i * P:i * P + P],
                        beta[:, c, hd:hd + 1], gr[:, c, hd, :], ALU.mult, ALU.mult)
            pfree[b1] = [a]
            a = tt([a], x, x, C("mstrict").unsqueeze(1).to_broadcast([P, 4, P]), ALU.mult)
            y = tm[:, g_]
            a2 = tt([a, m2], aT[:, g_], bank[b2][:, :].rearrange("p (i s) -> p i s", i=4), gr[:, c, 4 * q:4 * q + 4, :],
                    ALU.mult)
            pfree[b2] = [a2]
            b3 = nextbank()
            for i in range(4):
                m3 = pe([a, t_cst] + pfree[b3], TR(bank[b3][:, i * P:i * P + P], x[:, i, :], ident),
                        i == 3)
            l = cp([m3], lt[:, g_], bank[b3][:, :].rearrange("p (i s) -> p i s", i=4))
            pfree[b3] = [l]
            b4 = nextbank()
            for i in range(4):
                m4 = pe([a2, t_cst] + pfree[b4], TR(bank[b4][:, i * P:i * P + P], aT[:, g_, i, :],
                                                                           ident), i == 3)
            T["aT", g_] = act([m4], aT[:, g_], bank[b4][:, :].rearrange("p (i s) -> p i s", i=4), ACT.Copy)
            pfree[b4] = [T["aT", g_]]
            idb = ident.unsqueeze(1).to_broadcast([P, 4, P])
            a = tt([a], tm[:, g_], x, C("lev", 0, P).unsqueeze(1).to_broadcast([P, 4, P]), ALU.mult)
            T["T", g_] = tt([a], tm[:, g_], idb, tm[:, g_], ALU.subtract)
            a = tt([l], tT[:, g_], lt[:, g_], C("levT1").unsqueeze(1).to_broadcast([P, 4, P]), ALU.mult)
            T["TT", g_] = tt([a], tT[:, g_], idb, tT[:, g_], ALU.subtract)
            T["L", g_] = l
            T["pm", npm[0] % 2] = T["TT", g_]
            npm[0] += 1

        def level(lv_, g_):
            last = lv_ == 6
            b1 = nextbank()
            for i in range(4):
                m = pe([T["L", g_], T["T", g_]] + pfree[b1], MM(
                    bank[b1][:, i * P:i * P + P], lt[:, g_, i, :], tm[:, g_, i, :], start=(i == 0), stop=True), i == 3)
            x = pm[:, npm[0] % 2]
            key = ("pm", npm[0] % 2)
            npm[0] += 1
            a = tt([m, T.get(key), t_cst], x, bank[b1][:, :].rearrange("p (i s) -> p i s", i=4),
                   C("lev", lv_ * P, lv_ * P + P).unsqueeze(1).to_broadcast([P, 4, P]), ALU.mult)
            pfree[b1] = [a]
            b3 = nextbank()
            for i in range(4):
                m3 = pe([a, T["TT", g_]] + pfree[b3], MM(
                    bank[b3][:, i * P:i * P + P], x[:, i, :], tT[:, g_, i, :], start=(i == 0), stop=True), i == 3)
            m2 = m3
            if not last:
                b2 = nextbank()
                for i in range(4):
                    m2 = pe([a, T["TT", g_]] + pfree[b2], MM(
                        bank[b2][:, i * P:i * P + P], tT[:, g_, i, :], x[:, i, :], start=(i == 0), stop=True), i == 3)
                T["T", g_] = tt([m2], tm[:, g_], tm[:, g_], bank[b2][:, :].rearrange("p (i s) -> p i s", i=4),
                                ALU.subtract)
                pfree[b2] = [T["T", g_]]
            T[key] = m2
            T["TT", g_] = tt([m3, m2], tT[:, g_], tT[:, g_], bank[b3][:, :].rearrange("p (i s) -> p i s", i=4),
                             ALU.subtract)
            pfree[b3] = [T["TT", g_]]

        rv = h[:, :, :].rearrange("p a b -> p (a b)").rearrange("p (g i s) -> p g i s", g=4, i=4)
        kd = Z[:, 5120:6144].rearrange("p (g i s) -> p g i s", g=2, i=4)
        vt = []

        def tokmaj_v(c, q):
            b1 = nextbank()
            for i in range(4):
                m = pe([vt[4 * q + i], t_cst] + pfree[b1], TR(
                    bank[b1][:, i * P:i * P + P], vb[:, 4 * q + i, c * P:c * P + P], ident), i == 3)
            for i in range(4):
                hd = 4 * q + i
                a = act([m, bt], rv[:, 2 * c + q, i, :], bank[b1][:, i * P:i * P + P], ACT.Copy,
                        scale=beta[:, c, hd:hd + 1])
            pfree[b1] = [a]
            T["rv", 2 * c + q] = a

        def tokmaj_k(q):
            b1 = nextbank()
            for i in range(4):
                m = pe([kt[4 * q + i], t_cst] + pfree[b1], TR(
                    bank[b1][:, i * P:i * P + P], kb[:, 4 * q + i, 0:P], ident), i == 3)
            for i in range(4):
                hd = 4 * q + i
                a = act([m, G["kdec"]], kd[:, q, i, :], bank[b1][:, i * P:i * P + P], ACT.Copy,
                        scale=kdec[:, 0, hd:hd + 1])
            pfree[b1] = [a]
            T["kd", q] = a

        for n in range(8):
            b, m = tile_out("gdn", 16 + n, R2)
            vt.append(conv4(16 + n, vb[:, n, :], b, m))
            background(3)
        background(99)
        for g_ in range(4):
            bg.append(lambda g_=g_: ga_(g_ // 2, g_ % 2))
        for lv_ in range(1, 7):
            for g_ in range(4):
                bg.append(lambda lv_=lv_, g_=g_: level(lv_, g_))
        for q in range(2):
            bg.append(lambda q=q: tokmaj_k(q))
        for g_ in range(4):
            bg.append(lambda g_=g_: tokmaj_v(g_ // 2, g_ % 2))
        zt = []
        for n in range(8):
            b, m = tile_out("gdn", 24 + n, R2)
            a = act([m], zb[:, n, :], bank[b][:, 0:S], ACT.Silu)
            pfree[b] = [a]
            zt.append(a)
            background(4)
        background(99)
        vn = vb[:, :, :].rearrange("p a b -> p (a b)").rearrange("p (g i s) -> p g i s", g=4, i=4)
        ss = lt
        ot = []
        ob = kb
        for q in range(2):
            b1 = nextbank()
            for i in range(4):
                m = pe([T["TT", q], T["rv", q]] + pfree[b1], MM(
                    bank[b1][:, i * P:i * P + P], tT[:, q, i, :], rv[:, q, i, :], start=(i == 0), stop=True), i == 3)
            a0 = cp([m, T["rv", 3]], vn[:, q], bank[b1][:, :].rearrange("p (i s) -> p i s", i=4))
            pfree[b1] = [a0]
            T["vn", q] = a0
        for q in range(2):
            b2 = nextbank()
            for i in range(4):
                m = pe([T["kd", q], T["vn", q]] + pfree[b2], MM(
                    bank[b2][:, i * P:i * P + P], kd[:, q, i, :], vn[:, q, i, :], start=(i == 0), stop=True), i == 3)
            T["S", q] = act([m, T["TT", 3], T["TT", 2]], ss[:, q], bank[b2][:, :].rearrange("p (i s) -> p i s", i=4),
                            ACT.Copy)
            pfree[b2] = [T["S", q]]
        for q in range(2):
            b3 = nextbank()
            for i in range(4):
                m = pe([T["S", q], kt[7]] + pfree[b3], MM(
                    bank[b3][:, i * P:i * P + P], kb[:, 4 * q + i, P:2 * P], ss[:, q, i, :], start=(i == 0), stop=True), i == 3)
            T["ks", q] = m
            for i in range(4):
                hd = 4 * q + i
                a = stt([m, T["rv", 2 + q], G["nbeg"]], rv[:, 2 + q, i, :], bank[b3][:, i * P:i * P + P],
                        nbeg[:, 1, hd:hd + 1], rv[:, 2 + q, i, :], ALU.mult, ALU.add)
            pfree[b3] = [a]
            T["r1", q] = a
        for q in range(2):
            b1 = nextbank()
            for i in range(4):
                m = pe([T["TT", 2 + q], T["r1", q]] + pfree[b1], MM(
                    bank[b1][:, i * P:i * P + P], tT[:, 2 + q, i, :], rv[:, 2 + q, i, :], start=(i == 0), stop=True), i == 3)
            a = cp([m], vn[:, 2 + q], bank[b1][:, :].rearrange("p (i s) -> p i s", i=4))
            pfree[b1] = [a]
            T["vn", 2 + q] = a
        oh, ol = hh, hl
        for q in range(2):
            b1 = nextbank()
            for i in range(4):
                m = pe([T["vn", q], T["aT", q]] + pfree[b1], MM(
                    bank[b1][:, i * P:i * P + P], vn[:, q, i, :], aT[:, q, i, :], start=(i == 0), stop=True), i == 3)
            o0 = ob[:, 4 * q:4 * q + 4, 0:P]
            t0 = cp([m, T["ks", 0], T["ks", 1], T["kd", 0], T["kd", 1]], o0,
                    bank[b1][:, :].rearrange("p (i s) -> p i s", i=4))
            pfree[b1] = [t0]
            b2 = nextbank()
            for i in range(4):
                pe([T["S", q], G["qd", q]] + pfree[b2], MM(
                    bank[b2][:, i * P:i * P + P], ss[:, q, i, :], qdec[:, 4 * q + i, :], start=(i == 0), stop=False), False)
            for i in range(4):
                m = pe([T["vn", 2 + q], T["aT", 2 + q]], MM(
                    bank[b2][:, i * P:i * P + P], vn[:, 2 + q, i, :], aT[:, 2 + q, i, :], start=False, stop=True), i == 3)
            o1 = ob[:, 4 * q:4 * q + 4, P:2 * P]
            t1 = act([m, T["ks", 0], T["ks", 1]], o1, bank[b2][:, :].rearrange("p (i s) -> p i s", i=4), ACT.Copy)
            pfree[b2] = [t1]
            T["o", q] = (t0, t1)
        sq = qb
        rt_ = [None] * 4
        for i in range(4):
            t0, t1 = T["o", i // 2]
            v = sq[:, 2 * i:2 * i + 2, :]
            ov = ob[:, 2 * i:2 * i + 2, :]
            a = act([t0, t1, G["qd", 0], G["qd", 1], T["aT", 3]], v, ov, ACT.Square)
            b1 = nextbank()
            m = pe([a, t_ones] + pfree[b1], MM(bank[b1][:, :], ones[:, 2, :],
                   v.rearrange("p a b -> p (a b)"), start=True, stop=True))
            a = act([m], v.rearrange("p a b -> p (a b)"), bank[b1][:, :], ACT.Sqrt, bias=eps[:, 1:2], scale=1.0 / 128)
            pfree[b1] = [a]
            a = ve([a], RC(v, v))
            a = stt([a, t_vec, t0, t1], ov, ov, V("a_norm_g"), v, ALU.mult, ALU.mult)
            a = tt([a, zt[2 * i + 1]], ov, ov, zb[:, 2 * i:2 * i + 2, :], ALU.mult)
            rt_[i] = a
        otk = split(ob, [rt_[n // 2] for n in range(8)], oh, ol)
        for k in range(8):
            feed()
            toks = kmaj("gout", k, 0, oh[:, k, :], ol[:, k, :], otk[k], k == 0, k == 7,
                        [t for b in range(4) for t in pfree[b]])

        def post(toks, g, b, i):
            rt = residual(toks, 0, None, None, ALPHA2)
            x = norm(xa, rt, 8, 0, B[0], B[1], 4, 5, pfree[4] + pfree[5], lambda k: V(g, 8 * i + k),
                     lambda k: V(b, 8 * i + k), xa)
            pfree[4], pfree[5] = [x[0]], [x[0]]
            return x

        x3 = post(toks, "ln1_g_2", "ln1_b_2", 0)
        ht = split(xa, x3, hh, hl)
        toks = ffn("w130", "w20", False)
        x4 = post(toks, "ln2_g_2", "ln2_b_2", 0)
        ht = split(xa, x4, hh, hl)

        qq, kk_ = B[2], B[3]
        sw = B[4]

        def rope(dst, toks, n):
            x = dst[0:32, n, :]
            y = sw[0:32, n, :]
            a = ve([toks[n]], SH(y, x))
            b = tt([a, t_cst], y, y, C("sin")[0:32, :], ALU.mult)
            c = tt([b], x, x, C("cos")[0:32, :], ALU.mult)
            toks[n] = tt([c], x, x, y, ALU.add)

        qt, kt = [], []
        for n in range(8):
            b, m = tile_out("qkv", n, R2)
            a = act([m], qq[:, n, :], bank[b][:, 0:S], ACT.Copy)
            pfree[b] = [a]
            qt.append(a)
            bg.append(lambda n=n: rope(qq, qt, n))
            if n:
                background(1)
        for n in range(8):
            b, m = tile_out("qkv", 8 + n, R2)
            a = act([m], kk_[:, n, :], bank[b][:, 0:S], ACT.Copy)
            pfree[b] = [a]
            kt.append(a)
            bg.append(lambda n=n: rope(kk_, kt, n))
            background(1)
        background(99)
        for k in range(8):
            feed()
            j, wh, wl, wt = take("vt", k)
            for c in range(2):
                for n in range(2):
                    b = 2 * c + n
                    m = mm3(bank[b][:, :], wh[:, n * 512:n * 512 + 512], wl[:, n * 512:n * 512 + 512],
                            hh[:, k, c * P:c * P + P], hl[:, k, c * P:c * P + P],
                            [wt, ht[k]] + (pfree[b] if k == 0 else []), k == 0, k == 7, True, flip=True)
            finish(m)
        vv = B[5][:, :, :].rearrange("p a b -> p (a b)").rearrange("p (c n) -> p c n", c=2)
        vtk = []
        for b in range(4):
            a = act([m], vv[:, b // 2, (b % 2) * 512:(b % 2) * 512 + 512], bank[b][:, :], ACT.Copy)
            pfree[b] = [a]
            vtk.append(a)
        SC = 128.0 ** -0.5
        pr = B[0][:, :, :].rearrange("p a b -> p (a b)").rearrange("p (h s) -> p h s", h=8)
        p0 = B[1][:, 0:4, :].rearrange("p a b -> p (a b)").rearrange("p (h s) -> p h s", h=8)
        pT = B[4][:, :, :].rearrange("p a b -> p (a b)").rearrange("p (h s) -> p h s", h=8)
        stat = smv(176, 8)
        oo = B[2]
        ABK = [0, 1, 2, 3, 4, 5]
        na = [0]

        def abank():
            b = ABK[na[0] % 6]
            na[0] += 1
            return b

        prt = {}

        def scores(hd):
            b = abank()
            m = pe([qt[hd], kt[hd]] + pfree[b], MM(
                bank[b][:, 0:P], qq[:, hd, 0:P], kk_[:, hd, 0:P], start=True, stop=True))
            m1 = pe([], MM(bank[b][:, P:P + S], qq[:, hd, P:2 * P], kk_[:, hd, :], start=False,
                                           stop=True))
            a = tt([m, m1, t_cst, x4[7]], p0[:, hd, :], bank[b][:, 0:P], C("caus"), ALU.add)
            c = tt([m1, x4[7]], pr[:, hd, P:2 * P], bank[b][:, 2 * P:3 * P], C("caus"), ALU.add)
            c2 = cp([m1], pr[:, hd, 0:P], bank[b][:, P:2 * P])
            pfree[b] = [c2]
            s = stat[:, hd, :]
            a = ve([a], RD(s[:, 0:1], p0[:, hd, :], AX.X, ALU.max))
            c = ve([c, c2], RD(s[:, 1:2], pr[:, hd, :], AX.X, ALU.max))
            a = ts([a, c], s[:, 0:2], s[:, 0:2], -SC, None, ALU.mult)
            e0 = act([a], p0[:, hd, :], p0[:, hd, :], ACT.Exp, bias=s[:, 0:1], scale=SC, accum_out=s[:, 2:3])
            e1 = act([a], pr[:, hd, :], pr[:, hd, :], ACT.Exp, bias=s[:, 1:2], scale=SC, accum_out=s[:, 3:4])
            r = ve([e0, e1], RC(s[:, 4:6], s[:, 2:4]))
            a = ts([r, e0], p0[:, hd, :], p0[:, hd, :], s[:, 4:5], None, ALU.mult)
            c = ts([r, e1], pr[:, hd, :], pr[:, hd, :], s[:, 5:6], None, ALU.mult)
            prt[hd] = (a, c)

        def apply(hd):
            a, c = prt[hd]
            b = abank()
            t = pe([a, c, t_cst] + pfree[b], TR(bank[b][:, 0:P], p0[:, hd, :], ident), False)
            t = pe([], TR(bank[b][:, P:2 * P], pr[:, hd, 0:P], ident), False)
            t = pe([], TR(bank[b][:, 2 * P:3 * P], pr[:, hd, P:2 * P], ident))
            d = act([t, kt[7], prt.get(("m", hd - 4))], pT3[:, hd % 4, :], bank[b][:, 0:3 * P], ACT.Copy)
            pfree[b] = [d]
            b2 = abank()
            vh = lambda c: vv[:, c, hd * P:hd * P + P]
            pe([d, vtk[3], vtk[0], vtk[1], vtk[2]] + pfree[b2], MM(
                bank[b2][:, 0:S], vh(0), pT3[:, hd % 4, 0:S], start=True, stop=False), False)
            m = pe([], MM(bank[b2][:, P:S], vh(1), pT3[:, hd % 4, 2 * P:3 * P], start=False, stop=True))
            prt["m", hd] = m
            a = act([m], oo[:, hd, :], bank[b2][:, 0:S], ACT.Copy)
            pfree[b2] = [a]
            return a

        pT3 = B[4][:, :, :].rearrange("p a b -> p (a b)")[:, 0:1536].rearrange("p (h s) -> p h s", h=4)
        ott = [None] * 8
        for hd in range(8):
            scores(hd)
            if hd >= 3:
                ott[hd - 3] = apply(hd - 3)
        for hd in range(5, 8):
            ott[hd] = apply(hd)
        otk = split(oo, ott, hh, hl)
        for k in range(8):
            feed()
            toks = kmaj("bout", k, 0, hh[:, k, :], hl[:, k, :], otk[k], k == 0, k == 7,
                        [t for b in range(4) for t in pfree[b]])
        x5 = post(toks, "ln1_g_2", "ln1_b_2", 1)
        ht = split(xa, x5, hh, hl)
        toks = ffn("w131", "w21", False)
        x6 = post(toks, "ln2_g_2", "ln2_b_2", 1)
        ofin = h[:, :, :].rearrange("p a b -> p (a b)").rearrange("p (c n) -> p c n", c=2)
        for c in range(2):
            for q in range(2):
                b = 2 * c + q
                for i in range(4):
                    k = 4 * q + i
                    m = pe([x6[k]] + pfree[b], TR(
                        bank[b][:, i * P:i * P + P], xa[:, k, c * P:c * P + P], ident), i == 3)
                a = (act([m], ofin[:, c, q * 512:q * 512 + 512], bank[b][:, :], ACT.Copy) if q else
                     cp([m], ofin[:, c, q * 512:q * 512 + 512], bank[b][:, :]))
                if q == 0:
                    aw = a
            for t in (aw, a):
                queue["sync"].append(lambda g, t=t: g.wait_ge(t[0], t[1]))
            queue["sync"].append(lambda g, c=c: g.dma_start(out[c], ofin[:, c, :]).then_inc(s_out, 16))
        queue["sync"].append(lambda g: g.wait_ge(s_out, 32))
        assert fed[0] == len(PLAN) == sent[0] and len(used) == len(order)

        block = ctx.enter_context(nc.Block())

        @block.sync
        def _(g):
            for f in queue["sync"]:
                f(g)

        @block.gpsimd
        def _(g):
            for f in queue["gpsimd"]:
                f(g)

        @block.scalar
        def _(g):
            for f in queue["scalar"]:
                f(g)

        @block.tensor
        def _(g):
            for f in queue["tensor"]:
                f(g)

        @block.vector
        def _(g):
            for f in queue["vector"]:
                f(g)


ADA = [1, 0, 2, 4, 3, 5]


def _constants():
    i = np.arange(P)
    ident = np.eye(P, dtype=np.float32)
    tri = (i[:, None] <= i[None, :]).astype(np.float32)
    mlow = (i[None, :] <= i[:, None]).astype(np.float32)
    mstrict = (i[None, :] < i[:, None]).astype(np.float32)
    caus = np.where(i[None, :] <= i[:, None], 0.0, NEG).astype(np.float32)
    lev = []
    for n in range(7):
        m = 1 << n
        same = (i[:, None] // (2 * m)) == (i[None, :] // (2 * m))
        lev.append((same & ((i[:, None] // m) % 2 == 1) & ((i[None, :] // m) % 2 == 0)).astype(np.float32))
    freq = np.power(np.float32(500000.0), -np.arange(16, dtype=np.float32) / np.float32(16)).astype(np.float32)
    ang = np.arange(S, dtype=np.float32)[None, :] * freq[:, None]
    cos = np.zeros((P, S), np.float32)
    sin = np.zeros((P, S), np.float32)
    cos[0:16] = cos[16:32] = np.cos(ang)
    sin[0:16] = -np.sin(ang)
    sin[16:32] = np.sin(ang)
    cnt = np.concatenate([1.0 / np.minimum(np.arange(16) + 1, w) for w in (2, 4, 8, 16)]).astype(np.float32)
    parts = {"ident": ident, "tri": tri, "mlow": mlow, "mstrict": mstrict, "caus": caus,
             "lev": np.concatenate(lev, axis=1), "levT1": lev[0].T, "cos": cos, "sin": sin,
             "icnt": np.broadcast_to(cnt, (P, 64))}
    return np.ascontiguousarray(np.concatenate([parts[n] for n, _ in CST], axis=1))


def _cols(a):
    return np.asarray(a).reshape(-1, P).T


def _vectors(x):
    taps = lambda w: np.asarray(w).reshape(w.shape[0], -1, P).transpose(2, 1, 0).reshape(P, -1)
    w_in = np.asarray(x["a_w_in_2"])[0]
    parts = {
        "c": _cols(x["c"][0]), "b_ada": _cols(x["b_ada"][0]), "b_dw_a": _cols(x["b_dw_a"][0]),
        "ln_a_g": _cols(x["ln_a_g"][0]), "ln_a_b": _cols(x["ln_a_b"][0]), "pool_scale": _cols(x["pool_scale"][0]),
        "ln1_g": _cols(x["ln1_g"][0]), "ln1_b": _cols(x["ln1_b"][0]), "b_dw_f": _cols(x["b_dw_f"][0]),
        "w_dw_f": taps(x["w_dw_f"][0]), "w_dw_a": taps(x["w_dw_a"][0]), "ln2_g": _cols(x["ln2_g"][0]),
        "ln2_b": _cols(x["ln2_b"][0]), "a_conv": taps(x["a_conv_2"][0]), "a_norm_g": _cols(x["a_norm_g_2"][0]),
        "ln1_g_2": _cols(x["ln1_g_2"]), "ln1_b_2": _cols(x["ln1_b_2"]), "ln2_g_2": _cols(x["ln2_g_2"]),
        "ln2_b_2": _cols(x["ln2_b_2"]), "a_log": np.broadcast_to(x["a_a_log_2"][0], (P, 8)),
        "dt": np.broadcast_to(x["a_dt_bias_2"][0], (P, 8)),
        "w_ba": w_in[:, 4096:4112].reshape(8, P, 16).transpose(1, 0, 2).reshape(P, 128),
    }
    return np.ascontiguousarray(np.concatenate([parts[n] for n, _ in VEC], axis=1))


def _nmaj(w):
    return w.reshape(8, P, -1, P).transpose(2, 1, 0, 3).reshape(-1, P, 1024)


def _weights(x):
    g = {k: np.asarray(v) for k, v in x.items()}
    ada = _nmaj(g["w_ada"][0])
    units = {
        "ada": [ada[8 * ADA[n // 8] + n % 8] for n in range(48)],
        "in": _nmaj(g["w_in"][0]), "pw": g["w_pw_a"][0].reshape(4, P, 1024),
        "pool": [g["w_pool"][0].transpose(1, 0, 2).reshape(P, 1024)],
        "out": g["w_out"][0].reshape(8, P, 1024), "up": _nmaj(g["w_up"][0]),
        "down": g["w_down"][0].reshape(FF, P, 1024), "gdn": _nmaj(g["a_w_in_2"][0][:, 0:4096]),
        "gout": g["a_w_out_2"][0].reshape(8, P, 1024), "qkv": _nmaj(g["b_w_qkv_2"][0][:, 0:2048]),
        "vt": g["b_w_qkv_2"][0][:, 2048:3072].reshape(8, P, 1024), "bout": g["b_w_out_2"][0].reshape(8, P, 1024),
        "w130": _nmaj(g["f_w13_2"][0]), "w20": g["f_w2_2"][0].reshape(FF, P, 1024),
        "w131": _nmaj(g["f_w13_2"][1]), "w21": g["f_w2_2"][1].reshape(FF, P, 1024),
    }
    return np.stack([units[k][n] for k, n in PLAN])


def kernel(**inputs):
    import concourse.bacc as _bacc
    from concourse.bass_utils import run_bass_kernel_spmd as _run

    nc = _bacc.Bacc("TRN2", target_bir_lowering=False, num_devices=1)
    x = np.asarray(inputs["x"])[0]
    arrays = {
        "in_w": _weights(inputs),
        "in_v": _vectors(inputs),
        "in_c": _constants(),
        "in_x": np.ascontiguousarray(x.T.reshape(8, P, S).transpose(1, 0, 2)),
    }
    aps = {k: nc.dram_tensor(k, a.shape, F, kind="ExternalInput").ap() for k, a in arrays.items()}
    out = nc.dram_tensor("out", (1, S, D), F, kind="ExternalOutput").ap()
    program(nc, aps["in_w"], aps["in_v"], aps["in_c"], aps["in_x"], out.rearrange("b (c p) d -> (b c) p d", c=2))
    r = _run(nc, [arrays], core_ids=[0])
    return r.results[0]["out"]
```

```python
from contextlib import ExitStack

import numpy as np

import concourse.bass as bass
from concourse import mybir

F = mybir.dt.float32
FR = mybir.dt.float32r
ALU = mybir.AluOpType
ACT = mybir.ActivationFunctionType
AX = mybir.AxisListType

P = 128
S = 256
D = 1024
NC = D // P
FF = 22
HEADS = 8
ALPHA1 = 2.0 ** 0.25
ALPHA2 = 4.0 ** 0.25
LN_EPS = 1e-5
NORM_EPS = 1e-6
RAW = 11
SPLIT = 5
NEG = -1e30

VEC = [("b_ada", 48), ("b_dw_a", 4), ("ln_a_g", 4), ("ln_a_b", 4), ("pool_scale", 8), ("ln1_g", 8),
       ("ln1_b", 8), ("b_dw_f", 44), ("w_dw_f", 132), ("w_dw_a", 124), ("ln2_g", 8), ("ln2_b", 8),
       ("a_conv", 96), ("a_norm_g", 1), ("ln1_g_2", 16), ("ln1_b_2", 16), ("ln2_g_2", 16), ("ln2_b_2", 16),
       ("a_log", 8), ("dt", 8), ("w_ba", 128)]
VOFF = {}
_n = 0
for _name, _k in VEC:
    VOFF[_name] = _n
    _n += _k
NVEC = _n

CST = [("ident", 128), ("tri", 128), ("mlow", 128), ("mstrict", 128), ("caus", 128), ("lev", 7 * 128),
       ("levT1", 128), ("cos", 256), ("sin", 256), ("icnt", 64), ("sel", 240)]
COFF = {}
_n = 0
for _name, _k in CST:
    COFF[_name] = _n
    _n += _k
NCST = _n

MODS = {"sh1": 0, "sc1": 8, "g1": 16, "sh2": 24, "sc2": 32, "g2": 40}


def stream_plan():
    w = []
    for t in range(4):
        w += [("in", 4 + t), ("in", t)]
    w += [("in", 8 + t) for t in range(4)]
    w += [("in", 12 + t) for t in range(8)] + [("pool", 0)] + [("in", 20 + t) for t in range(8)]
    w += [("pw", k) for k in range(4)] + [("out", k) for k in range(8)]
    ffn = []
    for j in range(FF):
        ffn += [("up", j), ("up", FF + j)]
        if j >= 1:
            ffn += [("down", j - 1)]
    ffn += [("down", FF - 1)]
    w += ffn
    w += [("gdn", t) for t in range(32)] + [("gout", k) for k in range(8)]

    def swiglu(i):
        out = []
        for j in range(FF):
            out += [(f"w13{i}", j), (f"w13{i}", FF + j)]
            if j >= 1:
                out += [(f"w2{i}", j - 1)]
        return out + [(f"w2{i}", FF - 1)]

    w += swiglu(0)
    w += [("qkv", t) for t in range(16)] + [("vt", k) for k in range(8)] + [("bout", k) for k in range(8)]
    w += swiglu(1)
    plan = [("ada", n) for n in range(16)]
    rest = [("ada", n) for n in range(16, 48)]
    for i, u in enumerate(w):
        plan.append(u)
        if rest and (i >= 41 or i % 3 < 2):
            plan.append(rest.pop(0))
    return plan


PLAN = stream_plan()


def program(nc, wts, vecs, csts, xT, crep, out):
    with ExitStack() as ctx:
        def sb(name, shape, dt=F):
            return ctx.enter_context(nc.sbuf_tensor(name, shape, dt))

        def sem(name):
            return ctx.enter_context(nc.semaphore(name))

        raw = sb("raw", [P, RAW, 1024])
        hi = sb("hi", [P, SPLIT, 1024], FR)
        lo = sb("lo", [P, SPLIT, 1024], FR)
        vec = sb("vec", [P, NVEC])
        cst = sb("cst", [P, NCST])
        ones = sb("ones", [P, 3, P])
        eps = sb("eps", [P, 2])
        idle = sb("idle", [P, S], FR)
        dummy = sb("dumm", [P, 1])
        mod = sb("mod", [P, 48])
        crow = sb("crow", [P, D])
        xa = sb("xa", [P, NC, S])
        h = sb("h", [P, NC, S])
        hh = sb("hh", [P, NC, S], FR)
        hl = sb("hl", [P, NC, S], FR)
        B = [sb(f"B{i}", [P, NC, S]) for i in range(6)]
        st = sb("st", [P, 2, S])
        ev = sb("ev", [P, 4, S])
        fh = sb("fh", [P, 4, S], FR)
        fl = sb("fl", [P, 4, S], FR)
        Z = sb("Z", [P, 24 * 256])
        ypad = Z[:, 0:4 * 288].rearrange("p (g s) -> p g s", g=4)
        sm = sb("sm", [P, 256])
        bank = [ctx.enter_context(nc.psum_tensor(f"ps{i}", [P, 512], F)) for i in range(8)]

        def V(name, i=0, n=1):
            return vec[:, VOFF[name] + i:VOFF[name] + i + n]

        def C(name, a=0, b=None):
            n = dict(CST)[name]
            return cst[:, COFF[name] + a:COFF[name] + (n if b is None else b)]

        ident = C("ident")

        names = ["sync", "gpsimd", "scalar", "tensor", "vector"]
        done = {e: sem("d_" + e) for e in names[1:]}
        raws = [sem(f"s_raw{i}") for i in range(RAW)]
        s_vec, s_cst, s_x, s_out = sem("s_vec"), sem("s_cst"), sem("s_x"), sem("s_out")
        count = {e: 0 for e in names}
        queue = {e: [] for e in names}
        passed = {e: {} for e in names}

        def put(e, waits, make, sig=True):
            for t in waits:
                if t is None:
                    continue
                s, v = t
                if passed[e].get(id(s), 0) < v:
                    passed[e][id(s)] = v
                    queue[e].append(lambda g, s=s, v=v: g.wait_ge(s, v))
            if sig:
                queue[e].append(lambda g: make(g).then_inc(done[e], 1))
                count[e] += 1
                return (done[e], count[e])
            queue[e].append(lambda g: make(g))
            return None

        def pe(waits, make, sig=True):
            return put("tensor", waits, make, sig)

        def act(waits, o, i, f, sig=True, **kw):
            return put("scalar", waits, lambda g: g.activation(o, i, f, **kw), sig)

        def ve(waits, make):
            return put("vector", waits, make)

        def tt(waits, o, a, b, op, e="vector"):
            return put(e, waits, lambda g: g.tensor_tensor(o, a, b, op))

        def MM(o, l, r, start, stop):
            return lambda g: g.matmul(o, l, r, start=start, stop=stop, skip_group_check=True)

        def TR(o, i, idn):
            return lambda g: g.transpose(o, i, idn)

        def RC(o, i):
            return lambda g: g.reciprocal(o, i)

        def RD(o, i, ax, op):
            return lambda g: g.tensor_reduce(o, i, ax, op)

        def SH(o, i):
            return lambda g: g.stream_shuffle(o, i, [(p + 16) % 32 for p in range(32)])

        def ts(waits, o, a, s1, s2, op0, op1=None, e="vector"):
            if op1 is None:
                return put(e, waits, lambda g: g.tensor_scalar(o, a, s1, None, op0))
            return put(e, waits, lambda g: g.tensor_scalar(o, a, s1, s2, op0, op1))

        def stt(waits, o, a, s, b, op0, op1):
            return put("vector", waits, lambda g: g.scalar_tensor_tensor(out=o, in0=a, scalar=s, in1=b, op0=op0,
                                                                         op1=op1))

        def cp(waits, o, i, e="vector"):
            return put(e, waits, lambda g: g.tensor_copy(o, i))

        sent = [0]
        fed = [0]
        nsplit = [0]
        ready = []
        used = []

        def send(tok):
            i = sent[0]
            if i >= len(PLAN):
                return
            sent[0] += 1
            for t in [tok] if tok else []:
                s, v = t
                if passed["sync"].get(id(s), 0) < v:
                    passed["sync"][id(s)] = v
                    queue["sync"].append(lambda g, s=s, v=v: g.wait_ge(s, v))
            src = wts[i]
            queue["sync"].append(lambda g: g.dma_start(raw[:, i % RAW, :], src).then_inc(raws[i % RAW], 16))

        def landed(i):
            return (raws[i % RAW], 16 * (i // RAW + 1))

        released = {}

        def release(i, tok):
            released[i] = tok
            while sent[0] < len(PLAN) and sent[0] - RAW in released:
                send(released[sent[0] - RAW])

        late = []

        def run_late(force=False):
            while late and (force or late[0][0] + 2 <= len(used)):
                late.pop(0)[1]()

        modtok = {}

        def ada(i, n, r):
            name = ["sh1", "sc1", "g1", "sh2", "sc2", "g2"][MB_ORDER[n // 8]]
            mcol = mod[:, MODS[name] + n % 8:MODS[name] + n % 8 + 1]
            t = put("vector", [landed(i), cstok], lambda g: g.tensor_tensor_reduce(
                r, r, crow[:, :], 1.0, 0.0, ALU.mult, ALU.add, mcol))
            if n % 8 == 7:
                col = MODS[name]
                one = 1.0 if name[:2] == "sc" else 0.0
                modtok[name] = stt([t, t_vec], mod[:, col:col + 8], mod[:, col:col + 8], one, V("b_ada", col, 8),
                                   ALU.add, ALU.add)
            release(i, t)

        def feed_one():
            i = fed[0]
            fed[0] += 1
            while sent[0] <= i:
                late.pop(0)[1]()
            kind, n = PLAN[i]
            r = raw[:, i % RAW, :]
            if kind == "ada":
                late.append((len(used), lambda: ada(i, n, r)))
                return False
            j = nsplit[0]
            nsplit[0] += 1
            free = used[j - SPLIT] if j >= SPLIT else None
            a = act([landed(i), free], hi[:, j % SPLIT, :], r, ACT.Copy)
            b = tt([a, landed(i), free], lo[:, j % SPLIT, :], r, hi[:, j % SPLIT, :].bitcast(F), ALU.subtract)
            ready.append(b)
            release(i, b)
            return True

        MB_ORDER = [1, 0, 2, 4, 3, 5]

        def feed():
            for _ in range(2):
                if nsplit[0] - len(used) >= SPLIT or fed[0] >= len(PLAN):
                    return
                while fed[0] < len(PLAN) and not feed_one():
                    pass

        def spin(n):
            for _ in range(n):
                pe([t_ones], MM(bank[7][:, 0:S], idle[:, 0:P], idle[:, :], True, True), False)

        bg = []

        def background(n):
            for _ in range(min(n, len(bg))):
                bg.pop(0)()

        order = [u for u in PLAN if u[0] != "ada"]

        def take(kind, n, ahead=0):
            run_late()
            j = len(used) + ahead
            assert order[j] == (kind, n), (order[j], kind, n)
            while nsplit[0] <= j:
                feed()
            return j, hi[:, j % SPLIT, :], lo[:, j % SPLIT, :], ready[j]

        def finish(tok):
            used.append(tok)

        def mm3(o, wh, wl, xh, xl, waits, first, last, sig, flip=False):
            for n, (a, b) in enumerate(((wh, xh), (wh, xl), (wl, xh))):
                l, r = (b, a) if flip else (a, b)
                t = pe(waits if n == 0 else [], MM(
                    o, l, r, start=(first and n == 0), stop=(last and n == 2)),
                    sig and n == 2)
            return t

        def nmaj(kind, n, o, xh, xl, xt, free):
            j, wh, wl, t = take(kind, n)
            for k in range(8):
                w = [t, xt[k]] + (free if k == 0 else [])
                last = mm3(o, wh[:, k * 128:k * 128 + 128], wl[:, k * 128:k * 128 + 128], xh[:, k, :], xl[:, k, :],
                           w, k == 0, k == 7, k == 7)
            finish(last)
            return last

        def acc(b0, n):
            return bank[b0 + n // 2][:, (n % 2) * S:(n % 2) * S + S]

        def kmaj(kind, k, b0, xh, xl, xt, first, last, free):
            j, wh, wl, t = take(kind, k)
            toks = []
            for n in range(8):
                w = [t, xt] + (free if n == 0 else [])
                tok = mm3(acc(b0, n), wh[:, n * 128:n * 128 + 128], wl[:, n * 128:n * 128 + 128], xh, xl, w,
                          first and n % 2 == 0, last, n % 2 == 1)
                toks.append(tok)
            toks = [toks[n | 1] for n in range(8)]
            finish(toks[-1])
            return toks

        s_c = sem("s_c")
        queue["sync"].append(lambda g: g.dma_start(crow[:, :], crep).then_inc(s_c, 16))
        queue["sync"].append(lambda g: g.dma_start(vec[:, :], vecs).then_inc(s_vec, 16))
        queue["sync"].append(lambda g: g.dma_start(xa[:, :, :], xT).then_inc(s_x, 16))
        t_vec, t_x, t_cst = (s_vec, 16), (s_x, 16), (s_cst, 16)
        for i in range(RAW):
            send(None)
        queue["scalar"].append(lambda g: g.dma_start(cst[:, :], csts).then_inc(s_cst, 16))

        put("gpsimd", [], lambda g: g.memset(idle[:, :].bitcast(F), 1.0))
        t_ones = put("gpsimd", [], lambda g: g.memset(ones[:, 0, :], 1.0 / 1024))
        t_ones = put("gpsimd", [], lambda g: g.memset(ones[:, 1, :], 1.0 / 512))
        t_ones = put("gpsimd", [], lambda g: g.memset(ones[:, 2, :], 1.0))
        t_ones = put("gpsimd", [], lambda g: g.memset(eps[:, 0:1], LN_EPS))
        t_ones = put("gpsimd", [], lambda g: g.memset(eps[:, 1:2], NORM_EPS))
        t_ones = put("gpsimd", [], lambda g: g.memset(ypad[:, :, 0:32], 0.0))

        cstok = act([(s_c, 16)], crow[:, :], crow[:, :], ACT.Silu)

        def bc(a, n):
            return a.unsqueeze(1).to_broadcast([P, n, S])

        def stats_rstd(y, ytoks, nch, one, sq, yc, bm, bv, free):
            for k in range(nch):
                m = pe([ytoks[k], t_ones] + free, MM(bank[bm][:, 0:S], ones[:, one, :],
                       y[:, k, :], start=(k == 0), stop=(k == nch - 1)), k == nch - 1)
            ct = []
            for k in range(0, nch, 2):
                c = tt([m] + free, yc[:, k:k + 2, :], y[:, k:k + 2, :], bc(bank[bm][:, 0:S], 2), ALU.subtract)
                q = act([c], sq[:, k:k + 2, :], yc[:, k:k + 2, :], ACT.Square)
                ct += [c, c]
                for kk in (k, k + 1):
                    v = pe([q], MM(bank[bv][:, 0:S], ones[:, one, :], sq[:, kk, :], start=(kk == 0),
                                  stop=(kk == nch - 1)), kk == nch - 1)
            if used:
                spin(26)
            s = act([v], st[:, 0, :], bank[bv][:, 0:S], ACT.Sqrt, bias=eps[:, 0:1])
            r = ve([s], RC(st[:, 1, :], st[:, 0, :]))
            return ct, r, m, v

        def apply_norm(ct, r, nch, yc, gain, bias, o, gtoks=(), oh=None, ol=None, free=()):
            toks = []
            held = []

            def low(kk, v, b):
                toks.append(tt([v, b, *free], ol[:, kk, :], o[:, kk, :], oh[:, kk, :].bitcast(F), ALU.subtract))

            for k in range(0, nch, 2):
                a = tt([r, ct[k]], yc[:, k:k + 2, :], yc[:, k:k + 2, :], bc(st[:, 1, :], 2), ALU.mult)
                late_lows, held = held, []
                for kk in (k, k + 1):
                    if oh is not None:
                        b = act([a, *gtoks, *free], oh[:, kk, :], yc[:, kk, :], ACT.Identity, scale=gain(kk),
                                bias=bias(kk))
                    if late_lows:
                        low(*late_lows.pop(0))
                    v = ts([a, *gtoks], o[:, kk, :], yc[:, kk, :], gain(kk), bias(kk), ALU.mult, ALU.add)
                    if oh is not None:
                        held.append((kk, v, b))
                    else:
                        toks.append(v)
            for x in held:
                low(*x)
            return toks

        def norm(y, ytoks, nch, one, sq, yc, bm, bv, free, gain, bias, o, gtoks=(), oh=None, ol=None):
            ct, r, m, v = stats_rstd(y, ytoks, nch, one, sq, yc, bm, bv, free)
            return apply_norm(ct, r, nch, yc, gain, bias, o, gtoks, oh, ol)

        def warm(f):
            act([t_ones], dummy[:, 0:1], ones[:, 2, 0:1], f)

        def split(src, toks, oh, ol, n=NC, free=()):
            out = []
            for k in range(n):
                a = act([toks[k], *free], oh[:, k, :], src[:, k, :], ACT.Copy)
                out.append(tt([a], ol[:, k, :], src[:, k, :], oh[:, k, :].bitcast(F), ALU.subtract))
            return out

        def modcol(name):
            return lambda k: mod[:, MODS[name] + k:MODS[name] + k + 1]

        for _ in range(8):
            feed_one()
        run_late(True)
        ct, r0, _, _ = stats_rstd(xa, [t_x] * 8, 8, 0, B[0], B[1], 0, 1, [])
        for _ in range(8):
            feed_one()
        run_late(True)
        feed()
        ht = apply_norm(ct, r0, 8, B[1], modcol("sc1"), modcol("sh1"), h, [modtok["sc1"], modtok["sh1"]], hh, hl)
        xs = B[2]

        def scale_x(k, toks):
            return act([toks[k]], xs[:, k, :], xa[:, k, :], ACT.Copy, scale=ALPHA1)

        nb = [0]
        pfree = {b: [] for b in range(8)}

        early = {}

        def start_tiles(units, banks):
            jobs = []
            for i, (kind, n) in enumerate(units):
                feed()
                b = banks[nb[0] % len(banks)]
                nb[0] += 1
                jobs.append((kind, n, b, take(kind, n, i)))
            for k in range(8):
                for kind, n, b, (j, wh, wl, t) in jobs:
                    w = [t, ht[k]] + (pfree[b] if k == 0 else [])
                    early[kind, n] = (b, mm3(bank[b][:, 0:S], wh[:, k * 128:k * 128 + 128], wl[:, k * 128:k * 128 + 128],
                                             hh[:, k, :], hl[:, k, :], w, k == 0, k == 7, k == 7))
            for kind, n, b, _ in jobs:
                finish(early[kind, n][1])

        def tile_out(kind, n, banks, x=None):
            if (kind, n) in early:
                feed()
                return early.pop((kind, n))
            b = banks[nb[0] % len(banks)]
            nb[0] += 1
            feed()
            t = nmaj(kind, n, bank[b][:, 0:S], hh, hl, ht, pfree[b])
            return b, t

        R4 = [2, 3, 4, 5]
        start_tiles([("in", 4), ("in", 0)], R4)
        ya = ypad
        yt = []
        pad = t_ones
        for t in range(4):
            b, m = tile_out("in", 4 + t, R4)
            a = act([m], ev[:, t, :], bank[b][:, 0:S], ACT.Sigmoid)
            pfree[b] = [a]
            b, m = tile_out("in", t, R4)
            v = tt([m, a, pad], ya[:, t, 32:32 + S], bank[b][:, 0:S], ev[:, t, :], ALU.mult)
            pfree[b] = [v]
            yt.append(v)

        cv = B[0]
        cvt = [None] * 4

        def conv_tap(i):
            for t in range(4):
                w = V("w_dw_a", t * 31 + i)
                src = ya[:, t, 2 + i:2 + i + S]
                if i == 0:
                    cvt[t] = ts([yt[t], t_vec, pad], cv[:, t, :], src, w, V("b_dw_a", t), ALU.mult, ALU.add)
                else:
                    cvt[t] = stt([cvt[t]], cv[:, t, :], src, w, cv[:, t, :], ALU.mult, ALU.add)

        for i in range(31):
            bg.append(lambda i=i: conv_tap(i))

        pu = B[1][:, :, :].rearrange("p c s -> p (c s)")
        up = pu[:, 0:4 * 272].rearrange("p (g s) -> p g s", g=4)
        pz = put("gpsimd", [ht[7]], lambda g: g.memset(up[:, :, 0:16], 0.0))
        ut = []
        for t in range(4):
            b, m = tile_out("in", 8 + t, R4)
            a = act([m, ht[7]], up[:, t, 16:272], bank[b][:, 0:S], ACT.Copy)
            pfree[b] = [a]
            ut.append(a)
            background(2)
        pa, pb_ = B[2], B[3]
        ws = [pa[:, 0:5, :].rearrange("p c s -> p (c s)")[:, 0:1088].rearrange("p (g s) -> p g s", g=4),
              pb_[:, 0:5, :].rearrange("p c s -> p (c s)")[:, 0:1088].rearrange("p (g s) -> p g s", g=4)]
        src = up
        tk = ut[3]
        lv = []
        for lev in range(4):
            g0 = lev
            sh = 1 << lev
            dst = ws[lev % 2]
            t1 = tt([tk, pz, ut[3]], dst[:, g0:4, sh:272], src[:, g0:4, sh:272], src[:, g0:4, 0:272 - sh], ALU.add)
            t2 = cp([tk, t1], dst[:, g0:4, 0:sh], src[:, g0:4, 0:sh])
            lv.append((dst, t2))
            src, tk = dst, t2
        pooled = h
        pt = []
        for g in range(4):
            sgrp = lv[g][0][:, g, 16:272]
            a = tt([lv[3][1], t_cst], pooled[:, g, 0:16], sgrp[:, 0:16], C("icnt", g * 16, g * 16 + 16), ALU.mult)
            a = ts([a], pooled[:, g, 16:S], sgrp[:, 16:S], 0.5 ** (g + 1), None, ALU.mult)
            pt.append(tt([a], pooled[:, g, :], pooled[:, g, :], up[:, g, 16:272], ALU.subtract))
        ph, plo = fh, fl
        pst = []
        for g in range(4):
            a = act([pt[g]], ph[:, g, :], pooled[:, g, :], ACT.Copy)
            pst.append(tt([a], plo[:, g, :], pooled[:, g, :], ph[:, g, :].bitcast(F), ALU.subtract))
        ga = B[4]
        gat = []
        for n in range(8):
            b, m = tile_out("in", 12 + n, R4)
            a = act([m, ht[7]], ga[:, n, :], bank[b][:, 0:S], ACT.Sigmoid)
            pfree[b] = [a]
            gat.append(a)
            background(2)
        feed()
        j, wh, wl, wt = take("pool", 0)
        ybt = []
        yb = B[5]
        for n in range(8):
            b = R4[nb[0] % 4]
            nb[0] += 1
            m = mm3(bank[b][:, 0:S], wh[:, n * 128:n * 128 + 128], wl[:, n * 128:n * 128 + 128], ph[:, n // 2, :],
                    plo[:, n // 2, :], [wt, pst[n // 2], *pfree[b]], True, True, True)
            a = act([m, t_vec], yb[:, n, :], bank[b][:, 0:S], ACT.Copy, scale=V("pool_scale", n))
            pfree[b] = [a]
            ybt.append(a)
        finish(m)
        mg = B[1]
        for n in range(8):
            b, m = tile_out("in", 20 + n, R4)
            a = act([m, yt[n] if n < 4 else ybt[n - 4]], ev[:, n % 4, :], bank[b][:, 0:S], ACT.Sigmoid)
            pfree[b] = [a]
            ybt[n] = tt([a, ybt[n]], yb[:, n, :], yb[:, n, :], ev[:, n % 4, :], ALU.mult)
            background(2)
        background(99)
        yn = B[2]
        at = norm(cv, cvt, 4, 1, B[3], yn, 0, 1, [pst[3], lv[3][1]], lambda k: V("ln_a_g", k), lambda k: V("ln_a_b", k), yn)
        yh, yl = hh[:, 4:8, :], hl[:, 4:8, :]
        gates_done = used[-1]
        s4 = []
        for k in range(4):
            a = act([at[k]], cv[:, k, :], yn[:, k, :], ACT.Silu)
            b = cp([a, gates_done], yh[:, k, :], cv[:, k, :])
            s4.append(tt([b], yl[:, k, :], cv[:, k, :], yh[:, k, :].bitcast(F), ALU.subtract))
        for k in range(4):
            feed()
            toks = kmaj("pw", k, 2, yh[:, k, :], yl[:, k, :], s4[k], k == 0, k == 3,
                        [t for b in R4 for t in pfree[b]])
        mt = []
        for n in range(8):
            a = tt([toks[n], gat[n]], mg[:, n, :], acc(2, n), ga[:, n, :], ALU.mult)
            pfree[2 + n // 2] = [a]
            mt.append(tt([a, ybt[n]], mg[:, n, :], mg[:, n, :], yb[:, n, :], ALU.add))
        mt = split(mg, mt, hh, hl)
        xst = [scale_x(k, [t_x] * 8) for k in range(8)]
        for k in range(8):
            feed()
            toks = kmaj("out", k, 2, hh[:, k, :], hl[:, k, :], mt[k], k == 0, k == 7,
                        [t for b in R4 for t in pfree[b]])

        def residual(toks, b0, gate, gtok, alpha):
            out = []
            warm(ACT.Sqrt)
            if gate is None:
                for n in range(0, 8, 2):
                    v = xa[:, n:n + 2, :]
                    a = bank[b0 + n // 2][:, :].rearrange("p (a b) -> p a b", a=2)
                    t = stt([toks[n]], v, v, alpha, a, ALU.mult, ALU.add)
                    out += [t, t]
                    pfree[b0 + n // 2] = [t]
                return out
            for n in range(8):
                t = stt([toks[n], gtok, xst[n]], xa[:, n, :], acc(b0, n), gate(n), xs[:, n, :], ALU.mult, ALU.add)
                out.append(t)
                pfree[b0 + n // 2] = [t]
            return out

        rt = residual(toks, 2, modcol("g1"), modtok["g1"], ALPHA1)
        x1 = norm(xa, rt, 8, 0, B[0], B[1], 0, 1, [], lambda k: V("ln1_g", k), lambda k: V("ln1_b", k), xa)
        ht = norm(xa, x1, 8, 0, B[0], B[1], 0, 1, [], modcol("sc2"), modcol("sh2"), h,
                  [modtok["sc2"], modtok["sh2"]], hh, hl)
        xst = [scale_x(k, x1) for k in range(8)]

        R3 = [4, 5, 6]

        def ffn(kup, kdown, conv):
            ftoks = []
            ffree = []

            def down(j):
                feed()
                fr = [t for b in range(4) for t in pfree[b]] if j == 0 else []
                ts_ = kmaj(kdown, j, 0, fh[:, j % 4, :], fl[:, j % 4, :], ftoks[j], j == 0, j == FF - 1, fr)
                ffree.append(ts_[-1])
                return ts_

            evf = [None] * 4
            start_tiles([(kup, 0), (kup, FF), (kup, 1)], R3)
            for j in range(FF):
                got = []
                for half in (0, 1):
                    n = j + half * FF
                    b, m = tile_out(kup, n, R3)
                    slot = (2 * j + half) % 4
                    e = ev[:, slot, :]
                    p0 = bank[b][:, 0:S]
                    if conv:
                        a = act([m, evf[slot], t_vec], e, p0, ACT.Identity, scale=V("w_dw_f", n * 3 + 2),
                                bias=V("b_dw_f", n))
                        a = stt([a, m], e[:, 1:], p0[:, 0:S - 1], V("w_dw_f", n * 3 + 1), e[:, 1:], ALU.mult, ALU.add)
                        a = stt([a], e[:, 2:], p0[:, 0:S - 2], V("w_dw_f", n * 3), e[:, 2:], ALU.mult, ALU.add)
                        pfree[b] = [a]
                        if half == 1:
                            a = act([a], e, e, ACT.Gelu_apprx_tanh)
                    else:
                        a = act([m, evf[slot]], e, p0, ACT.Silu if half == 0 else ACT.Copy)
                        pfree[b] = [a]
                    got.append(a)
                s0, s1 = (2 * j) % 4, (2 * j + 1) % 4
                f = tt(got, ev[:, s0, :], ev[:, s0, :], ev[:, s1, :], ALU.mult)
                fr = [ffree[j - 4]] if j >= 4 else []
                a = act([f] + fr, fh[:, j % 4, :], ev[:, s0, :], ACT.Copy)
                z = tt([a], fl[:, j % 4, :], ev[:, s0, :], fh[:, j % 4, :].bitcast(F), ALU.subtract)
                evf[s0] = z
                evf[s1] = f
                ftoks.append(z)
                if j >= 1:
                    down(j - 1)
            return down(FF - 1)

        evlast = [None]
        toks = ffn("up", "down", True)
        rt = residual(toks, 0, modcol("g2"), modtok["g2"], ALPHA1)
        x2 = norm(xa, rt, 8, 0, B[0], B[1], 4, 5, pfree[4] + pfree[5], lambda k: V("ln2_g", k), lambda k: V("ln2_b", k), xa, (), hh, hl)
        ht = x2

        qb, kb, vb, zb = B[2], B[3], B[4], B[5]
        R2 = [4, 5]
        pfree[4], pfree[5] = [x2[0]], [x2[0]]

        def ba():
            for c in range(2):
                for k in range(8):
                    t = pe([x2[k], t_vec] + pfree[6], MM(
                        bank[6][:, c * 16:c * 16 + 16], xa[:, k, c * 128:c * 128 + 128], V("w_ba", k * 16, 16),
                        start=(c == 0 and k == 0), stop=(k == 7)), k == 7)
            return t

        pba = bank[6][:, 0:32].rearrange("p (c n) -> p c n", c=2)

        def smv(o, n=2):
            return sm[:, o:o + 8 * n].rearrange("p (c n) -> p c n", c=n)

        beta = smv(0)
        gg = smv(16)
        ex = smv(96)
        ax = smv(112)
        rl = smv(128)
        soon = []

        def conv4(n, dst, b, m, toks):
            p0 = bank[b][:, 0:S]
            w = lambda i: V("a_conv", n * 4 + i)
            a = act([m, t_vec], dst, p0, ACT.Copy, scale=w(3))
            for i in (2, 1, 0):
                d = 3 - i
                a = stt([a, m], dst[:, d:], p0[:, 0:S - d], w(i), dst[:, d:], ALU.mult, ALU.add)
            pfree[b] = [a]
            soon.append(lambda: toks.append(act([a], dst, dst, ACT.Silu)))
            if len(soon) > 1:
                soon.pop(0)()

        def settle():
            while soon:
                soon.pop(0)()

        norms = {}

        def head_norms(dst, sqs, sqb, scale, bsum, bb, key, ready_of, apply):
            def squares(i):
                q = act(ready_of(2 * i) + ready_of(2 * i + 1) + sqs(i), sqb[:, 2 * i:2 * i + 2, :],
                        dst[:, 2 * i:2 * i + 2, :], ACT.Square)
                norms[key, "sq", i] = q

            def sums(i):
                for n in (2 * i, 2 * i + 1):
                    m = pe([norms[key, "sq", i], t_cst] + pfree[bsum], MM(
                        bank[bsum][:, 0:S], C("sel", 112 - 16 * n, 240 - 16 * n), sqb[:, n, :], start=(n == 0),
                        stop=(n == 7)), n % 2 == 1)
                norms[key, "m"] = m

            def root():
                a = act([norms[key, "m"], norms.get("st")], st[:, 0, :], bank[bsum][:, 0:S], ACT.Sqrt,
                        bias=eps[:, 1:2], scale=scale)
                pfree[bsum] = [a]
                norms["st"] = norms[key, "r"] = ve([a, norms.get("rd")], RC(st[:, 1, :], st[:, 0, :]))

            def spread(i):
                for n in (2 * i, 2 * i + 1):
                    m = pe([norms[key, "r"]] + pfree[bb[i % 2]], MM(
                        bank[bb[i % 2]][:, (n % 2) * S:(n % 2) * S + S], ident[:, 16 * n:16 * n + 1].to_broadcast([P, P]),
                        st[:, 1, :], start=(n % 2 == 0), stop=True))
                norms["rd"] = m
                pfree[bb[i % 2]] = [apply(i, m, bank[bb[i % 2]][:, :].rearrange("p (a b) -> p a b", a=2))]

            return ([lambda i=i: squares(i) for i in range(4)], [lambda i=i: sums(i) for i in range(4)], root,
                    [lambda i=i: spread(i) for i in range(4)])

        def l2(dst, toks, scale, sqb, banks, busy, key):
            def apply(i, m, v):
                d = dst[:, 2 * i:2 * i + 2, :]
                toks[2 * i] = toks[2 * i + 1] = stt([m], d, d, scale, v, ALU.mult, ALU.mult)
                return toks[2 * i]

            sq, sm_, root, spread = head_norms(dst, lambda i: busy(), sqb, 1.0, banks[0], banks[1:], key,
                                               lambda n: [toks[n]], apply)
            return sq[0:2] + [sm_[0], sq[2], sm_[1], sq[3], sm_[2], lambda: (sm_[3](), root())] + spread

        qt, kt = [], []
        start_tiles([("gdn", 0), ("gdn", 1)], R2)
        for n in range(8):
            b, m = tile_out("gdn", n, R2)
            conv4(n, qb[:, n, :], b, m, qt)
            if n == 3:
                bat = ba()
            if n == 5:
                bt = act([bat], beta, pba[:, :, 0:8], ACT.Sigmoid)
                at0 = tt([bat, bt, t_vec], ax, pba[:, :, 8:16], V("dt", 0, 8).unsqueeze(1).to_broadcast([P, 2, 8]), ALU.add)
                pfree[6] = [bt, at0]
                a1 = ts([at0], rl, ax, 0.0, None, ALU.max)
                a2 = stt([a1], ex, rl, -2.0, ax, ALU.mult, ALU.add)
                a3 = act([a2], ex, ex, ACT.Exp)
                a3b = act([t_vec], sm[:, 80:88], V("a_log", 0, 8), ACT.Exp)
                a4 = act([a3], ex, ex, ACT.Ln, bias=1.0)
                a5 = tt([a4], ex, ex, rl, ALU.add)
                gt = stt([a5, a3b], gg, ex, -1.0, sm[:, 80:88].unsqueeze(1).to_broadcast([P, 2, 8]), ALU.mult, ALU.mult)
        bg.extend(l2(qb, qt, 128.0 ** -0.5, B[0], [0, 1, 2], lambda: [], "q"))
        bg.insert(0, settle)
        for n in range(8):
            b, m = tile_out("gdn", 8 + n, R2)
            conv4(8 + n, kb[:, n, :], b, m, kt)
            background(1)

        gr = Z[:, 0:2048].rearrange("p (c n s) -> p c n s", c=2, n=8)
        dmat = gr
        gcol = smv(32)
        egc = smv(144)
        nbeg = smv(48)
        kdec = smv(160)
        G = {}

        def gates():
            for c in range(2):
                m = pe([gt, t_cst] + pfree[6], MM(
                    bank[6][:, c * 8:c * 8 + 8], C("tri"), gg[:, c, :], start=(c == 0), stop=True))
            G["gc"] = cp([m], gcol, bank[6][:, 0:16].rearrange("p (c n) -> p c n", c=2))
            pfree[6] = [G["gc"]]
            a = act([G["gc"]], egc, gcol, ACT.Exp)
            G["nbeg"] = stt([a, bt], nbeg, egc, -1.0, beta, ALU.mult, ALU.mult)

        qdec = Z[:, 2048:3072].rearrange("p (n s) -> p n s", n=8)

        def rows(c, q):
            bk = [0, 1, 2, 3][(2 * c + q) % 4]
            for i in range(4):
                hd = 4 * q + i
                m = pe([gt, t_cst] + pfree[bk], MM(
                    bank[bk][:, i * P:i * P + P], gg[:, c, hd:hd + 1].to_broadcast([P, P]), C("tri"),
                    start=(i == 0), stop=True), i == 3)
            for i in range(4):
                hd = 4 * q + i
                G["read"] = a = ts([m, G["gc"]], gr[:, c, hd, :], bank[bk][:, i * P:i * P + P], gcol[:, c, hd:hd + 1], -1.0,
                       ALU.subtract, ALU.mult)
                if c == 0:
                    G["read"] = G["kl", hd] = ts([m, G["gc"]], kdec[:, 0, hd:hd + 1], bank[bk][:, i * P + P - 1:i * P + P],
                                     gcol[:, c, hd:hd + 1], None, ALU.subtract)
            v = gr[:, c, 4 * q:4 * q + 4, :]
            a = ts([a], v, v, 0.0, None, ALU.min)
            a = act([a], v, v, ACT.Exp)
            a = tt([a, t_cst], v, v, C("mlow").unsqueeze(1).to_broadcast([P, 4, P]), ALU.mult)
            G["D", c, q] = a
            fr = [a]
            if c == 1:
                qv = qdec[:, 4 * q:4 * q + 4, :].rearrange("p a b -> p (a b)")
                e = act([m, G["read"]], qv, bank[bk][:, :], ACT.Exp)
                fr.append(e)
                G["qd", q] = tt([e, qt[4 * q + 3]], qdec[:, 4 * q:4 * q + 4, :], qdec[:, 4 * q:4 * q + 4, :],
                                qb[:, 4 * q:4 * q + 4, P:2 * P], ALU.mult)
            pfree[bk] = fr
            if c == 0 and q == 1:
                G["kdec"] = act([G["kl", 7]], kdec[:, 0, :], kdec[:, 0, :], ACT.Exp)

        bg.append(gates)
        for c in range(2):
            for q in range(2):
                bg.append(lambda c=c, q=q: rows(c, q))
        bg.extend(l2(kb, kt, 1.0, B[0], [3, 1, 2], lambda: [norms["q", "m"]], "k"))

        bg.insert(0, settle)
        lt = Z[:, 3072:5120].rearrange("p (g i s) -> p g i s", g=4, i=4)
        tm = B[0][:, :, :].rearrange("p a b -> p (a b)").rearrange("p (g i s) -> p g i s", g=4, i=4)
        tT = B[1][:, :, :].rearrange("p a b -> p (a b)").rearrange("p (g i s) -> p g i s", g=4, i=4)
        aT = Z[:, 0:2048].rearrange("p (g i s) -> p g i s", g=4, i=4)
        pm = ev[:, :, :].rearrange("p a b -> p (a b)").rearrange("p (g i s) -> p g i s", g=2, i=4)
        T = {}
        npm = [0]
        BK = [0, 1, 2, 3, 6]
        nbk = [0]

        def nextbank():
            b = BK[nbk[0] % 5]
            nbk[0] += 1
            return b

        def ga_(c, q):
            g_ = 2 * c + q
            b1 = nextbank()
            sl = slice(c * P, c * P + P)
            for i in range(4):
                hd = 4 * q + i
                m = pe([kt[hd]] + pfree[b1], MM(
                    bank[b1][:, i * P:i * P + P], kb[:, hd, sl], kb[:, hd, sl], start=(i == 0), stop=True), i == 3)
            b2 = nextbank()
            for i in range(4):
                hd = 4 * q + i
                m2 = pe([kt[hd], qt[hd]] + pfree[b2], MM(
                    bank[b2][:, i * P:i * P + P], qb[:, hd, sl], kb[:, hd, sl], start=(i == 0), stop=True), i == 3)
            x = pm[:, npm[0] % 2]
            w = T.get(("pm", npm[0] % 2))
            for i in range(4):
                hd = 4 * q + i
                a = stt([m, G["D", c, q], bt, w], x[:, i, :], bank[b1][:, i * P:i * P + P],
                        beta[:, c, hd:hd + 1], gr[:, c, hd, :], ALU.mult, ALU.mult)
            pfree[b1] = [a]
            a = tt([a], x, x, C("mstrict").unsqueeze(1).to_broadcast([P, 4, P]), ALU.mult)
            y = tm[:, g_]
            a2 = tt([a, m2], aT[:, g_], bank[b2][:, :].rearrange("p (i s) -> p i s", i=4), gr[:, c, 4 * q:4 * q + 4, :],
                    ALU.mult)
            pfree[b2] = [a2]
            b3 = nextbank()
            for i in range(4):
                m3 = pe([a, t_cst] + pfree[b3], TR(bank[b3][:, i * P:i * P + P], x[:, i, :], ident),
                        i == 3)
            l = cp([m3], lt[:, g_], bank[b3][:, :].rearrange("p (i s) -> p i s", i=4))
            pfree[b3] = [l]
            b4 = nextbank()
            for i in range(4):
                m4 = pe([a2, t_cst] + pfree[b4], TR(bank[b4][:, i * P:i * P + P], aT[:, g_, i, :],
                                                                           ident), i == 3)
            T["aT", g_] = act([m4], aT[:, g_], bank[b4][:, :].rearrange("p (i s) -> p i s", i=4), ACT.Copy)
            pfree[b4] = [T["aT", g_]]
            idb = ident.unsqueeze(1).to_broadcast([P, 4, P])
            a = tt([a], tm[:, g_], x, C("lev", 0, P).unsqueeze(1).to_broadcast([P, 4, P]), ALU.mult)
            T["T", g_] = tt([a], tm[:, g_], idb, tm[:, g_], ALU.subtract)
            a = tt([l], tT[:, g_], lt[:, g_], C("levT1").unsqueeze(1).to_broadcast([P, 4, P]), ALU.mult)
            T["TT", g_] = tt([a], tT[:, g_], idb, tT[:, g_], ALU.subtract)
            T["L", g_] = l
            T["pm", npm[0] % 2] = T["TT", g_]
            npm[0] += 1

        def level_p(lv_, g_):
            b1 = nextbank()
            for i in range(4):
                m = pe([T["L", g_], T["T", g_]] + pfree[b1], MM(bank[b1][:, i * P:i * P + P], lt[:, g_, i, :],
                                                               tm[:, g_, i, :], start=(i == 0), stop=True), i == 3)
            key = T["slot", g_] = ("pm", npm[0] % 2)
            npm[0] += 1
            a = tt([m, T.get(key), t_cst], pm[:, key[1]], bank[b1][:, :].rearrange("p (i s) -> p i s", i=4),
                   C("lev", lv_ * P, lv_ * P + P).unsqueeze(1).to_broadcast([P, 4, P]), ALU.mult)
            pfree[b1] = [a]
            T["P", g_] = a

        def level_t(lv_, g_):
            a, key = T["P", g_], T["slot", g_]
            x = pm[:, key[1]]
            b3 = nextbank()
            for i in range(4):
                m3 = pe([a, T["TT", g_]] + pfree[b3], MM(bank[b3][:, i * P:i * P + P], x[:, i, :], tT[:, g_, i, :],
                                                        start=(i == 0), stop=True), i == 3)
            m2 = m3
            if lv_ < 6:
                b2 = nextbank()
                for i in range(4):
                    m2 = pe([a, T["TT", g_]] + pfree[b2], MM(bank[b2][:, i * P:i * P + P], tT[:, g_, i, :], x[:, i, :],
                                                            start=(i == 0), stop=True), i == 3)
                T["T", g_] = tt([m2], tm[:, g_], tm[:, g_], bank[b2][:, :].rearrange("p (i s) -> p i s", i=4),
                                ALU.subtract)
                pfree[b2] = [T["T", g_]]
            T[key] = m2
            T["TT", g_] = tt([m3, m2], tT[:, g_], tT[:, g_], bank[b3][:, :].rearrange("p (i s) -> p i s", i=4),
                             ALU.subtract)
            pfree[b3] = [T["TT", g_]]

        rv = h[:, :, :].rearrange("p a b -> p (a b)").rearrange("p (g i s) -> p g i s", g=4, i=4)
        kd = Z[:, 5120:6144].rearrange("p (g i s) -> p g i s", g=2, i=4)
        vt = []

        def tokmaj_v(c, q):
            b1 = nextbank()
            for i in range(4):
                m = pe([vt[4 * q + i], t_cst] + pfree[b1], TR(
                    bank[b1][:, i * P:i * P + P], vb[:, 4 * q + i, c * P:c * P + P], ident), i == 3)
            for i in range(4):
                hd = 4 * q + i
                a = act([m, bt], rv[:, 2 * c + q, i, :], bank[b1][:, i * P:i * P + P], ACT.Copy,
                        scale=beta[:, c, hd:hd + 1])
            pfree[b1] = [a]
            T["rv", 2 * c + q] = a

        def tokmaj_k(q):
            b1 = nextbank()
            for i in range(4):
                m = pe([kt[4 * q + i], t_cst] + pfree[b1], TR(
                    bank[b1][:, i * P:i * P + P], kb[:, 4 * q + i, 0:P], ident), i == 3)
            for i in range(4):
                hd = 4 * q + i
                a = act([m, G["kdec"]], kd[:, q, i, :], bank[b1][:, i * P:i * P + P], ACT.Copy,
                        scale=kdec[:, 0, hd:hd + 1])
            pfree[b1] = [a]
            T["kd", q] = a

        for n in range(8):
            b, m = tile_out("gdn", 16 + n, R2)
            conv4(16 + n, vb[:, n, :], b, m, vt)
            background(3)
        background(99)
        settle()
        for g_ in range(4):
            bg.append(lambda g_=g_: ga_(g_ // 2, g_ % 2))
        steps = [(lv_, g_) for lv_ in range(1, 7) for g_ in range(4)]
        for n, u in enumerate(steps):
            bg.append(lambda u=u: level_p(*u))
            if n:
                bg.append(lambda u=steps[n - 1]: level_t(*u))
        bg.append(lambda: level_t(*steps[-1]))
        for q in range(2):
            bg.append(lambda q=q: tokmaj_k(q))
        for g_ in range(4):
            bg.append(lambda g_=g_: tokmaj_v(g_ // 2, g_ % 2))
        zt = []
        for n in range(8):
            b, m = tile_out("gdn", 24 + n, R2)
            a = act([m], zb[:, n, :], bank[b][:, 0:S], ACT.Silu)
            pfree[b] = [a]
            zt.append(a)
            background(6)
        background(99)
        vn = vb[:, :, :].rearrange("p a b -> p (a b)").rearrange("p (g i s) -> p g i s", g=4, i=4)
        ss = lt
        ot = []
        ob = kb
        for q in range(2):
            b1 = nextbank()
            for i in range(4):
                m = pe([T["TT", q], T["rv", q]] + pfree[b1], MM(
                    bank[b1][:, i * P:i * P + P], tT[:, q, i, :], rv[:, q, i, :], start=(i == 0), stop=True), i == 3)
            a0 = cp([m, T["rv", 3]], vn[:, q], bank[b1][:, :].rearrange("p (i s) -> p i s", i=4))
            pfree[b1] = [a0]
            T["vn", q] = a0
        for q in range(2):
            b2 = nextbank()
            for i in range(4):
                m = pe([T["kd", q], T["vn", q]] + pfree[b2], MM(
                    bank[b2][:, i * P:i * P + P], kd[:, q, i, :], vn[:, q, i, :], start=(i == 0), stop=True), i == 3)
            T["S", q] = act([m, T["TT", 3], T["TT", 2]], ss[:, q], bank[b2][:, :].rearrange("p (i s) -> p i s", i=4),
                            ACT.Copy)
            pfree[b2] = [T["S", q]]
        for q in range(2):
            b3 = nextbank()
            for i in range(4):
                m = pe([T["S", q], kt[7]] + pfree[b3], MM(
                    bank[b3][:, i * P:i * P + P], kb[:, 4 * q + i, P:2 * P], ss[:, q, i, :], start=(i == 0), stop=True), i == 3)
            T["ks", q] = m
            for i in range(4):
                hd = 4 * q + i
                a = stt([m, T["rv", 2 + q], G["nbeg"]], rv[:, 2 + q, i, :], bank[b3][:, i * P:i * P + P],
                        nbeg[:, 1, hd:hd + 1], rv[:, 2 + q, i, :], ALU.mult, ALU.add)
            pfree[b3] = [a]
            T["r1", q] = a
        for q in range(2):
            b1 = nextbank()
            for i in range(4):
                m = pe([T["TT", 2 + q], T["r1", q]] + pfree[b1], MM(
                    bank[b1][:, i * P:i * P + P], tT[:, 2 + q, i, :], rv[:, 2 + q, i, :], start=(i == 0), stop=True), i == 3)
            a = cp([m], vn[:, 2 + q], bank[b1][:, :].rearrange("p (i s) -> p i s", i=4))
            pfree[b1] = [a]
            T["vn", 2 + q] = a
        oh, ol = hh, hl
        for q in range(2):
            b1 = nextbank()
            for i in range(4):
                m = pe([T["vn", q], T["aT", q]] + pfree[b1], MM(
                    bank[b1][:, i * P:i * P + P], vn[:, q, i, :], aT[:, q, i, :], start=(i == 0), stop=True), i == 3)
            o0 = ob[:, 4 * q:4 * q + 4, 0:P]
            t0 = cp([m, T["ks", 0], T["ks", 1], T["kd", 0], T["kd", 1]], o0,
                    bank[b1][:, :].rearrange("p (i s) -> p i s", i=4))
            pfree[b1] = [t0]
            b2 = nextbank()
            for i in range(4):
                pe([T["S", q], G["qd", q]] + pfree[b2], MM(
                    bank[b2][:, i * P:i * P + P], ss[:, q, i, :], qdec[:, 4 * q + i, :], start=(i == 0), stop=False), False)
            for i in range(4):
                m = pe([T["vn", 2 + q], T["aT", 2 + q]], MM(
                    bank[b2][:, i * P:i * P + P], vn[:, 2 + q, i, :], aT[:, 2 + q, i, :], start=False, stop=True), i == 3)
            o1 = ob[:, 4 * q:4 * q + 4, P:2 * P]
            t1 = act([m, T["ks", 0], T["ks", 1]], o1, bank[b2][:, :].rearrange("p (i s) -> p i s", i=4), ACT.Copy)
            pfree[b2] = [t1]
            T["o", q] = (t0, t1)
        sq = qb
        rt_ = [None] * 4

        def gated(i, m, v):
            ov = ob[:, 2 * i:2 * i + 2, :]
            a = stt([m, t_vec], ov, ov, V("a_norm_g"), v, ALU.mult, ALU.mult)
            rt_[i] = tt([a, zt[2 * i + 1]], ov, ov, zb[:, 2 * i:2 * i + 2, :], ALU.mult)
            return a

        warm(ACT.Sqrt)
        osq, osum, oroot, ospread = head_norms(ob, lambda i: [G["qd", 0], G["qd", 1], T["aT", 3]], sq, 1.0 / 128, 4,
                                               [5, 6], "o", lambda n: list(T["o", n // 4]), gated)
        for f in osq + osum + [oroot] + ospread:
            f()
        otk = split(ob, [rt_[n // 2] for n in range(8)], oh, ol)
        for k in range(8):
            feed()
            toks = kmaj("gout", k, 0, oh[:, k, :], ol[:, k, :], otk[k], k == 0, k == 7,
                        [t for b in range(4) for t in pfree[b]])

        def post(toks, g, b, i, parts=(hh, hl)):
            rt = residual(toks, 0, None, None, ALPHA2)
            x = norm(xa, rt, 8, 0, B[0], B[1], 4, 5, pfree[4] + pfree[5], lambda k: V(g, 8 * i + k),
                     lambda k: V(b, 8 * i + k), xa, (), *parts)
            pfree[4], pfree[5] = [x[0]], [x[0]]
            return x

        x3 = post(toks, "ln1_g_2", "ln1_b_2", 0)
        ht = x3
        toks = ffn("w130", "w20", False)
        x4 = post(toks, "ln2_g_2", "ln2_b_2", 0)
        ht = x4

        qq, kk_ = B[2], B[3]
        sw = B[4]

        def rope(dst, toks, n):
            x = dst[0:32, n, :]
            y = sw[0:32, n, :]
            a = ve([toks[n]], SH(y, x))
            b = tt([a, t_cst], y, y, C("sin")[0:32, :], ALU.mult)
            c = tt([b], x, x, C("cos")[0:32, :], ALU.mult)
            toks[n] = tt([c], x, x, y, ALU.add)

        qt, kt = [], []
        start_tiles([("qkv", 0), ("qkv", 1)], R2)
        for n in range(8):
            b, m = tile_out("qkv", n, R2)
            a = act([m], qq[:, n, :], bank[b][:, 0:S], ACT.Copy)
            pfree[b] = [a]
            qt.append(a)
            bg.append(lambda n=n: rope(qq, qt, n))
            if n:
                background(1)
        for n in range(8):
            b, m = tile_out("qkv", 8 + n, R2)
            a = act([m], kk_[:, n, :], bank[b][:, 0:S], ACT.Copy)
            pfree[b] = [a]
            kt.append(a)
            bg.append(lambda n=n: rope(kk_, kt, n))
            background(1)
        background(99)
        SC = 128.0 ** -0.5
        pr = B[0][:, :, :].rearrange("p a b -> p (a b)").rearrange("p (h s) -> p h s", h=8)
        p0 = B[1][:, 0:4, :].rearrange("p a b -> p (a b)").rearrange("p (h s) -> p h s", h=8)
        pT3 = B[4][:, :, :].rearrange("p a b -> p (a b)")[:, 0:1536].rearrange("p (h s) -> p h s", h=4)
        stat = smv(176, 8)
        ABK = [4, 5, 6]
        na = [0]

        def abank():
            b = ABK[na[0] % 3]
            na[0] += 1
            return b

        prt = {}

        def scores(hd):
            b = abank()
            m = pe([qt[hd], kt[hd]] + pfree[b], MM(
                bank[b][:, 0:P], qq[:, hd, 0:P], kk_[:, hd, 0:P], start=True, stop=True))
            m1 = pe([], MM(bank[b][:, P:P + S], qq[:, hd, P:2 * P], kk_[:, hd, :], start=False,
                                           stop=True))
            a = tt([m, m1, t_cst, x4[7]], p0[:, hd, :], bank[b][:, 0:P], C("caus"), ALU.add)
            c = tt([m1, x4[7]], pr[:, hd, P:2 * P], bank[b][:, 2 * P:3 * P], C("caus"), ALU.add)
            c2 = cp([m1], pr[:, hd, 0:P], bank[b][:, P:2 * P])
            pfree[b] = [c2]
            s = stat[:, hd, :]
            a = ve([a], RD(s[:, 0:1], p0[:, hd, :], AX.X, ALU.max))
            c = ve([c, c2], RD(s[:, 1:2], pr[:, hd, :], AX.X, ALU.max))
            a = ts([a, c], s[:, 0:2], s[:, 0:2], -SC, None, ALU.mult)
            e0 = act([a], p0[:, hd, :], p0[:, hd, :], ACT.Exp, bias=s[:, 0:1], scale=SC, accum_out=s[:, 2:3])
            e1 = act([a], pr[:, hd, :], pr[:, hd, :], ACT.Exp, bias=s[:, 1:2], scale=SC, accum_out=s[:, 3:4])
            prt["e", hd] = (e0, e1)

        def weights(hd):
            e0, e1 = prt["e", hd]
            s = stat[:, hd, :]
            r = ve([e0, e1], RC(s[:, 4:6], s[:, 2:4]))
            a = ts([r, e0], p0[:, hd, :], p0[:, hd, :], s[:, 4:5], None, ALU.mult)
            c = ts([r, e1], pr[:, hd, :], pr[:, hd, :], s[:, 5:6], None, ALU.mult)
            prt[hd] = (a, c)

        warm(ACT.Exp)
        for k in range(8):
            feed()
            j, wh, wl, wt = take("vt", k)
            for c in range(2):
                for n in range(2):
                    b = 2 * c + n
                    m = mm3(bank[b][:, :], wh[:, n * 512:n * 512 + 512], wl[:, n * 512:n * 512 + 512],
                            hh[:, k, c * P:c * P + P], hl[:, k, c * P:c * P + P],
                            [wt, ht[k]] + (pfree[b] if k == 0 else []), k == 0, k == 7, True, flip=True)
            finish(m)
            scores(k)
            if k:
                weights(k - 1)
        vv = B[5][:, :, :].rearrange("p a b -> p (a b)").rearrange("p (c n) -> p c n", c=2)
        vtk = []
        for b in (0, 2, 1, 3):
            w = vv[:, b // 2, (b % 2) * 512:(b % 2) * 512 + 512]
            a = act([m], w, bank[b][:, :], ACT.Copy) if b < 2 else cp([m], w, bank[b][:, :])
            pfree[b] = [a]
            vtk.append(a)
        weights(7)

        def turned(hd):
            a, c = prt[hd]
            b = abank()
            pe([a, c, t_cst] + pfree[b], TR(bank[b][:, 0:P], p0[:, hd, :], ident), False)
            pe([], TR(bank[b][:, P:2 * P], pr[:, hd, 0:P], ident), False)
            t = pe([], TR(bank[b][:, 2 * P:3 * P], pr[:, hd, P:2 * P], ident))
            d = act([t, kt[7], prt.get(("m", hd - 4))], pT3[:, hd % 4, :], bank[b][:, 0:3 * P], ACT.Copy)
            pfree[b] = [d]
            prt["d", hd] = d

        otk = [None] * 8

        def apply(hd):
            b2 = abank()
            vh = lambda c: vv[:, c, hd * P:hd * P + P]
            pe([prt["d", hd], *vtk] + pfree[b2], MM(
                bank[b2][:, 0:S], vh(0), pT3[:, hd % 4, 0:S], start=True, stop=False), False)
            m = pe([], MM(bank[b2][:, P:S], vh(1), pT3[:, hd % 4, 2 * P:3 * P], start=False, stop=True))
            prt["m", hd] = m
            a = act([m], hh[:, hd, :], bank[b2][:, 0:S], ACT.Copy)
            otk[hd] = tt([a], hl[:, hd, :], bank[b2][:, 0:S], hh[:, hd, :].bitcast(F), ALU.subtract)
            pfree[b2] = [otk[hd]]

        turned(0)
        turned(1)
        apply(0)
        turned(2)
        apply(1)
        for k in range(8):
            feed()
            toks = kmaj("bout", k, 0, hh[:, k, :], hl[:, k, :], otk[k], k == 0, k == 7,
                        [t for b in range(4) for t in pfree[b]])
            if k < 5:
                turned(k + 3)
            if k < 6:
                apply(k + 2)
        x5 = post(toks, "ln1_g_2", "ln1_b_2", 1)
        ht = x5
        toks = ffn("w131", "w21", False)
        x6 = post(toks, "ln2_g_2", "ln2_b_2", 1, ())
        ofin = h[:, :, :].rearrange("p a b -> p (a b)").rearrange("p (c n) -> p c n", c=2)
        for c in range(2):
            for q in range(2):
                b = 2 * c + q
                for i in range(4):
                    k = 4 * q + i
                    m = pe([x6[k]] + pfree[b], TR(
                        bank[b][:, i * P:i * P + P], xa[:, k, c * P:c * P + P], ident), i == 3)
                a = (act([m], ofin[:, c, q * 512:q * 512 + 512], bank[b][:, :], ACT.Copy) if q else
                     cp([m], ofin[:, c, q * 512:q * 512 + 512], bank[b][:, :]))
                if q == 0:
                    aw = a
            for t in (aw, a):
                queue["sync"].append(lambda g, t=t: g.wait_ge(t[0], t[1]))
            queue["sync"].append(lambda g, c=c: g.dma_start(out[c], ofin[:, c, :]).then_inc(s_out, 16))
        queue["sync"].append(lambda g: g.wait_ge(s_out, 32))
        assert fed[0] == len(PLAN) == sent[0] and len(used) == len(order)

        block = ctx.enter_context(nc.Block())

        @block.sync
        def _(g):
            for f in queue["sync"]:
                f(g)

        @block.gpsimd
        def _(g):
            for f in queue["gpsimd"]:
                f(g)

        @block.scalar
        def _(g):
            for f in queue["scalar"]:
                f(g)

        @block.tensor
        def _(g):
            for f in queue["tensor"]:
                f(g)

        @block.vector
        def _(g):
            for f in queue["vector"]:
                f(g)


ADA = [1, 0, 2, 4, 3, 5]


def _constants():
    i = np.arange(P)
    ident = np.eye(P, dtype=np.float32)
    tri = (i[:, None] <= i[None, :]).astype(np.float32)
    mlow = (i[None, :] <= i[:, None]).astype(np.float32)
    mstrict = (i[None, :] < i[:, None]).astype(np.float32)
    caus = np.where(i[None, :] <= i[:, None], 0.0, NEG).astype(np.float32)
    lev = []
    for n in range(7):
        m = 1 << n
        same = (i[:, None] // (2 * m)) == (i[None, :] // (2 * m))
        lev.append((same & ((i[:, None] // m) % 2 == 1) & ((i[None, :] // m) % 2 == 0)).astype(np.float32))
    freq = np.power(np.float32(500000.0), -np.arange(16, dtype=np.float32) / np.float32(16)).astype(np.float32)
    ang = np.arange(S, dtype=np.float32)[None, :] * freq[:, None]
    cos = np.zeros((P, S), np.float32)
    sin = np.zeros((P, S), np.float32)
    cos[0:16] = cos[16:32] = np.cos(ang)
    sin[0:16] = -np.sin(ang)
    sin[16:32] = np.sin(ang)
    cnt = np.concatenate([1.0 / np.minimum(np.arange(16) + 1, w) for w in (2, 4, 8, 16)]).astype(np.float32)
    parts = {"ident": ident, "tri": tri, "mlow": mlow, "mstrict": mstrict, "caus": caus,
             "lev": np.concatenate(lev, axis=1), "levT1": lev[0].T, "cos": cos, "sin": sin,
             "icnt": np.broadcast_to(cnt, (P, 64)),
             "sel": np.broadcast_to(((np.arange(240) >= 112) & (np.arange(240) < 128)).astype(np.float32), (P, 240))}
    return np.ascontiguousarray(np.concatenate([parts[n] for n, _ in CST], axis=1))


def _cols(a):
    return np.asarray(a).reshape(-1, P).T


def _vectors(x):
    taps = lambda w: np.asarray(w).reshape(w.shape[0], -1, P).transpose(2, 1, 0).reshape(P, -1)
    w_in = np.asarray(x["a_w_in_2"])[0]
    parts = {
        "b_ada": _cols(x["b_ada"][0]), "b_dw_a": _cols(x["b_dw_a"][0]),
        "ln_a_g": _cols(x["ln_a_g"][0]), "ln_a_b": _cols(x["ln_a_b"][0]), "pool_scale": _cols(x["pool_scale"][0]),
        "ln1_g": _cols(x["ln1_g"][0]), "ln1_b": _cols(x["ln1_b"][0]), "b_dw_f": _cols(x["b_dw_f"][0]),
        "w_dw_f": taps(x["w_dw_f"][0]), "w_dw_a": taps(x["w_dw_a"][0]), "ln2_g": _cols(x["ln2_g"][0]),
        "ln2_b": _cols(x["ln2_b"][0]), "a_conv": taps(x["a_conv_2"][0]), "a_norm_g": _cols(x["a_norm_g_2"][0]),
        "ln1_g_2": _cols(x["ln1_g_2"]), "ln1_b_2": _cols(x["ln1_b_2"]), "ln2_g_2": _cols(x["ln2_g_2"]),
        "ln2_b_2": _cols(x["ln2_b_2"]), "a_log": np.broadcast_to(x["a_a_log_2"][0], (P, 8)),
        "dt": np.broadcast_to(x["a_dt_bias_2"][0], (P, 8)),
        "w_ba": w_in[:, 4096:4112].reshape(8, P, 16).transpose(1, 0, 2).reshape(P, 128),
    }
    return np.ascontiguousarray(np.concatenate([parts[n] for n, _ in VEC], axis=1))


def _nmaj(w):
    return w.reshape(8, P, -1, P).transpose(2, 1, 0, 3).reshape(-1, P, 1024)


def _weights(x):
    g = {k: np.asarray(v) for k, v in x.items()}
    ada = g["w_ada"][0].T.reshape(48, P, D)
    units = {
        "ada": [ada[8 * ADA[n // 8] + n % 8] for n in range(48)],
        "in": _nmaj(g["w_in"][0]), "pw": g["w_pw_a"][0].reshape(4, P, 1024),
        "pool": [g["w_pool"][0].transpose(1, 0, 2).reshape(P, 1024)],
        "out": g["w_out"][0].reshape(8, P, 1024), "up": _nmaj(g["w_up"][0]),
        "down": g["w_down"][0].reshape(FF, P, 1024), "gdn": _nmaj(g["a_w_in_2"][0][:, 0:4096]),
        "gout": g["a_w_out_2"][0].reshape(8, P, 1024), "qkv": _nmaj(g["b_w_qkv_2"][0][:, 0:2048]),
        "vt": g["b_w_qkv_2"][0][:, 2048:3072].reshape(8, P, 1024), "bout": g["b_w_out_2"][0].reshape(8, P, 1024),
        "w130": _nmaj(g["f_w13_2"][0]), "w20": g["f_w2_2"][0].reshape(FF, P, 1024),
        "w131": _nmaj(g["f_w13_2"][1]), "w21": g["f_w2_2"][1].reshape(FF, P, 1024),
    }
    return np.stack([units[k][n] for k, n in PLAN])


def kernel(**inputs):
    import concourse.bacc as _bacc
    from concourse.bass_utils import run_bass_kernel_spmd as _run

    nc = _bacc.Bacc("TRN2", target_bir_lowering=False, num_devices=1, dynamic_dma_scratch_size=1024)
    x = np.asarray(inputs["x"])[0]
    arrays = {
        "in_w": _weights(inputs),
        "in_v": _vectors(inputs),
        "in_c": _constants(),
        "in_r": np.ascontiguousarray(np.broadcast_to(np.asarray(inputs["c"])[0], (P, D))),
        "in_x": np.ascontiguousarray(x.T.reshape(8, P, S).transpose(1, 0, 2)),
    }
    aps = {k: nc.dram_tensor(k, a.shape, F, kind="ExternalInput").ap() for k, a in arrays.items()}
    out = nc.dram_tensor("out", (1, S, D), F, kind="ExternalOutput").ap()
    program(nc, aps["in_w"], aps["in_v"], aps["in_c"], aps["in_x"], aps["in_r"], out.rearrange("b (c p) d -> (b c) p d", c=2))
    r = _run(nc, [arrays], core_ids=[0])
    return r.results[0]["out"]
```

```python
from contextlib import ExitStack

import numpy as np

import concourse.bass as bass
from concourse import mybir

F = mybir.dt.float32
FR = mybir.dt.float32r
ALU = mybir.AluOpType
ACT = mybir.ActivationFunctionType
AX = mybir.AxisListType

P = 128
S = 256
D = 1024
NC = D // P
FF = 22
HEADS = 8
ALPHA1 = 2.0 ** 0.25
ALPHA2 = 4.0 ** 0.25
LN_EPS = 1e-5
NORM_EPS = 1e-6
RAW = 11
SPLIT = 5
NEG = -1e30

VEC = [("b_ada", 48), ("b_dw_a", 4), ("ln_a_g", 4), ("ln_a_b", 4), ("pool_scale", 8), ("ln1_g", 8),
       ("ln1_b", 8), ("b_dw_f", 44), ("w_dw_f", 132), ("w_dw_a", 124), ("ln2_g", 8), ("ln2_b", 8),
       ("a_conv", 96), ("a_norm_g", 1), ("ln1_g_2", 16), ("ln1_b_2", 16), ("ln2_g_2", 16), ("ln2_b_2", 16),
       ("a_log", 8), ("dt", 8), ("w_ba", 128)]
VOFF = {}
_n = 0
for _name, _k in VEC:
    VOFF[_name] = _n
    _n += _k
NVEC = _n

CST = [("ident", 128), ("tri", 128), ("mstrict", 128), ("caus0", 128), ("caus", 128), ("lev", 7 * 128),
       ("levT1", 128), ("cos", 256), ("sin", 256), ("icnt", 64), ("sel", 240)]
COFF = {}
_n = 0
for _name, _k in CST:
    COFF[_name] = _n
    _n += _k
NCST = _n

MODS = {"sh1": 0, "sc1": 8, "g1": 16, "sh2": 24, "sc2": 32, "g2": 40}


def stream_plan():
    w = []
    for t in range(4):
        w += [("in", 4 + t), ("in", t)]
    w += [("in", 8 + t) for t in range(4)]
    w += [("in", 12 + t) for t in range(8)] + [("pool", 0)] + [("in", 20 + t) for t in range(8)]
    w += [("pw", k) for k in range(4)] + [("out", k) for k in range(8)]
    ffn = []
    for j in range(FF):
        ffn += [("up", j), ("up", FF + j)]
        if j >= 2:
            ffn += [("down", j - 2)]
    ffn += [("down", FF - 2), ("down", FF - 1)]
    w += ffn
    w += [("gdn", t) for t in range(32)] + [("gout", k) for k in range(8)]

    def swiglu(i):
        out = []
        for j in range(FF):
            out += [(f"w13{i}", j), (f"w13{i}", FF + j)]
            if j >= 2:
                out += [(f"w2{i}", j - 2)]
        return out + [(f"w2{i}", FF - 2), (f"w2{i}", FF - 1)]

    w += swiglu(0)
    w += [("qkv", t) for t in range(16)] + [("vt", k) for k in range(8)] + [("bout", k) for k in range(8)]
    w += swiglu(1)
    plan = [("ada", n) for n in range(16)]
    rest = [("ada", n) for n in range(16, 48)]
    for i, u in enumerate(w):
        plan.append(u)
        if rest and ((i >= 50 and i % 3 == 0) or (i < 42 and i % 3 < 2)):
            plan.append(rest.pop(0))
    return plan


PLAN = stream_plan()


def program(nc, wts, vecs, csts, xT, crep, out):
    with ExitStack() as ctx:
        def sb(name, shape, dt=F):
            return ctx.enter_context(nc.sbuf_tensor(name, shape, dt))

        def sem(name):
            return ctx.enter_context(nc.semaphore(name))

        raw = sb("raw", [P, RAW, 1024])
        hi = sb("hi", [P, SPLIT, 1024], FR)
        lo = sb("lo", [P, SPLIT, 1024], FR)
        vec = sb("vec", [P, NVEC])
        cst = sb("cst", [P, NCST])
        ones = sb("ones", [P, 3, P])
        eps = sb("eps", [P, 2])
        idle = sb("idle", [P, S], FR)
        dummy = sb("dumm", [P, 1])
        mod = sb("mod", [P, 48])
        crow = sb("crow", [P, D])
        xa = sb("xa", [P, NC, S])
        h = sb("h", [P, NC, S])
        hh = sb("hh", [P, NC, S], FR)
        hl = sb("hl", [P, NC, S], FR)
        B = [sb(f"B{i}", [P, NC, S]) for i in range(6)]
        st = sb("st", [P, 2, S])
        ev = sb("ev", [P, 4, S])
        fh = sb("fh", [P, 4, S], FR)
        fl = sb("fl", [P, 4, S], FR)
        Z = sb("Z", [P, 24 * 256])
        ypad = Z[:, 0:4 * 288].rearrange("p (g s) -> p g s", g=4)
        sm = sb("sm", [P, 256])
        bank = [ctx.enter_context(nc.psum_tensor(f"ps{i}", [P, 512], F)) for i in range(8)]

        def V(name, i=0, n=1):
            return vec[:, VOFF[name] + i:VOFF[name] + i + n]

        def C(name, a=0, b=None):
            n = dict(CST)[name]
            return cst[:, COFF[name] + a:COFF[name] + (n if b is None else b)]

        ident = C("ident")

        names = ["sync", "gpsimd", "scalar", "tensor", "vector"]
        done = {e: sem("d_" + e) for e in names[1:]}
        raws = [sem(f"s_raw{i}") for i in range(RAW)]
        s_vec, s_cst, s_x, s_out = sem("s_vec"), sem("s_cst"), sem("s_x"), sem("s_out")
        count = {e: 0 for e in names}
        queue = {e: [] for e in names}
        passed = {e: {} for e in names}

        def put(e, waits, make, sig=True):
            for t in waits:
                if t is None:
                    continue
                s, v = t
                if passed[e].get(id(s), 0) < v:
                    passed[e][id(s)] = v
                    queue[e].append(lambda g, s=s, v=v: g.wait_ge(s, v))
            if sig:
                queue[e].append(lambda g: make(g).then_inc(done[e], 1))
                count[e] += 1
                return (done[e], count[e])
            queue[e].append(lambda g: make(g))
            return None

        def pe(waits, make, sig=True):
            return put("tensor", waits, make, sig)

        def act(waits, o, i, f, sig=True, **kw):
            return put("scalar", waits, lambda g: g.activation(o, i, f, **kw), sig)

        def ve(waits, make):
            return put("vector", waits, make)

        def tt(waits, o, a, b, op, e="vector"):
            return put(e, waits, lambda g: g.tensor_tensor(o, a, b, op))

        def MM(o, l, r, start, stop):
            return lambda g: g.matmul(o, l, r, start=start, stop=stop, skip_group_check=True)

        def TR(o, i, idn):
            return lambda g: g.transpose(o, i, idn)

        def RC(o, i):
            return lambda g: g.reciprocal(o, i)

        def RD(o, i, ax, op):
            return lambda g: g.tensor_reduce(o, i, ax, op)

        def SH(o, i):
            return lambda g: g.stream_shuffle(o, i, [(p + 16) % 32 for p in range(32)])

        def ts(waits, o, a, s1, s2, op0, op1=None, e="vector"):
            if op1 is None:
                return put(e, waits, lambda g: g.tensor_scalar(o, a, s1, None, op0))
            return put(e, waits, lambda g: g.tensor_scalar(o, a, s1, s2, op0, op1))

        def stt(waits, o, a, s, b, op0, op1):
            return put("vector", waits, lambda g: g.scalar_tensor_tensor(out=o, in0=a, scalar=s, in1=b, op0=op0,
                                                                         op1=op1))

        def cp(waits, o, i, e="vector"):
            return put(e, waits, lambda g: g.tensor_copy(o, i))

        sent = [0]
        fed = [0]
        nsplit = [0]
        ready = []
        used = []

        def send(tok):
            i = sent[0]
            if i >= len(PLAN):
                return
            sent[0] += 1
            for t in [tok] if tok else []:
                s, v = t
                if passed["sync"].get(id(s), 0) < v:
                    passed["sync"][id(s)] = v
                    queue["sync"].append(lambda g, s=s, v=v: g.wait_ge(s, v))
            src = wts[i]
            queue["sync"].append(lambda g: g.dma_start(raw[:, i % RAW, :], src).then_inc(raws[i % RAW], 16))

        def landed(i):
            return (raws[i % RAW], 16 * (i // RAW + 1))

        released = {}

        def release(i, tok):
            released[i] = tok
            while sent[0] < len(PLAN) and sent[0] - RAW in released:
                send(released[sent[0] - RAW])

        late = []

        def run_late(force=False):
            while late and (force or late[0][0] + 2 <= len(used)):
                late.pop(0)[1]()

        modtok = {}

        def ada(i, n, r):
            name = ["sh1", "sc1", "g1", "sh2", "sc2", "g2"][MB_ORDER[n // 8]]
            mcol = mod[:, MODS[name] + n % 8:MODS[name] + n % 8 + 1]
            t = put("vector", [landed(i), cstok], lambda g: g.tensor_tensor_reduce(
                r, r, crow[:, :], 1.0, 0.0, ALU.mult, ALU.add, mcol))
            if n % 8 == 7:
                col = MODS[name]
                one = 1.0 if name[:2] == "sc" else 0.0
                modtok[name] = stt([t, t_vec], mod[:, col:col + 8], mod[:, col:col + 8], one, V("b_ada", col, 8),
                                   ALU.add, ALU.add)
            release(i, t)

        def feed_one():
            i = fed[0]
            fed[0] += 1
            while sent[0] <= i:
                late.pop(0)[1]()
            kind, n = PLAN[i]
            r = raw[:, i % RAW, :]
            if kind == "ada":
                late.append((len(used), lambda: ada(i, n, r)))
                return False
            j = nsplit[0]
            nsplit[0] += 1
            free = used[j - SPLIT] if j >= SPLIT else None
            a = act([landed(i), free], hi[:, j % SPLIT, :], r, ACT.Copy)
            b = tt([a, landed(i), free], lo[:, j % SPLIT, :], r, hi[:, j % SPLIT, :].bitcast(F), ALU.subtract)
            ready.append(b)
            release(i, b)
            return True

        MB_ORDER = [1, 0, 2, 4, 3, 5]

        def feed():
            for _ in range(2):
                if nsplit[0] - len(used) >= SPLIT or fed[0] >= len(PLAN):
                    return
                while fed[0] < len(PLAN) and not feed_one():
                    pass

        def spin(n):
            for _ in range(n):
                pe([t_ones] + pfree[7], MM(bank[7][:, 0:S], idle[:, 0:P], idle[:, :], True, True), False)

        bg = []
        pfree = {b: [] for b in range(8)}

        def background(n):
            for _ in range(min(n, len(bg))):
                bg.pop(0)()

        order = [u for u in PLAN if u[0] != "ada"]

        def take(kind, n, ahead=0):
            run_late()
            j = len(used) + ahead
            assert order[j] == (kind, n), (order[j], kind, n)
            while nsplit[0] <= j:
                feed()
            return j, hi[:, j % SPLIT, :], lo[:, j % SPLIT, :], ready[j]

        def finish(tok):
            used.append(tok)

        def mm3(o, wh, wl, xh, xl, waits, first, last, sig, flip=False):
            for n, (a, b) in enumerate(((wh, xh), (wh, xl), (wl, xh))):
                l, r = (b, a) if flip else (a, b)
                t = pe(waits if n == 0 else [], MM(
                    o, l, r, start=(first and n == 0), stop=(last and n == 2)),
                    sig and n == 2)
            return t

        def nmaj(kind, n, o, xh, xl, xt, free):
            j, wh, wl, t = take(kind, n)
            for k in range(8):
                w = [t, xt[k]] + (free if k == 0 else [])
                last = mm3(o, wh[:, k * 128:k * 128 + 128], wl[:, k * 128:k * 128 + 128], xh[:, k, :], xl[:, k, :],
                           w, k == 0, k == 7, k == 7)
            finish(last)
            return last

        def acc(b0, n):
            return bank[(b0 + n // 2) % 8][:, (n % 2) * S:(n % 2) * S + S]

        def kmaj(kind, k, b0, xh, xl, xt, first, last, free):
            j, wh, wl, t = take(kind, k)
            toks = []
            for n in range(8):
                w = [t, xt] + (free if n == 0 else [])
                tok = mm3(acc(b0, n), wh[:, n * 128:n * 128 + 128], wl[:, n * 128:n * 128 + 128], xh, xl, w,
                          first and n % 2 == 0, last, n % 2 == 1)
                toks.append(tok)
            toks = [toks[n | 1] for n in range(8)]
            finish(toks[-1])
            return toks

        s_c = sem("s_c")
        queue["sync"].append(lambda g: g.dma_start(crow[:, :], crep).then_inc(s_c, 16))
        queue["sync"].append(lambda g: g.dma_start(vec[:, :], vecs).then_inc(s_vec, 16))
        queue["sync"].append(lambda g: g.dma_start(xa[:, :, :], xT).then_inc(s_x, 16))
        t_vec, t_x, t_cst = (s_vec, 16), (s_x, 16), (s_cst, 16)
        for i in range(RAW):
            send(None)
        queue["scalar"].append(lambda g: g.dma_start(cst[:, :], csts).then_inc(s_cst, 16))

        put("gpsimd", [], lambda g: g.memset(idle[:, :].bitcast(F), 1.0))
        t_ones = put("gpsimd", [], lambda g: g.memset(ones[:, 0, :], 1.0 / 1024))
        t_ones = put("gpsimd", [], lambda g: g.memset(ones[:, 1, :], 1.0 / 512))
        t_ones = put("gpsimd", [], lambda g: g.memset(ones[:, 2, :], 1.0))
        t_ones = put("gpsimd", [], lambda g: g.memset(eps[:, 0:1], LN_EPS))
        t_ones = put("gpsimd", [], lambda g: g.memset(eps[:, 1:2], NORM_EPS))
        t_ones = put("gpsimd", [], lambda g: g.memset(ypad[:, :, 0:32], 0.0))

        cstok = act([(s_c, 16)], crow[:, :], crow[:, :], ACT.Silu)

        def bc(a, n):
            return a.unsqueeze(1).to_broadcast([P, n, S])

        def stats_rstd(y, ytoks, nch, one, sq, yc, bm, bv, free):
            for k in range(nch):
                m = pe([ytoks[k], t_ones] + free, MM(bank[bm][:, 0:S], ones[:, one, :],
                       y[:, k, :], start=(k == 0), stop=(k == nch - 1)), k == nch - 1)
            if used:
                spin(14)
            ct, qs = [], []
            for k in range(0, nch, 2):
                c = tt([m] + free, yc[:, k:k + 2, :], y[:, k:k + 2, :], bc(bank[bm][:, 0:S], 2), ALU.subtract)
                q = act([c], sq[:, k:k + 2, :], yc[:, k:k + 2, :], ACT.Square)
                ct += [c, c]
                qs.append(q)
            for k in range(0, nch, 2):
                if k in (0, nch - 2):
                    for kk in (k, k + 1):
                        v = pe([qs[k // 2]], MM(bank[bv][:, 0:S], ones[:, one, :], sq[:, kk, :], start=(kk == 0),
                                                stop=(kk == nch - 1)), kk == nch - 1)
                else:
                    q = tt([qs[k // 2]], sq[:, k, :], sq[:, k, :], sq[:, k + 1, :], ALU.add)
                    v = pe([q], MM(bank[bv][:, 0:S], ones[:, one, :], sq[:, k, :], start=False, stop=False), False)
            if used:
                feed()
            if used:
                spin(38)
            s = act([v], st[:, 0, :], bank[bv][:, 0:S], ACT.Sqrt, bias=eps[:, 0:1])
            r = ve([s], RC(st[:, 1, :], st[:, 0, :]))
            return ct, r, m, v

        def apply_norm(ct, r, nch, yc, gain, bias, o, gtoks=(), oh=None, ol=None, free=()):
            toks = []
            held = []

            def low(kk, v, b):
                toks.append(tt([v, b, *free], ol[:, kk, :], o[:, kk, :], oh[:, kk, :].bitcast(F), ALU.subtract))

            for k in range(0, nch, 2):
                a = tt([r, ct[k]], yc[:, k:k + 2, :], yc[:, k:k + 2, :], bc(st[:, 1, :], 2), ALU.mult)
                late_lows, held = held, []
                for kk in (k, k + 1):
                    if oh is not None:
                        b = act([a, *gtoks, *free], oh[:, kk, :], yc[:, kk, :], ACT.Identity, scale=gain(kk),
                                bias=bias(kk))
                    if late_lows:
                        low(*late_lows.pop(0))
                    if oh is None and kk % 2:
                        v = act([a, *gtoks], o[:, kk, :], yc[:, kk, :], ACT.Identity, scale=gain(kk), bias=bias(kk))
                    else:
                        v = ts([a, *gtoks], o[:, kk, :], yc[:, kk, :], gain(kk), bias(kk), ALU.mult, ALU.add)
                    if oh is not None:
                        held.append((kk, v, b))
                    else:
                        toks.append(v)
            for x in held:
                low(*x)
            return toks

        def norm(y, ytoks, nch, one, sq, yc, bm, bv, free, gain, bias, o, gtoks=(), oh=None, ol=None):
            ct, r, m, v = stats_rstd(y, ytoks, nch, one, sq, yc, bm, bv, free)
            return apply_norm(ct, r, nch, yc, gain, bias, o, gtoks, oh, ol)

        def warm(f):
            act([t_ones], dummy[:, 0:1], ones[:, 2, 0:1], f)

        def split(src, toks, oh, ol, n=NC, free=()):
            out = []
            for k in range(n):
                a = act([toks[k], *free], oh[:, k, :], src[:, k, :], ACT.Copy)
                out.append(tt([a], ol[:, k, :], src[:, k, :], oh[:, k, :].bitcast(F), ALU.subtract))
            return out

        def modcol(name):
            return lambda k: mod[:, MODS[name] + k:MODS[name] + k + 1]

        for _ in range(8):
            feed_one()
        run_late(True)
        ct, r0, _, _ = stats_rstd(xa, [t_x] * 8, 8, 0, B[0], B[1], 0, 1, [])
        for _ in range(8):
            feed_one()
        run_late(True)
        feed()
        ht = apply_norm(ct, r0, 8, B[1], modcol("sc1"), modcol("sh1"), h, [modtok["sc1"], modtok["sh1"]], hh, hl)
        xs = B[2]

        def scale_x(k, toks):
            return act([toks[k]], xs[:, k, :], xa[:, k, :], ACT.Copy, scale=ALPHA1)

        nb = [0]

        early = {}

        def start_tiles(units, banks):
            jobs = []
            for i, (kind, n) in enumerate(units):
                feed()
                b = banks[nb[0] % len(banks)]
                nb[0] += 1
                jobs.append((kind, n, b, take(kind, n, i)))
            for k in range(8):
                for kind, n, b, (j, wh, wl, t) in jobs:
                    w = [t, ht[k]] + (pfree[b] if k == 0 else [])
                    early[kind, n] = (b, mm3(bank[b][:, 0:S], wh[:, k * 128:k * 128 + 128], wl[:, k * 128:k * 128 + 128],
                                             hh[:, k, :], hl[:, k, :], w, k == 0, k == 7, k == 7))
            for kind, n, b, _ in jobs:
                finish(early[kind, n][1])

        def tile_out(kind, n, banks, x=None):
            if (kind, n) in early:
                feed()
                return early.pop((kind, n))
            b = banks[nb[0] % len(banks)]
            nb[0] += 1
            feed()
            t = nmaj(kind, n, bank[b][:, 0:S], hh, hl, ht, pfree[b])
            return b, t

        R4 = [2, 3, 4, 5]
        start_tiles([("in", 4), ("in", 0)], R4)
        ya = ypad
        yt = []
        pad = t_ones
        for t in range(4):
            b, m = tile_out("in", 4 + t, R4)
            a = act([m], ev[:, t, :], bank[b][:, 0:S], ACT.Sigmoid)
            pfree[b] = [a]
            b, m = tile_out("in", t, R4)
            v = tt([m, a, pad], ya[:, t, 32:32 + S], bank[b][:, 0:S], ev[:, t, :], ALU.mult)
            pfree[b] = [v]
            yt.append(v)

        cv = B[0]
        cvt = [None] * 4

        def conv_tap(i):
            for t in range(4):
                w = V("w_dw_a", t * 31 + i)
                src = ya[:, t, 2 + i:2 + i + S]
                if i == 0:
                    cvt[t] = ts([yt[t], t_vec, pad], cv[:, t, :], src, w, V("b_dw_a", t), ALU.mult, ALU.add)
                else:
                    cvt[t] = stt([cvt[t]], cv[:, t, :], src, w, cv[:, t, :], ALU.mult, ALU.add)

        ndg = [0]
        dused = []

        dtok = {}

        def conv_build(i):
            for t in range(4):
                d = cv[:, 4 + (ndg[0] % 8) // 2, (ndg[0] % 2) * P:(ndg[0] % 2) * P + P]
                fr = [dused[ndg[0] - 8]] if ndg[0] >= 8 else [yt[3], t_cst, t_vec]
                ndg[0] += 1
                dtok[i, t] = d, act(fr, d, ident, ACT.Copy, scale=V("w_dw_a", t * 31 + i))

        def conv_diag(i):
            if i < 30:
                conv_build(i + 1)
            for t in range(4):
                d, a = dtok[i, t]
                dused.append(pe([a, yt[t]], MM(acc(0, t), d, ya[:, t, 2 + i:2 + i + S], i == 16 and t % 2 == 0,
                                               i == 30)))

        def conv_sum():
            for b in range(2):
                a = tt([dused[-1], *cvt], cv[:, 2 * b:2 * b + 2, :], cv[:, 2 * b:2 * b + 2, :],
                       bank[b][:, :].rearrange("p (a b) -> p a b", a=2), ALU.add)
            cvt[:] = [a] * 4

        for i in range(16):
            bg.append(lambda i=i: conv_tap(i))
            if i == 0:
                bg.append(lambda: conv_build(16))
            else:
                bg.append(lambda i=i: conv_diag(15 + i))
        bg.append(conv_sum)

        pu = B[1][:, :, :].rearrange("p c s -> p (c s)")
        up = pu[:, 0:4 * 272].rearrange("p (g s) -> p g s", g=4)
        pz = put("gpsimd", [ht[7]], lambda g: g.memset(up[:, :, 0:16], 0.0))
        ut = []
        for t in range(4):
            b, m = tile_out("in", 8 + t, R4)
            a = act([m, ht[7]], up[:, t, 16:272], bank[b][:, 0:S], ACT.Copy)
            pfree[b] = [a]
            ut.append(a)
            background(2)
        pa, pb_ = B[2], B[3]
        ws = [pa[:, 0:5, :].rearrange("p c s -> p (c s)")[:, 0:1088].rearrange("p (g s) -> p g s", g=4),
              pb_[:, 0:5, :].rearrange("p c s -> p (c s)")[:, 0:1088].rearrange("p (g s) -> p g s", g=4)]
        lv = []
        pst = []
        pooled = h
        ph, plo = fh, fl

        def window(lev):
            src, tk = lv[-1] if lv else (up, ut[3])
            sh = 1 << lev
            dst = ws[lev % 2]
            t1 = tt([tk, pz, ut[3]], dst[:, lev:4, sh:272], src[:, lev:4, sh:272], src[:, lev:4, 0:272 - sh], ALU.add)
            lv.append((dst, cp([tk, t1], dst[:, lev:4, 0:sh], src[:, lev:4, 0:sh])))

        gtok = []

        def pool_group(g):
            if g:
                p = act(gtok[g - 1], ph[:, g - 1, :], pooled[:, g - 1, :], ACT.Copy)
            if g < 4:
                pool_mean(g)
            if g:
                pst.append(tt([p], plo[:, g - 1, :], pooled[:, g - 1, :], ph[:, g - 1, :].bitcast(F), ALU.subtract))

        def pool_mean(g):
            sgrp = lv[g][0][:, g, 16:272]
            a = tt([lv[3][1], t_cst], pooled[:, g, 0:16], sgrp[:, 0:16], C("icnt", g * 16, g * 16 + 16), ALU.mult)
            b = stt([lv[3][1]], pooled[:, g, 16:S], sgrp[:, 16:S], 0.5 ** (g + 1), up[:, g, 32:272], ALU.mult, ALU.subtract)
            a = tt([a], pooled[:, g, 0:16], pooled[:, g, 0:16], up[:, g, 16:32], ALU.subtract)
            gtok.append([a, b])

        for i in range(8):
            bg.insert(2 * i, (lambda i=i: window(i)) if i < 4 else (lambda i=i: pool_group(i - 4)))
        bg.insert(15, lambda: pool_group(4))
        ga = B[4]
        gat = []
        for n in range(8):
            b, m = tile_out("in", 12 + n, R4)
            a = act([m, ht[7]], ga[:, n, :], bank[b][:, 0:S], ACT.Sigmoid)
            pfree[b] = [a]
            gat.append(a)
            background(2)
        feed()
        assert len(pst) == 4
        j, wh, wl, wt = take("pool", 0)
        ybt = []
        yb = B[5]
        for n in range(8):
            b = R4[nb[0] % 4]
            nb[0] += 1
            m = mm3(bank[b][:, 0:S], wh[:, n * 128:n * 128 + 128], wl[:, n * 128:n * 128 + 128], ph[:, n // 2, :],
                    plo[:, n // 2, :], [wt, pst[n // 2], *pfree[b]], True, True, True)
            a = act([m, t_vec], yb[:, n, :], bank[b][:, 0:S], ACT.Copy, scale=V("pool_scale", n))
            pfree[b] = [a]
            ybt.append(a)
        finish(m)
        mg = B[1]
        for n in range(8):
            b, m = tile_out("in", 20 + n, R4)
            a = act([m, yt[n] if n < 4 else ybt[n - 4]], ev[:, n % 4, :], bank[b][:, 0:S], ACT.Sigmoid)
            pfree[b] = [a]
            ybt[n] = tt([a, ybt[n]], yb[:, n, :], yb[:, n, :], ev[:, n % 4, :], ALU.mult)
            background(2)
        background(99)
        yn = B[2]
        warm(ACT.Sqrt)
        at = norm(cv, cvt, 4, 1, B[3], yn, 0, 1, [pst[3], lv[3][1]], lambda k: V("ln_a_g", k), lambda k: V("ln_a_b", k), yn)
        yh, yl = hh[:, 4:8, :], hl[:, 4:8, :]
        gates_done = used[-1]
        s4 = []
        for k in range(4):
            a = act([at[k]], cv[:, k, :], yn[:, k, :], ACT.Silu)
            b = cp([a, gates_done], yh[:, k, :], cv[:, k, :])
            s4.append(tt([b], yl[:, k, :], cv[:, k, :], yh[:, k, :].bitcast(F), ALU.subtract))
        for k in range(4):
            feed()
            toks = kmaj("pw", k, 2, yh[:, k, :], yl[:, k, :], s4[k], k == 0, k == 3,
                        [t for b in R4 for t in pfree[b]])
        mt = []
        for n in range(8):
            a = tt([toks[n], gat[n]], mg[:, n, :], acc(2, n), ga[:, n, :], ALU.mult)
            pfree[2 + n // 2] = [a]
            a = tt([a, ybt[n]], mg[:, n, :], mg[:, n, :], yb[:, n, :], ALU.add)
            a = act([a], hh[:, n, :], mg[:, n, :], ACT.Copy)
            if n:
                mt.append(tt([a0], hl[:, n - 1, :], mg[:, n - 1, :], hh[:, n - 1, :].bitcast(F), ALU.subtract))
            a0 = a
        mt.append(tt([a0], hl[:, 7, :], mg[:, 7, :], hh[:, 7, :].bitcast(F), ALU.subtract))
        xst = [scale_x(k, [t_x] * 8) for k in range(8)]
        for k in range(8):
            if k < 7:
                feed()
            toks = kmaj("out", k, 6, hh[:, k, :], hl[:, k, :], mt[k], k == 0, k == 7,
                        [t for b in (6, 7, 0, 1) for t in pfree[b]])

        def residual(toks, b0, gate, gtok, alpha):
            out = []
            warm(ACT.Sqrt)
            if gate is None:
                for n in range(0, 8, 2):
                    v = xa[:, n:n + 2, :]
                    a = bank[b0 + n // 2][:, :].rearrange("p (a b) -> p a b", a=2)
                    t = stt([toks[n]], v, v, alpha, a, ALU.mult, ALU.add)
                    out += [t, t]
                    pfree[b0 + n // 2] = [t]
                return out
            for n in range(8):
                t = stt([toks[n], gtok, xst[n]], xa[:, n, :], acc(b0, n), gate(n), xs[:, n, :], ALU.mult, ALU.add)
                out.append(t)
                pfree[(b0 + n // 2) % 8] = [t]
            return out

        rt = residual(toks, 6, modcol("g1"), modtok["g1"], ALPHA1)
        x1 = norm(xa, rt, 8, 0, B[0], B[1], 4, 5, pfree[4] + pfree[5], lambda k: V("ln1_g", k), lambda k: V("ln1_b", k),
                  xa)
        ht = norm(xa, x1, 8, 0, B[0], B[1], 4, 5, [], modcol("sc2"), modcol("sh2"), h,
                  [modtok["sc2"], modtok["sh2"]], hh, hl)
        pfree[4], pfree[5] = [ht[0]], [ht[0]]
        xst = [None] * 8

        def scaled(k):
            xst[k] = scale_x(k, x1)

        for k in range(8):
            bg.append(lambda k=k: scaled(k))

        R3 = [4, 5, 6, 7]

        def ffn(kup, kdown, conv):
            ftoks = []
            ffree = []

            def down(j):
                if j < FF - 1:
                    feed()
                fr = [t for b in range(4) for t in pfree[b]] if j == 0 else []
                ts_ = kmaj(kdown, j, 0, fh[:, j % 4, :], fl[:, j % 4, :], ftoks[j], j == 0, j == FF - 1, fr)
                ffree.append(ts_[-1])
                return ts_

            evf = [None] * 4
            start_tiles([(kup, 0), (kup, FF), (kup, 1)], R3)
            for j in range(FF):
                got = []
                for half in (0, 1):
                    n = j + half * FF
                    b, m = tile_out(kup, n, R3)
                    slot = (2 * j + half) % 4
                    e = ev[:, slot, :]
                    p0 = bank[b][:, 0:S]
                    if conv:
                        a = act([m, evf[slot], t_vec], e, p0, ACT.Identity, scale=V("w_dw_f", n * 3 + 2),
                                bias=V("b_dw_f", n))
                        a = stt([a, m], e[:, 1:], p0[:, 0:S - 1], V("w_dw_f", n * 3 + 1), e[:, 1:], ALU.mult, ALU.add)
                        a = stt([a], e[:, 2:], p0[:, 0:S - 2], V("w_dw_f", n * 3), e[:, 2:], ALU.mult, ALU.add)
                        pfree[b] = [a]
                        if half == 1:
                            a = act([a], e, e, ACT.Gelu_apprx_tanh)
                    else:
                        a = act([m, evf[slot]], e, p0, ACT.Silu if half == 0 else ACT.Copy)
                        pfree[b] = [a]
                    got.append(a)
                s0, s1 = (2 * j) % 4, (2 * j + 1) % 4
                f = tt(got, ev[:, s0, :], ev[:, s0, :], ev[:, s1, :], ALU.mult)
                fr = [ffree[j - 4]] if j >= 4 else []
                a = act([f] + fr, fh[:, j % 4, :], ev[:, s0, :], ACT.Copy)
                z = tt([a], fl[:, j % 4, :], ev[:, s0, :], fh[:, j % 4, :].bitcast(F), ALU.subtract)
                evf[s0] = z
                evf[s1] = f
                ftoks.append(z)
                if j >= 2:
                    down(j - 2)
                background(1)
            down(FF - 2)
            return down(FF - 1)

        evlast = [None]
        toks = ffn("up", "down", True)
        rt = residual(toks, 0, modcol("g2"), modtok["g2"], ALPHA1)
        x2 = norm(xa, rt, 8, 0, B[0], B[1], 4, 5, pfree[4] + pfree[5], lambda k: V("ln2_g", k), lambda k: V("ln2_b", k), xa, (), hh, hl)
        ht = x2

        qb, kb, vb, zb = B[2], B[3], B[4], B[5]
        R2 = [4, 5, 7]
        pfree[4], pfree[5] = [x2[0]], [x2[0]]

        def ba():
            for c in range(2):
                for k in range(8):
                    t = pe([x2[k], t_vec] + pfree[6], MM(
                        bank[6][:, c * 16:c * 16 + 16], xa[:, k, c * 128:c * 128 + 128], V("w_ba", k * 16, 16),
                        start=(c == 0 and k == 0), stop=(k == 7)), k == 7)
            return t

        pba = bank[6][:, 0:32].rearrange("p (c n) -> p c n", c=2)

        def smv(o, n=2):
            return sm[:, o:o + 8 * n].rearrange("p (c n) -> p c n", c=n)

        beta = smv(0)
        gg = smv(16)
        ex = smv(96)
        ax = smv(112)
        rl = smv(128)
        soon = []

        def conv4(n, dst, b, m, toks):
            p0 = bank[b][:, 0:S]
            w = lambda i: V("a_conv", n * 4 + i)
            a = act([m, t_vec], dst, p0, ACT.Copy, scale=w(3))
            for i in (2, 1, 0):
                d = 3 - i
                a = stt([a, m], dst[:, d:], p0[:, 0:S - d], w(i), dst[:, d:], ALU.mult, ALU.add)
            pfree[b] = [a]
            soon.append(lambda: toks.append(act([a], dst, dst, ACT.Silu)))
            if len(soon) > 1:
                soon.pop(0)()

        def settle():
            while soon:
                soon.pop(0)()

        norms = {}

        def head_norms(dst, sqs, sqb, scale, bsum, bb, key, ready_of, apply):
            def squares(i):
                q = act(ready_of(2 * i) + ready_of(2 * i + 1) + sqs(i), sqb[:, 2 * i:2 * i + 2, :],
                        dst[:, 2 * i:2 * i + 2, :], ACT.Square)
                norms[key, "sq", i] = q

            def sums(i):
                for n in (2 * i, 2 * i + 1):
                    m = pe([norms[key, "sq", i], t_cst] + pfree[bsum], MM(
                        bank[bsum][:, 0:S], C("sel", 112 - 16 * n, 240 - 16 * n), sqb[:, n, :], start=(n == 0),
                        stop=(n == 7)), n % 2 == 1)
                norms[key, "m"] = m

            def root():
                a = act([norms[key, "m"], norms.get("st")], st[:, 0, :], bank[bsum][:, 0:S], ACT.Sqrt,
                        bias=eps[:, 1:2], scale=scale)
                pfree[bsum] = [a]
                norms["st"] = norms[key, "r"] = ve([a, norms.get("rd")], RC(st[:, 1, :], st[:, 0, :]))

            def spread(i):
                for n in (2 * i, 2 * i + 1):
                    m = pe([norms[key, "r"]] + pfree[bb[i % 2]], MM(
                        bank[bb[i % 2]][:, (n % 2) * S:(n % 2) * S + S], ident[:, 16 * n:16 * n + 1].to_broadcast([P, P]),
                        st[:, 1, :], start=(n % 2 == 0), stop=True))
                norms["rd"] = m
                pfree[bb[i % 2]] = [apply(i, m, bank[bb[i % 2]][:, :].rearrange("p (a b) -> p a b", a=2))]

            return ([lambda i=i: squares(i) for i in range(4)], [lambda i=i: sums(i) for i in range(4)], root,
                    [lambda i=i: spread(i) for i in range(4)])

        def l2(dst, toks, scale, sqb, banks, busy, key):
            def apply(i, m, v):
                d = dst[:, 2 * i:2 * i + 2, :]
                toks[2 * i] = toks[2 * i + 1] = stt([m], d, d, scale, v, ALU.mult, ALU.mult)
                return toks[2 * i]

            sq, sm_, root, spread = head_norms(dst, lambda i: busy(), sqb, 1.0, banks[0], banks[1:], key,
                                               lambda n: [toks[n]], apply)
            return sq[0:2] + [sm_[0], sq[2], sm_[1], sq[3], sm_[2], lambda: (sm_[3](), root())] + spread

        qt, kt = [], []
        RQ = [4, 5, 7, 0, 1, 2, 3]
        start_tiles([("gdn", 0), ("gdn", 1), ("gdn", 2)], RQ)
        for n in range(8):
            b, m = tile_out("gdn", n, RQ)
            conv4(n, qb[:, n, :], b, m, qt)
            if n == 3:
                bat = ba()
            if n == 5:
                bt = act([bat], beta, pba[:, :, 0:8], ACT.Sigmoid)
                at0 = tt([bat, bt, t_vec], ax, pba[:, :, 8:16], V("dt", 0, 8).unsqueeze(1).to_broadcast([P, 2, 8]), ALU.add)
                pfree[6] = [bt, at0]
                a1 = ts([at0], rl, ax, 0.0, None, ALU.max)
                a2 = stt([a1], ex, rl, -2.0, ax, ALU.mult, ALU.add)
                a3 = act([a2], ex, ex, ACT.Exp)
                a3b = act([t_vec], sm[:, 80:88], V("a_log", 0, 8), ACT.Exp)
                a4 = act([a3], ex, ex, ACT.Ln, bias=1.0)
                a5 = tt([a4], ex, ex, rl, ALU.add)
                gt = stt([a5, a3b], gg, ex, -1.0, sm[:, 80:88].unsqueeze(1).to_broadcast([P, 2, 8]), ALU.mult, ALU.mult)
        gr = Z[:, 0:2048].rearrange("p (c n s) -> p c n s", c=2, n=8)
        dmat = gr
        gcol = smv(32)
        egc = smv(144)
        nbeg = smv(48)
        kdec = smv(160)
        G = {}

        def gates():
            for c in range(2):
                m = pe([gt, t_cst] + pfree[6], MM(
                    bank[6][:, c * 8:c * 8 + 8], C("tri"), gg[:, c, :], start=(c == 0), stop=True))
            G["gc"] = cp([m], gcol, bank[6][:, 0:16].rearrange("p (c n) -> p c n", c=2))
            pfree[6] = [G["gc"]]

        qdec = Z[:, 2048:3072].rearrange("p (n s) -> p n s", n=8)

        def rows(c, q):
            bk = [3, 6][q]
            for i in range(4):
                hd = 4 * q + i
                m = pe([gt, t_cst] + pfree[bk], MM(
                    bank[bk][:, i * P:i * P + P], gg[:, c, hd:hd + 1].to_broadcast([P, P]), C("tri"),
                    start=(i == 0), stop=True), i == 3)
            for i in range(4):
                hd = 4 * q + i
                a = act([m, G["gc"]], gr[:, c, hd, :], bank[bk][:, i * P:i * P + P], ACT.Identity, scale=-1.0,
                        bias=gcol[:, c, hd:hd + 1])
            if c == 0:
                a = act([a], kdec[:, 0, 4 * q:4 * q + 4], gr[:, c, 4 * q:4 * q + 4, P - 1], ACT.Copy, scale=-1.0)
            else:
                qv = qdec[:, 4 * q:4 * q + 4, :].rearrange("p a b -> p (a b)")
                a = act([m], qv, bank[bk][:, :], ACT.Copy)
            pfree[bk] = [a]
            v = gr[:, c, 4 * q:4 * q + 4, :]
            G["x", c, q] = tt([a, t_cst], v, v, C("caus").unsqueeze(1).to_broadcast([P, 4, P]), ALU.min)

        def decays():
            feed()
            a = act([G["gc"]], egc, gcol, ACT.Exp)
            G["nbeg"] = stt([a, bt], nbeg, egc, -1.0, beta, ALU.mult, ALU.mult)
            G["kdec"] = act([G["x", 0, 1]], kdec[:, 0, :], kdec[:, 0, :], ACT.Exp)
            for c in range(2):
                for q in range(2):
                    v = gr[:, c, 4 * q:4 * q + 4, :]
                    G["D", c, q] = act([G["x", c, q]], v, v, ACT.Exp)
            for q in range(2):
                v = qdec[:, 4 * q:4 * q + 4, :]
                e = act([G["x", 1, q]], v, v, ACT.Exp)
                G["qd", q] = tt([e, qt[4 * q + 3]], v, v, qb[:, 4 * q:4 * q + 4, P:2 * P], ALU.mult)

        lq = l2(qb, qt, 128.0 ** -0.5, B[0], [0, 1, 2], lambda: [], "q")
        rw = [lambda c=c, q=q: rows(c, q) for c in range(2) for q in range(2)]
        bg.extend([settle, lq[0], gates, lq[1], rw[0], lq[2], lq[3], rw[1], lq[4], lq[5], rw[2], lq[6], rw[3]] + lq[7:])
        for n in range(8):
            b, m = tile_out("gdn", 8 + n, R2)
            conv4(8 + n, kb[:, n, :], b, m, kt)
            background(2)

        bg.append(decays)
        bg.extend(l2(kb, kt, 1.0, B[0], [3, 1, 2], lambda: [norms["q", "m"]], "k"))

        bg.insert(0, settle)
        lt = Z[:, 3072:5120].rearrange("p (g i s) -> p g i s", g=4, i=4)
        tm = B[0][:, :, :].rearrange("p a b -> p (a b)").rearrange("p (g i s) -> p g i s", g=4, i=4)
        tT = B[1][:, :, :].rearrange("p a b -> p (a b)").rearrange("p (g i s) -> p g i s", g=4, i=4)
        aT = Z[:, 0:2048].rearrange("p (g i s) -> p g i s", g=4, i=4)
        pm = ev[:, :, :].rearrange("p a b -> p (a b)").rearrange("p (g i s) -> p g i s", g=2, i=4)
        T = {}
        npm = [0]
        BK = [0, 1, 2, 3, 6]
        nbk = [0]

        def nextbank():
            b = BK[nbk[0] % 5]
            nbk[0] += 1
            return b

        def ga_(c, q):
            g_ = 2 * c + q
            b1 = nextbank()
            sl = slice(c * P, c * P + P)
            for i in range(4):
                hd = 4 * q + i
                m = pe([kt[hd]] + pfree[b1], MM(
                    bank[b1][:, i * P:i * P + P], kb[:, hd, sl], kb[:, hd, sl], start=(i == 0), stop=True), i == 3)
            b2 = nextbank()
            for i in range(4):
                hd = 4 * q + i
                m2 = pe([kt[hd], qt[hd]] + pfree[b2], MM(
                    bank[b2][:, i * P:i * P + P], qb[:, hd, sl], kb[:, hd, sl], start=(i == 0), stop=True), i == 3)
            x = pm[:, npm[0] % 2]
            w = T.get(("pm", npm[0] % 2))
            for i in range(4):
                hd = 4 * q + i
                a = stt([m, G["D", c, q], bt, w], x[:, i, :], bank[b1][:, i * P:i * P + P],
                        beta[:, c, hd:hd + 1], gr[:, c, hd, :], ALU.mult, ALU.mult)
            pfree[b1] = [a]
            a = tt([a], x, x, C("mstrict").unsqueeze(1).to_broadcast([P, 4, P]), ALU.mult)
            y = tm[:, g_]
            a2 = tt([a, m2], aT[:, g_], bank[b2][:, :].rearrange("p (i s) -> p i s", i=4), gr[:, c, 4 * q:4 * q + 4, :],
                    ALU.mult)
            pfree[b2] = [a2]
            b3 = nextbank()
            for i in range(4):
                m3 = pe([a, t_cst] + pfree[b3], TR(bank[b3][:, i * P:i * P + P], x[:, i, :], ident),
                        i == 3)
            l = act([m3], lt[:, g_], bank[b3][:, :].rearrange("p (i s) -> p i s", i=4), ACT.Copy)
            pfree[b3] = [l]
            b4 = nextbank()
            for i in range(4):
                m4 = pe([a2, t_cst] + pfree[b4], TR(bank[b4][:, i * P:i * P + P], aT[:, g_, i, :],
                                                                           ident), i == 3)
            T["aT", g_] = act([m4], aT[:, g_], bank[b4][:, :].rearrange("p (i s) -> p i s", i=4), ACT.Copy)
            pfree[b4] = [T["aT", g_]]
            idb = ident.unsqueeze(1).to_broadcast([P, 4, P])
            a = tt([a], tm[:, g_], x, C("lev", 0, P).unsqueeze(1).to_broadcast([P, 4, P]), ALU.mult)
            T["T", g_] = tt([a], tm[:, g_], idb, tm[:, g_], ALU.subtract)
            a = tt([l], tT[:, g_], lt[:, g_], C("levT1").unsqueeze(1).to_broadcast([P, 4, P]), ALU.mult)
            T["TT", g_] = tt([a], tT[:, g_], idb, tT[:, g_], ALU.subtract)
            T["L", g_] = l
            T["pm", npm[0] % 2] = T["TT", g_]
            npm[0] += 1 if g_ < 2 else 2

        def level_p(lv_, g_):
            b1 = nextbank()
            for i in range(4):
                m = pe([T["L", g_], T["T", g_]] + pfree[b1], MM(bank[b1][:, i * P:i * P + P], lt[:, g_, i, :],
                                                               tm[:, g_, i, :], start=(i == 0), stop=True), i == 3)
            key = T["slot", g_] = ("pm", npm[0] % 2)
            npm[0] += 1
            a = tt([m, T.get(key), t_cst], pm[:, key[1]], bank[b1][:, :].rearrange("p (i s) -> p i s", i=4),
                   C("lev", lv_ * P, lv_ * P + P).unsqueeze(1).to_broadcast([P, 4, P]), ALU.mult)
            pfree[b1] = [a]
            T["P", g_] = a

        def level_t(lv_, g_):
            a, key = T["P", g_], T["slot", g_]
            x = pm[:, key[1]]
            b3 = nextbank()
            for i in range(4):
                m3 = pe([a, T["TT", g_]] + pfree[b3], MM(bank[b3][:, i * P:i * P + P], x[:, i, :], tT[:, g_, i, :],
                                                        start=(i == 0), stop=True), i == 3)
            m2 = m3
            if lv_ < 6:
                b2 = nextbank()
                for i in range(4):
                    m2 = pe([a, T["TT", g_]] + pfree[b2], MM(bank[b2][:, i * P:i * P + P], tT[:, g_, i, :], x[:, i, :],
                                                            start=(i == 0), stop=True), i == 3)
                T["T", g_] = tt([m2], tm[:, g_], tm[:, g_], bank[b2][:, :].rearrange("p (i s) -> p i s", i=4),
                                ALU.subtract)
                pfree[b2] = [T["T", g_]]
            T[key] = m2
            T["TT", g_] = tt([m3, m2], tT[:, g_], tT[:, g_], bank[b3][:, :].rearrange("p (i s) -> p i s", i=4),
                             ALU.subtract)
            pfree[b3] = [T["TT", g_]]

        rv = h[:, :, :].rearrange("p a b -> p (a b)").rearrange("p (g i s) -> p g i s", g=4, i=4)
        kd = Z[:, 5120:6144].rearrange("p (g i s) -> p g i s", g=2, i=4)
        vt = []

        def tokmaj_v(c, q):
            b1 = nextbank()
            for i in range(4):
                m = pe([vt[4 * q + i], t_cst] + pfree[b1], TR(
                    bank[b1][:, i * P:i * P + P], vb[:, 4 * q + i, c * P:c * P + P], ident), i == 3)
            for i in range(4):
                hd = 4 * q + i
                a = act([m, bt], rv[:, 2 * c + q, i, :], bank[b1][:, i * P:i * P + P], ACT.Copy,
                        scale=beta[:, c, hd:hd + 1])
            pfree[b1] = [a]
            T["rv", 2 * c + q] = a

        def tokmaj_k(q):
            b1 = nextbank()
            for i in range(4):
                m = pe([kt[4 * q + i], t_cst] + pfree[b1], TR(
                    bank[b1][:, i * P:i * P + P], kb[:, 4 * q + i, 0:P], ident), i == 3)
            for i in range(4):
                hd = 4 * q + i
                a = act([m, G["kdec"]], kd[:, q, i, :], bank[b1][:, i * P:i * P + P], ACT.Copy,
                        scale=kdec[:, 0, hd:hd + 1])
            pfree[b1] = [a]
            T["kd", q] = a

        for n in range(8):
            b, m = tile_out("gdn", 16 + n, R2)
            conv4(16 + n, vb[:, n, :], b, m, vt)
            background(3)
        background(99)
        settle()
        for q in range(2):
            bg.append(lambda q=q: ga_(0, q))
            bg.append(lambda q=q: tokmaj_k(q))
        vn = vb[:, :, :].rearrange("p a b -> p (a b)").rearrange("p (g i s) -> p g i s", g=4, i=4)
        ss = lt

        def solve(g_):
            b1 = nextbank()
            for i in range(4):
                m = pe([T["TT", g_], T["rv", g_], T.get(("r1", g_ - 2))] + pfree[b1], MM(
                    bank[b1][:, i * P:i * P + P], tT[:, g_, i, :], rv[:, g_, i, :], start=(i == 0), stop=True), i == 3)
            a = cp([m, T["rv", 3]], vn[:, g_], bank[b1][:, :].rearrange("p (i s) -> p i s", i=4))
            pfree[b1] = [a]
            T["vn", g_] = a

        def state(q):
            b2 = nextbank()
            for i in range(4):
                m = pe([T["kd", q], T["vn", q]] + pfree[b2], MM(
                    bank[b2][:, i * P:i * P + P], kd[:, q, i, :], vn[:, q, i, :], start=(i == 0), stop=True), i == 3)
            T["S", q] = act([m, T["TT", 0], T["TT", 1]], ss[:, q], bank[b2][:, :].rearrange("p (i s) -> p i s", i=4),
                            ACT.Copy)
            pfree[b2] = [T["S", q]]

        def carry(q):
            b3 = nextbank()
            for i in range(4):
                m = pe([T["S", q], kt[7]] + pfree[b3], MM(
                    bank[b3][:, i * P:i * P + P], kb[:, 4 * q + i, P:2 * P], ss[:, q, i, :], start=(i == 0), stop=True), i == 3)
            T["ks", q] = m
            for i in range(4):
                hd = 4 * q + i
                a = stt([m, T["rv", 2 + q], G["nbeg"]], rv[:, 2 + q, i, :], bank[b3][:, i * P:i * P + P],
                        nbeg[:, 1, hd:hd + 1], rv[:, 2 + q, i, :], ALU.mult, ALU.add)
            pfree[b3] = [a]
            T["r1", q] = a

        steps = sorted([(lv_, g_) for lv_ in range(1, 7) for g_ in range(4)], key=lambda u: (u[0] + 2 * (u[1] // 2), u[1]))
        between = {21: solve, 22: state, 23: carry}
        for n, u in enumerate(steps):
            bg.append(lambda u=u: level_p(*u))
            if n:
                bg.append(lambda u=steps[n - 1]: level_t(*u))
            if n in (1, 3):
                bg.append(lambda q=n // 2: ga_(1, q))
            if n in (4, 6, 8, 10):
                bg.append(lambda g_=n // 2 - 2: tokmaj_v(g_ // 2, g_ % 2))
            if n in between:
                for q in range(2):
                    bg.append(lambda f=between[n], q=q: f(q))
        bg.append(lambda: level_t(*steps[-1]))
        zt = []
        for n in range(8):
            b, m = tile_out("gdn", 24 + n, R2)
            a = act([m], zb[:, n, :], bank[b][:, 0:S], ACT.Silu)
            pfree[b] = [a]
            zt.append(a)
            background([2, 2, 4, 4, 6, 6, 6, 6][n])
        background(99)
        warm(ACT.Sqrt)
        ob = kb
        for q in range(2):
            solve(2 + q)
        oh, ol = hh, hl
        for q in range(2):
            b1 = nextbank()
            for i in range(4):
                m = pe([T["vn", q], T["aT", q]] + pfree[b1], MM(
                    bank[b1][:, i * P:i * P + P], vn[:, q, i, :], aT[:, q, i, :], start=(i == 0), stop=True), i == 3)
            o0 = ob[:, 4 * q:4 * q + 4, 0:P]
            t0 = cp([m, T["ks", 0], T["ks", 1], T["kd", 0], T["kd", 1]], o0,
                    bank[b1][:, :].rearrange("p (i s) -> p i s", i=4))
            pfree[b1] = [t0]
            b2 = nextbank()
            for i in range(4):
                pe([T["S", q], G["qd", q]] + pfree[b2], MM(
                    bank[b2][:, i * P:i * P + P], ss[:, q, i, :], qdec[:, 4 * q + i, :], start=(i == 0), stop=False), False)
            for i in range(4):
                m = pe([T["vn", 2 + q], T["aT", 2 + q]], MM(
                    bank[b2][:, i * P:i * P + P], vn[:, 2 + q, i, :], aT[:, 2 + q, i, :], start=False, stop=True), i == 3)
            o1 = ob[:, 4 * q:4 * q + 4, P:2 * P]
            t1 = act([m, T["ks", 0], T["ks", 1]], o1, bank[b2][:, :].rearrange("p (i s) -> p i s", i=4), ACT.Copy)
            pfree[b2] = [t1]
            T["o", q] = (t0, t1)
        sq = qb
        rt_ = [None] * 4

        def gated(i, m, v):
            ov = ob[:, 2 * i:2 * i + 2, :]
            a = stt([m, t_vec], ov, ov, V("a_norm_g"), v, ALU.mult, ALU.mult)
            rt_[i] = tt([a, zt[2 * i + 1]], ov, ov, zb[:, 2 * i:2 * i + 2, :], ALU.mult)
            return a

        osq, osum, oroot, ospread = head_norms(ob, lambda i: [G["qd", 0], G["qd", 1], T["aT", 3]], sq, 1.0 / 128, 4,
                                               [5, 6], "o", lambda n: list(T["o", n // 4]), gated)
        for f in osq + osum:
            f()
        spin(24)
        oroot()
        otk = []

        def oparts(i):
            hs = [act([rt_[i]], oh[:, k, :], ob[:, k, :], ACT.Copy) for k in (2 * i, 2 * i + 1)]
            for k in (2 * i, 2 * i + 1):
                otk.append(tt([hs[k % 2]], ol[:, k, :], ob[:, k, :], oh[:, k, :].bitcast(F), ALU.subtract))

        for i in range(4):
            ospread[i]()
            if i:
                oparts(i - 1)
        oparts(3)
        for k in range(8):
            if k < 7:
                feed()
            toks = kmaj("gout", k, 0, oh[:, k, :], ol[:, k, :], otk[k], k == 0, k == 7,
                        [t for b in range(4) for t in pfree[b]])

        def post(toks, g, b, i, parts=(hh, hl)):
            rt = residual(toks, 0, None, None, ALPHA2)
            x = norm(xa, rt, 8, 0, B[0], B[1], 4, 5, pfree[4] + pfree[5], lambda k: V(g, 8 * i + k),
                     lambda k: V(b, 8 * i + k), xa, (), *parts)
            pfree[4], pfree[5] = [x[0]], [x[0]]
            return x

        x3 = post(toks, "ln1_g_2", "ln1_b_2", 0)
        ht = x3
        toks = ffn("w130", "w20", False)
        x4 = post(toks, "ln2_g_2", "ln2_b_2", 0)
        ht = x4

        qq, kk_ = B[2], B[3]
        sw = B[4]

        def rope(dst, toks, n):
            x = dst[0:32, n:n + 2, :]
            y = sw[0:32, n:n + 2, :]
            two = [32, 2, S]
            a = ve([toks[n], toks[n + 1]], SH(y, x))
            b = tt([a, t_cst], y, y, C("sin")[0:32, :].unsqueeze(1).to_broadcast(two), ALU.mult)
            c = tt([b], x, x, C("cos")[0:32, :].unsqueeze(1).to_broadcast(two), ALU.mult)
            toks[n] = toks[n + 1] = tt([c], x, x, y, ALU.add)

        qt, kt = [], []
        R2 = [4, 5, 6, 7]
        start_tiles([("qkv", 0), ("qkv", 1), ("qkv", 2)], R2)
        for n in range(8):
            b, m = tile_out("qkv", n, R2)
            a = act([m], qq[:, n, :], bank[b][:, 0:S], ACT.Copy)
            pfree[b] = [a]
            qt.append(a)
            if n % 2:
                bg.append(lambda n=n: rope(qq, qt, n - 1))
            if n:
                background(1)
        for n in range(8):
            b, m = tile_out("qkv", 8 + n, R2)
            a = act([m], kk_[:, n, :], bank[b][:, 0:S], ACT.Copy)
            pfree[b] = [a]
            kt.append(a)
            if n % 2:
                bg.append(lambda n=n: rope(kk_, kt, n - 1))
            background(1)
        background(99)
        SC = 128.0 ** -0.5
        pr = B[0][:, :, :].rearrange("p a b -> p (a b)").rearrange("p (h s) -> p h s", h=8)
        p0 = B[1][:, 0:4, :].rearrange("p a b -> p (a b)").rearrange("p (h s) -> p h s", h=8)
        pT3 = B[4][:, :, :].rearrange("p a b -> p (a b)")[:, 0:1536].rearrange("p (h s) -> p h s", h=4)
        stat = smv(176, 8)
        ABK = [4, 5, 6, 7]
        na = [0]

        def abank():
            b = ABK[na[0] % 4]
            na[0] += 1
            return b

        prt = {}

        def scores(hd):
            b = abank()
            m = pe([qt[hd], kt[hd]] + pfree[b], MM(
                bank[b][:, 0:P], qq[:, hd, 0:P], kk_[:, hd, 0:P], start=True, stop=True))
            m1 = pe([], MM(bank[b][:, P:P + S], qq[:, hd, P:2 * P], kk_[:, hd, :], start=False,
                                           stop=True))
            s = stat[:, hd, :]
            a = put("vector", [m1, t_cst, x4[7]], lambda g: g.tensor_tensor_reduce(
                p0[:, hd, :], bank[b][:, 0:P], C("caus"), 1.0, -3e38, ALU.add, ALU.max, s[:, 0:1]))
            a = put("vector", [a], lambda g: g.tensor_tensor_reduce(
                pr[:, hd, :], bank[b][:, P:3 * P], C("caus0", 0, 256), 1.0, -3e38, ALU.add, ALU.max, s[:, 1:2]))
            pfree[b] = [a]
            prt["s", hd] = ts([a], s[:, 0:2], s[:, 0:2], -SC, None, ALU.mult)

        def exps(hd):
            a = prt["s", hd]
            s = stat[:, hd, :]
            e0 = act([a], p0[:, hd, :], p0[:, hd, :], ACT.Exp, bias=s[:, 0:1], scale=SC, accum_out=s[:, 2:3])
            e1 = act([a], pr[:, hd, :], pr[:, hd, :], ACT.Exp, bias=s[:, 1:2], scale=SC, accum_out=s[:, 3:4])
            prt["e", hd] = (e0, e1)

        def weights(hd):
            e0, e1 = prt["e", hd]
            s = stat[:, hd, :]
            r = ve([e0, e1], RC(s[:, 4:6], s[:, 2:4]))
            a = ts([r, e0], p0[:, hd, :], p0[:, hd, :], s[:, 4:5], None, ALU.mult)
            c = ts([r, e1], pr[:, hd, :], pr[:, hd, :], s[:, 5:6], None, ALU.mult)
            prt[hd] = (a, c)

        warm(ACT.Exp)
        for k in range(8):
            feed()
            j, wh, wl, wt = take("vt", k)
            for c in range(2):
                for n in range(2):
                    b = 2 * c + n
                    m = mm3(bank[b][:, :], wh[:, n * 512:n * 512 + 512], wl[:, n * 512:n * 512 + 512],
                            hh[:, k, c * P:c * P + P], hl[:, k, c * P:c * P + P],
                            [wt, ht[k]] + (pfree[b] if k == 0 else []), k == 0, k == 7, True, flip=True)
            finish(m)
            if k:
                exps(k - 1)
            scores(k)
            if k > 1:
                weights(k - 2)
        exps(7)
        vv = B[5][:, :, :].rearrange("p a b -> p (a b)").rearrange("p (c n) -> p c n", c=2)
        vtk = []
        for b in (0, 2, 1, 3):
            w = vv[:, b // 2, (b % 2) * 512:(b % 2) * 512 + 512]
            a = act([m], w, bank[b][:, :], ACT.Copy) if b < 2 else cp([m], w, bank[b][:, :])
            pfree[b] = [a]
            vtk.append(a)
        weights(6)
        weights(7)

        def turned(hd):
            a, c = prt[hd]
            b = abank()
            pe([a, c, t_cst] + pfree[b], TR(bank[b][:, 0:P], p0[:, hd, :], ident), False)
            pe([], TR(bank[b][:, P:2 * P], pr[:, hd, 0:P], ident), False)
            t = pe([], TR(bank[b][:, 2 * P:3 * P], pr[:, hd, P:2 * P], ident))
            d = act([t, kt[7], prt.get(("m", hd - 4))], pT3[:, hd % 4, :], bank[b][:, 0:3 * P], ACT.Copy)
            pfree[b] = [d]
            prt["d", hd] = d

        otk = [None] * 8

        def apply(hd):
            b2 = abank()
            vh = lambda c: vv[:, c, hd * P:hd * P + P]
            pe([prt["d", hd], *vtk] + pfree[b2], MM(
                bank[b2][:, 0:S], vh(0), pT3[:, hd % 4, 0:S], start=True, stop=False), False)
            m = pe([], MM(bank[b2][:, P:S], vh(1), pT3[:, hd % 4, 2 * P:3 * P], start=False, stop=True))
            prt["m", hd] = m
            a = act([m], hh[:, hd, :], bank[b2][:, 0:S], ACT.Copy)
            otk[hd] = tt([a], hl[:, hd, :], bank[b2][:, 0:S], hh[:, hd, :].bitcast(F), ALU.subtract)
            pfree[b2] = [otk[hd]]

        turned(0)
        turned(1)
        apply(0)
        turned(2)
        apply(1)
        for k in range(8):
            if k < 7:
                feed()
            toks = kmaj("bout", k, 0, hh[:, k, :], hl[:, k, :], otk[k], k == 0, k == 7,
                        [t for b in range(4) for t in pfree[b]])
            if k < 5:
                turned(k + 3)
            if k < 6:
                apply(k + 2)
        x5 = post(toks, "ln1_g_2", "ln1_b_2", 1)
        ht = x5
        toks = ffn("w131", "w21", False)
        x6 = post(toks, "ln2_g_2", "ln2_b_2", 1, ())
        ofin = h[:, :, :].rearrange("p a b -> p (a b)").rearrange("p (c n) -> p c n", c=2)
        for c in range(2):
            for q in range(2):
                b = 2 * c + q
                for i in range(4):
                    k = 4 * q + i
                    m = pe([x6[k]] + pfree[b], TR(
                        bank[b][:, i * P:i * P + P], xa[:, k, c * P:c * P + P], ident), i == 3)
                a = (act([m], ofin[:, c, q * 512:q * 512 + 512], bank[b][:, :], ACT.Copy) if q else
                     cp([m], ofin[:, c, q * 512:q * 512 + 512], bank[b][:, :]))
                if q == 0:
                    aw = a
            for t in (aw, a):
                queue["sync"].append(lambda g, t=t: g.wait_ge(t[0], t[1]))
            queue["sync"].append(lambda g, c=c: g.dma_start(out[c], ofin[:, c, :]).then_inc(s_out, 16))
        queue["sync"].append(lambda g: g.wait_ge(s_out, 32))
        assert fed[0] == len(PLAN) == sent[0] and len(used) == len(order)

        block = ctx.enter_context(nc.Block())

        @block.sync
        def _(g):
            for f in queue["sync"]:
                f(g)

        @block.gpsimd
        def _(g):
            for f in queue["gpsimd"]:
                f(g)

        @block.scalar
        def _(g):
            for f in queue["scalar"]:
                f(g)

        @block.tensor
        def _(g):
            for f in queue["tensor"]:
                f(g)

        @block.vector
        def _(g):
            for f in queue["vector"]:
                f(g)


ADA = [1, 0, 2, 4, 3, 5]


def _constants():
    i = np.arange(P)
    ident = np.eye(P, dtype=np.float32)
    tri = (i[:, None] <= i[None, :]).astype(np.float32)
    mstrict = (i[None, :] < i[:, None]).astype(np.float32)
    caus = np.where(i[None, :] <= i[:, None], 0.0, NEG).astype(np.float32)
    lev = []
    for n in range(7):
        m = 1 << n
        same = (i[:, None] // (2 * m)) == (i[None, :] // (2 * m))
        lev.append((same & ((i[:, None] // m) % 2 == 1) & ((i[None, :] // m) % 2 == 0)).astype(np.float32))
    freq = np.power(np.float32(500000.0), -np.arange(16, dtype=np.float32) / np.float32(16)).astype(np.float32)
    ang = np.arange(S, dtype=np.float32)[None, :] * freq[:, None]
    cos = np.zeros((P, S), np.float32)
    sin = np.zeros((P, S), np.float32)
    cos[0:16] = cos[16:32] = np.cos(ang)
    sin[0:16] = -np.sin(ang)
    sin[16:32] = np.sin(ang)
    cnt = np.concatenate([1.0 / np.minimum(np.arange(16) + 1, w) for w in (2, 4, 8, 16)]).astype(np.float32)
    parts = {"ident": ident, "tri": tri, "mstrict": mstrict, "caus0": np.zeros_like(caus), "caus": caus,
             "lev": np.concatenate(lev, axis=1), "levT1": lev[0].T, "cos": cos, "sin": sin,
             "icnt": np.broadcast_to(cnt, (P, 64)),
             "sel": np.broadcast_to(((np.arange(240) >= 112) & (np.arange(240) < 128)).astype(np.float32), (P, 240))}
    return np.ascontiguousarray(np.concatenate([parts[n] for n, _ in CST], axis=1))


def _cols(a):
    return np.asarray(a).reshape(-1, P).T


def _vectors(x):
    taps = lambda w: np.asarray(w).reshape(w.shape[0], -1, P).transpose(2, 1, 0).reshape(P, -1)
    w_in = np.asarray(x["a_w_in_2"])[0]
    parts = {
        "b_ada": _cols(x["b_ada"][0]), "b_dw_a": _cols(x["b_dw_a"][0]),
        "ln_a_g": _cols(x["ln_a_g"][0]), "ln_a_b": _cols(x["ln_a_b"][0]), "pool_scale": _cols(x["pool_scale"][0]),
        "ln1_g": _cols(x["ln1_g"][0]), "ln1_b": _cols(x["ln1_b"][0]), "b_dw_f": _cols(x["b_dw_f"][0]),
        "w_dw_f": taps(x["w_dw_f"][0]), "w_dw_a": taps(x["w_dw_a"][0]), "ln2_g": _cols(x["ln2_g"][0]),
        "ln2_b": _cols(x["ln2_b"][0]), "a_conv": taps(x["a_conv_2"][0]), "a_norm_g": _cols(x["a_norm_g_2"][0]),
        "ln1_g_2": _cols(x["ln1_g_2"]), "ln1_b_2": _cols(x["ln1_b_2"]), "ln2_g_2": _cols(x["ln2_g_2"]),
        "ln2_b_2": _cols(x["ln2_b_2"]), "a_log": np.broadcast_to(x["a_a_log_2"][0], (P, 8)),
        "dt": np.broadcast_to(x["a_dt_bias_2"][0], (P, 8)),
        "w_ba": w_in[:, 4096:4112].reshape(8, P, 16).transpose(1, 0, 2).reshape(P, 128),
    }
    return np.ascontiguousarray(np.concatenate([parts[n] for n, _ in VEC], axis=1))


def _nmaj(w):
    return w.reshape(8, P, -1, P).transpose(2, 1, 0, 3).reshape(-1, P, 1024)


def _weights(x):
    g = {k: np.asarray(v) for k, v in x.items()}
    ada = g["w_ada"][0].T.reshape(48, P, D)
    units = {
        "ada": [ada[8 * ADA[n // 8] + n % 8] for n in range(48)],
        "in": _nmaj(g["w_in"][0]), "pw": g["w_pw_a"][0].reshape(4, P, 1024),
        "pool": [g["w_pool"][0].transpose(1, 0, 2).reshape(P, 1024)],
        "out": g["w_out"][0].reshape(8, P, 1024), "up": _nmaj(g["w_up"][0]),
        "down": g["w_down"][0].reshape(FF, P, 1024), "gdn": _nmaj(g["a_w_in_2"][0][:, 0:4096]),
        "gout": g["a_w_out_2"][0].reshape(8, P, 1024), "qkv": _nmaj(g["b_w_qkv_2"][0][:, 0:2048]),
        "vt": g["b_w_qkv_2"][0][:, 2048:3072].reshape(8, P, 1024), "bout": g["b_w_out_2"][0].reshape(8, P, 1024),
        "w130": _nmaj(g["f_w13_2"][0]), "w20": g["f_w2_2"][0].reshape(FF, P, 1024),
        "w131": _nmaj(g["f_w13_2"][1]), "w21": g["f_w2_2"][1].reshape(FF, P, 1024),
    }
    return np.stack([units[k][n] for k, n in PLAN])


def kernel(**inputs):
    import concourse.bacc as _bacc
    from concourse.bass_utils import run_bass_kernel_spmd as _run

    nc = _bacc.Bacc("TRN2", target_bir_lowering=False, num_devices=1, dynamic_dma_scratch_size=1024)
    x = np.asarray(inputs["x"])[0]
    arrays = {
        "in_w": _weights(inputs),
        "in_v": _vectors(inputs),
        "in_c": _constants(),
        "in_r": np.ascontiguousarray(np.broadcast_to(np.asarray(inputs["c"])[0], (P, D))),
        "in_x": np.ascontiguousarray(x.T.reshape(8, P, S).transpose(1, 0, 2)),
    }
    aps = {k: nc.dram_tensor(k, a.shape, F, kind="ExternalInput").ap() for k, a in arrays.items()}
    out = nc.dram_tensor("out", (1, S, D), F, kind="ExternalOutput").ap()
    program(nc, aps["in_w"], aps["in_v"], aps["in_c"], aps["in_x"], aps["in_r"], out.rearrange("b (c p) d -> (b c) p d", c=2))
    r = _run(nc, [arrays], core_ids=[0])
    return r.results[0]["out"]
```
